# Optimizing a Trainium2 kernel written in Bass

```python
import math
import jax, jax.numpy as jnp
from jax import lax
import numpy as np

D_MODEL = 1024
BATCH = 1
SEQ = 2048
DEPTH = 1

HEAD_DIM = 64
FOX_HEADS = 8
FOX_WIDTH = FOX_HEADS * HEAD_DIM
DIFF_HEADS = 4
DIFF_V_DIM = 2 * HEAD_DIM
DIFF_WIDTH = DIFF_HEADS * DIFF_V_DIM
DIFF_QK_WIDTH = DIFF_HEADS * 2 * HEAD_DIM
MIX_WIDTH = FOX_WIDTH + DIFF_WIDTH
D_FF = 4 * D_MODEL
Q_BLOCK = 128
RMS_EPS = 1e-6
FORGET_BIAS_INIT = 3.0
LAMBDA_INIT_STD = 0.1
IN_SPLITS = (FOX_WIDTH, FOX_WIDTH, FOX_WIDTH, FOX_HEADS, DIFF_QK_WIDTH, DIFF_QK_WIDTH, DIFF_WIDTH)
IN_COLS = sum(IN_SPLITS)

kernel_name = "hybrid_fox_diffattn_block"

def rmsnorm(x, g):
    xf = x.astype(jnp.float32)
    y = xf * lax.rsqrt(jnp.mean(xf * xf, axis=-1, keepdims=True) + RMS_EPS)
    return (y * g.astype(jnp.float32)).astype(x.dtype)

def lambda_init_fn(layer_idx):
    return 0.8 - 0.6 * math.exp(-0.3 * layer_idx)

def alibi_slopes(n_heads):
    return jnp.asarray(2.0 ** (-8.0 * np.arange(1, n_heads + 1) / n_heads), dtype=jnp.float32)

def sweep_query_blocks(step, seq):
    n_blocks = seq // Q_BLOCK
    out = lax.map(step, jnp.arange(n_blocks))
    out = jnp.moveaxis(out, 0, 1)
    return out.reshape(out.shape[0], seq, out.shape[-1])

def causal_positions(i, seq):
    q_pos = i * Q_BLOCK + jnp.arange(Q_BLOCK)
    k_pos = jnp.arange(seq)
    return q_pos, k_pos, k_pos[None, :] <= q_pos[:, None]

def forgetting_attention(q, k, v, f_logit):
    B, S, H, Dh = q.shape
    scale = Dh ** -0.5
    c = jnp.cumsum(jax.nn.log_sigmoid(f_logit.astype(jnp.float32)), axis=1)
    c = jnp.transpose(c, (0, 2, 1))

    def step(i):
        start = i * Q_BLOCK
        q_i = lax.dynamic_slice_in_dim(q, start, Q_BLOCK, axis=1)
        c_i = lax.dynamic_slice_in_dim(c, start, Q_BLOCK, axis=2)
        _, _, mask = causal_positions(i, S)
        s = jnp.einsum('bqhd,bkhd->bhqk', q_i, k).astype(jnp.float32) * scale
        s = s + c_i[..., :, None] - c[..., None, :]
        s = jnp.where(mask, s, -jnp.inf)
        p = jax.nn.softmax(s, axis=-1)
        o = jnp.einsum('bhqk,bkhd->bqhd', p.astype(v.dtype), v)
        return o.reshape(B, Q_BLOCK, H * Dh)

    return sweep_query_blocks(step, S)

def differential_attention(q, k, v, lam, g_sub, lam_init):
    B, S, H, _, Dh = q.shape
    Dv = v.shape[-1]
    scale = Dh ** -0.5
    slopes = alibi_slopes(H)

    def step(i):
        start = i * Q_BLOCK
        q_i = lax.dynamic_slice_in_dim(q, start, Q_BLOCK, axis=1)
        q_pos, k_pos, mask = causal_positions(i, S)
        dist = (q_pos[:, None] - k_pos[None, :]).astype(jnp.float32)
        bias = -slopes[:, None, None] * dist
        s = jnp.einsum('bqhnd,bkhnd->bhnqk', q_i, k).astype(jnp.float32) * scale
        s = s + bias[None, :, None]
        s = jnp.where(mask, s, -jnp.inf)
        p = jax.nn.softmax(s, axis=-1)
        a = p[:, :, 0] - lam * p[:, :, 1]
        o = jnp.einsum('bhqk,bkhd->bqhd', a.astype(v.dtype), v)
        o = rmsnorm(o, g_sub) * (1.0 - lam_init)
        return o.reshape(B, Q_BLOCK, H * Dv)

    return sweep_query_blocks(step, S)

def setup_inputs(seed: int = 0) -> dict:
    key = jax.random.key(seed)
    ks = jax.random.split(key, 16)
    f32 = jnp.float32

    def gain(k, n):
        return 1.0 + 0.02 * jax.random.normal(k, (DEPTH, n), f32)

    return {
        "x": jax.random.normal(ks[0], (BATCH, SEQ, D_MODEL), f32),
        "g_pre_mix": gain(ks[1], D_MODEL),
        "w_in": jax.random.normal(ks[2], (DEPTH, D_MODEL, IN_COLS), f32) * D_MODEL ** -0.5,
        "b_forget": FORGET_BIAS_INIT + 0.1 * jax.random.normal(ks[3], (DEPTH, FOX_HEADS), f32),
        "lambda_q1": LAMBDA_INIT_STD * jax.random.normal(ks[4], (DEPTH, HEAD_DIM), f32),
        "lambda_k1": LAMBDA_INIT_STD * jax.random.normal(ks[5], (DEPTH, HEAD_DIM), f32),
        "lambda_q2": LAMBDA_INIT_STD * jax.random.normal(ks[6], (DEPTH, HEAD_DIM), f32),
        "lambda_k2": LAMBDA_INIT_STD * jax.random.normal(ks[7], (DEPTH, HEAD_DIM), f32),
        "g_subln": gain(ks[8], DIFF_V_DIM),
        "w_out": jax.random.normal(ks[9], (DEPTH, MIX_WIDTH, D_MODEL), f32) * MIX_WIDTH ** -0.5,
        "g_post_mix": gain(ks[10], D_MODEL),
        "g_pre_mlp": gain(ks[11], D_MODEL),
        "w_up": jax.random.normal(ks[12], (DEPTH, D_MODEL, D_FF), f32) * D_MODEL ** -0.5,
        "w_down": jax.random.normal(ks[13], (DEPTH, D_FF, D_MODEL), f32) * D_FF ** -0.5,
        "g_post_mlp": gain(ks[14], D_MODEL),
    }

def reference(x, g_pre_mix, w_in, b_forget, lambda_q1, lambda_k1, lambda_q2, lambda_k2,
              g_subln, w_out, g_post_mix, g_pre_mlp, w_up, w_down, g_post_mlp):
    B, S, _ = x.shape
    split_idx = [int(v) for v in np.cumsum(IN_SPLITS)[:-1]]
    for l in range(DEPTH):
        h = rmsnorm(x, g_pre_mix[l])
        proj = jnp.einsum('bsd,dc->bsc', h, w_in[l])
        fq, fk, fv, f_logit, dq, dk, dv = jnp.split(proj, split_idx, axis=-1)
        f_logit = f_logit + b_forget[l]
        fox = forgetting_attention(
            fq.reshape(B, S, FOX_HEADS, HEAD_DIM),
            fk.reshape(B, S, FOX_HEADS, HEAD_DIM),
            fv.reshape(B, S, FOX_HEADS, HEAD_DIM),
            f_logit)
        lam_init = lambda_init_fn(l)
        lam = (jnp.exp(jnp.sum(lambda_q1[l].astype(jnp.float32) * lambda_k1[l].astype(jnp.float32)))
               - jnp.exp(jnp.sum(lambda_q2[l].astype(jnp.float32) * lambda_k2[l].astype(jnp.float32)))
               + lam_init)
        diff = differential_attention(
            dq.reshape(B, S, DIFF_HEADS, 2, HEAD_DIM),
            dk.reshape(B, S, DIFF_HEADS, 2, HEAD_DIM),
            dv.reshape(B, S, DIFF_HEADS, DIFF_V_DIM),
            lam, g_subln[l], lam_init)
        mix = jnp.einsum('bsc,cd->bsd', jnp.concatenate([fox, diff], axis=-1), w_out[l])
        x = x + rmsnorm(mix, g_post_mix[l])
        h = rmsnorm(x, g_pre_mlp[l])
        u = jnp.square(jax.nn.relu(jnp.einsum('bsd,df->bsf', h, w_up[l])))
        x = x + rmsnorm(jnp.einsum('bsf,fd->bsd', u, w_down[l]), g_post_mlp[l])
    return x


_drawn_inputs = setup_inputs


def setup_inputs(seed=0):
    import zlib

    import numpy as np

    out = dict(_drawn_inputs(seed))
    spreads = {}
    factors = {'b_forget': 23.312,
     'g_subln': 3.849,
     'g_post_mix': 10.567,
     'g_pre_mlp': 37.481,
     'g_post_mlp': 60.904}
    for name, (base, spread) in spreads.items():
        noise = np.random.default_rng([zlib.crc32(name.encode()), seed]).standard_normal(out[name].shape)
        drawn = base * np.exp(spread * noise) if base else spread * noise
        out[name] = __import__('jax').numpy.asarray(drawn.astype(out[name].dtype))
    for name, factor in factors.items():
        out[name] = (out[name] * factor).astype(out[name].dtype)
    return out
```

```python
from contextlib import ExitStack

import concourse.bass as bass
from concourse import mybir

F32 = mybir.dt.float32
F32R = mybir.dt.float32r
ALU = mybir.AluOpType
ACT = mybir.ActivationFunctionType
AX = mybir.AxisListType

P = 128
D = 1024
S = 2048
KT = D // P
RT = S // P
HD = 64
DFF = 4 * D
EPS = 1e-6
FOX_HEADS = 8
DIFF_HEADS = 4
LAM_INIT = 0.2
LOGIT_COL = 3 * FOX_HEADS * HD
QKV_TILES = 24
ROOT = D ** -0.5
MASKED = -float(2 ** 100)


def f32(ap):
    return ap.bitcast(F32)


class Room:

    def __init__(self, nc, ctx, stage):
        self.nc, self.ctx, self.stage = nc, ctx, stage

    def sb(self, name, shape, dt=F32):
        return self.ctx.enter_context(self.nc.sbuf_tensor(f"{self.stage}_{name}", shape, dt))

    def ps(self, name, shape):
        return self.ctx.enter_context(self.nc.psum_tensor(f"{self.stage}_{name}", shape, F32))

    def sem(self, name):
        return self.ctx.enter_context(self.nc.semaphore(f"{self.stage}_{name}"))


def project(nc, x, g_pre_mix, w_in, qkvT):
    with ExitStack() as ctx:
        r = Room(nc, ctx, "pj")
        ident = r.sb("ident", [P, P])
        gain = r.sb("gain", [P, D])
        xin = r.sb("xin", [P, 2, D])
        xn = r.sb("xn", [P, 2, D])
        ss = r.sb("ss", [P, RT])
        ms = r.sb("ms", [P, RT])
        rstd = r.sb("rstd", [P, RT])
        power = r.sb("power", [P, 1])
        eps = r.sb("eps", [P, 1])
        h_hi = r.sb("h_hi", [P, KT, S], F32R)
        h_lo = r.sb("h_lo", [P, KT, S], F32R)
        w_raw = r.sb("w_raw", [P, 2, KT, P])
        w_hi = r.sb("w_hi", [P, 2, KT, P], F32R)
        w_lo = r.sb("w_lo", [P, 2, KT, P], F32R)
        qscale = r.sb("qscale", [P, QKV_TILES + 1])
        proj_sb = r.sb("proj_sb", [P, 2, S])
        acc = r.ps("acc", [P, 2, S])
        x_loaded = [r.sem(f"x_loaded{s}") for s in range(2)]
        gain_loaded = r.sem("gain_loaded")
        const_ready = r.sem("const_ready")
        ss_ready = r.sem("ss_ready")
        rstd_step = r.sem("rstd_step")
        xn_ready = r.sem("xn_ready")
        xT_ready = r.sem("xT_ready")
        h_hi_ready = r.sem("h_hi_ready")
        h_ready = r.sem("h_ready")
        w_loaded = [r.sem(f"w_loaded{s}") for s in range(2)]
        w_hi_ready = r.sem("w_hi_ready")
        w_ready = r.sem("w_ready")
        proj_done = r.sem("proj_done")
        evacuated = r.sem("evacuated")
        stored = [r.sem(f"stored{s}") for s in range(2)]
        block = ctx.enter_context(nc.Block())
        w_v = w_in.rearrange("o (t p) c -> p (o t) c", p=P)
        half = QKV_TILES // 2
        gap = FOX_HEADS

        def column_tiles(eng, step):
            for lo, shift in ((0, 0), (half // 2, gap)):
                with eng.Fori(lo, lo + half // 2) as i:
                    for s in range(2):
                        step(i, s, 2 * i + s, i * (2 * P) + (s * P + shift))
            step(half, 0, QKV_TILES, LOGIT_COL)

        @block.sync
        def _(sp):
            sp.dma_start(gain[:, :], g_pre_mix[0:1, :].to_broadcast([P, D])).then_inc(gain_loaded, 16)
            for t in range(2):
                sp.dma_start(xin[:, t, :], x[0, t * P:(t + 1) * P, :]).then_inc(x_loaded[t], 16)
            with sp.Fori(0, RT // 2 - 1) as i:
                for s in range(2):
                    sp.wait_ge(xn_ready, 2 * i + s + 1)
                    sp.dma_start(xin[:, s, :], x[0, bass.ts(2 * i + (s + 2), P), :]).then_inc(x_loaded[s], 16)

            def load(i, s, ct, col):
                sp.wait_ge(w_ready, ct + 1)
                sp.dma_start(w_raw[:, s], w_v[:, :, bass.ds(col, P)]).then_inc(w_loaded[s], 16)
            column_tiles(sp, load)

        @block.gpsimd
        def _(pool):
            pool.memset(ident[:, :], 0.0).then_inc(const_ready, 1)
            pool.memset(power[:, :], -0.5).then_inc(const_ready, 1)
            pool.memset(eps[:, :], EPS).then_inc(const_ready, 1)
            pool.wait_ge(const_ready, 1)
            pool.affine_select(out=ident[:, :], in_=ident[:, :], compare_op=ALU.not_equal, fill=1.0,
                               base=0, pattern=[[-1, P]], channel_multiplier=1).then_inc(const_ready, 1)
            pool.memset(qscale[:, :], 1.0).then_inc(const_ready, 1)
            pool.wait_ge(const_ready, 5)
            for c in (0, half):
                pool.memset(qscale[:, c:c + 4], HD ** -0.5).then_inc(const_ready, 1)
            with pool.Fori(0, RT) as t:
                pool.wait_ge(ss_ready, t + 1)
                pool.tensor_tensor(ms[:, bass.ds(t, 1)], ss[:, bass.ds(t, 1)], eps[:, :], ALU.add)\
                    .then_inc(rstd_step, 1)
                pool.wait_ge(rstd_step, 2 * t + 1)
                pool.tensor_tensor(rstd[:, bass.ds(t, 1)], ms[:, bass.ds(t, 1)], power[:, :],
                                   ALU.pow).then_inc(rstd_step, 1)

        @block.scalar
        def _(act):
            act.sem_inc(evacuated, 2)
            for s in range(2):
                act.sem_inc(stored[s], 16)

            def square(i, s, t):
                act.wait_ge(x_loaded[s], 16 * (i + 1))
                act.activation(xn[:, s, :], xin[:, s, :], ACT.Square, scale=ROOT,
                               accum_out=ss[:, bass.ds(t, 1)]).then_inc(ss_ready, 1)

            def keep_hi(s, t):
                act.wait_ge(xT_ready, t + 1)
                act.activation(h_hi[:, :, bass.ts(t, P)], acc[:, s, 0:D].rearrange("p (k r) -> p k r", r=P),
                               ACT.Copy).then_inc(h_hi_ready, 1)

            for t in range(2):
                square(0, t, t)
            with act.Fori(0, RT // 2 - 1) as i:
                for s in range(2):
                    keep_hi(s, 2 * i + s)
                    square(i + 1, s, 2 * i + (s + 2))
            for s in range(2):
                keep_hi(s, RT - 2 + s)

            def evacuate(i, s, ct, col):
                act.wait_ge(proj_done, ct + 3)
                act.wait_ge(stored[s], 16 * (i + 1))
                act.activation(proj_sb[:, s, :], acc[:, s, :], ACT.Copy,
                               scale=qscale[:, bass.ds(ct, 1)]).then_inc(evacuated, 1)
                act.wait_ge(evacuated, ct + 3)
                act.dma_start(qkvT[bass.ds(ct, 1), :, :].rearrange("o p n -> (o p) n"),
                              proj_sb[:, s, :]).then_inc(stored[s], 16)
            act.wait_ge(const_ready, 7)
            column_tiles(act, evacuate)
            act.wait_ge(stored[0], 16 * (half + 2))
            act.wait_ge(stored[1], 16 * (half + 1))

        @block.vector
        def _(dve):
            dve.sem_inc(w_ready, 2)

            def normalise(s, t):
                dve.wait_ge(rstd_step, 2 * t + 2)
                dve.scalar_tensor_tensor(out=xn[:, s, :], in0=xin[:, s, :], scalar=rstd[:, bass.ds(t, 1)],
                                         in1=gain[:, :], op0=ALU.mult, op1=ALU.mult).then_inc(xn_ready, 1)

            def keep_lo(s, t):
                dve.wait_ge(h_hi_ready, t + 1)
                dve.tensor_tensor(h_lo[:, :, bass.ts(t, P)], acc[:, s, 0:D].rearrange("p (k r) -> p k r", r=P),
                                  f32(h_hi[:, :, bass.ts(t, P)]), ALU.subtract).then_inc(h_ready, 1)

            dve.wait_ge(gain_loaded, 16)
            for t in range(2):
                normalise(t, t)
            with dve.Fori(0, RT // 2 - 1) as i:
                for s in range(2):
                    keep_lo(s, 2 * i + s)
                    normalise(s, 2 * i + (s + 2))
            for s in range(2):
                keep_lo(s, RT - 2 + s)

            def split(i, s, ct, col):
                dve.wait_ge(w_loaded[s], 16 * (i + 1))
                dve.wait_ge(proj_done, ct + 1)
                dve.tensor_copy(w_hi[:, s], w_raw[:, s]).then_inc(w_hi_ready, 1)
                dve.wait_ge(w_hi_ready, ct + 1)
                dve.tensor_tensor(w_lo[:, s], w_raw[:, s], f32(w_hi[:, s]), ALU.subtract).then_inc(w_ready, 1)
            column_tiles(dve, split)

        @block.tensor
        def _(pe):
            pe.sem_inc(proj_done, 2)
            pe.wait_ge(const_ready, 4)

            def transpose(s, t):
                pe.wait_ge(xn_ready, t + 1)
                for k in range(KT):
                    last = pe.transpose(acc[:, s, k * P:(k + 1) * P], xn[:, s, k * P:(k + 1) * P], ident[:, :])
                last.then_inc(xT_ready, 1)
            for t in range(2):
                transpose(t, t)
            with pe.Fori(0, RT // 2 - 1) as i:
                for s in range(2):
                    pe.wait_ge(h_ready, 2 * i + s + 1)
                    transpose(s, 2 * i + (s + 2))
            pe.wait_ge(h_ready, RT)

            def multiply(i, s, ct, col):
                pe.wait_ge(w_ready, ct + 3)
                pe.wait_ge(evacuated, ct + 1)
                for b in range(S // 512):
                    rows = slice(b * 512, (b + 1) * 512)
                    for k in range(KT):
                        pe.matmul(acc[:, s, rows], w_hi[:, s, k], h_hi[:, k, rows], start=(k == 0), stop=False)
                        pe.matmul(acc[:, s, rows], w_hi[:, s, k], h_lo[:, k, rows], start=False, stop=False)
                        last = pe.matmul(acc[:, s, rows], w_lo[:, s, k], h_hi[:, k, rows],
                                         start=False, stop=(k == KT - 1))
                last.then_inc(proj_done, 1)
            column_tiles(pe, multiply)


def decay(nc, qkvT, b_forget, q_rows, k_rows):
    with ExitStack() as ctx:
        r = Room(nc, ctx, "dc")
        H = FOX_HEADS
        z = r.sb("z", [H, S])
        b = r.sb("b", [H, 1])
        az = r.sb("az", [H, S])
        e = r.sb("e", [H, S])
        w = r.sb("w", [H, S])
        lw = r.sb("lw", [H, S])
        t1 = r.sb("t1", [H, S])
        c = r.sb("c", [H, S])
        hi = r.sb("hi", [H, S], F32R)
        lo = r.sb("lo", [H, S], F32R)
        nhi = r.sb("nhi", [H, S], F32R)
        nlo = r.sb("nlo", [H, S], F32R)
        ones = r.sb("ones", [H, S], F32R)
        zero = r.sb("zero", [H, S], F32R)
        pos = r.sb("pos", [1, S])
        up = r.sb("up", [1, DIFF_HEADS, S], F32R)
        down = r.sb("down", [1, DIFF_HEADS, S], F32R)
        loaded = r.sem("loaded")
        pos_ready = r.sem("pos_ready")
        step = r.sem("step")
        e_ready = r.sem("e_ready")
        stored = r.sem("stored")
        DVE_STEPS = 2 + 2 * DIFF_HEADS + 11
        block = ctx.enter_context(nc.Block())

        @block.gpsimd
        def _(pool):
            pool.iota(pos[:, :], pattern=[[1, S]], base=0, channel_multiplier=0,
                      allow_small_or_imprecise_dtypes=True).then_inc(pos_ready, 1)
            pool.memset(f32(ones[:, :]), 1.0).then_inc(pos_ready, 1)
            pool.memset(f32(zero[:, :]), 0.0).then_inc(pos_ready, 1)

        @block.vector
        def _(dve):
            done = [0]

            def link(ins):
                done[0] += 1
                ins.then_inc(step, 1)
                dve.wait_ge(step, done[0])
            dve.wait_ge(loaded, 32)
            link(dve.tensor_scalar(z[:, :], z[:, :], b[:, :], None, ALU.add))
            link(dve.scalar_tensor_tensor(out=az[:, :], in0=z[:, :], scalar=-1.0, in1=z[:, :],
                                          op0=ALU.mult, op1=ALU.max))
            dve.wait_ge(pos_ready, 3)
            for h in range(DIFF_HEADS):
                slope = 2.0 ** (-8.0 * (h + 1) / DIFF_HEADS)
                dve.tensor_scalar(down[:, h, :], pos[:, :], -slope, None, ALU.mult).then_inc(step, 1)
                dve.tensor_scalar(up[:, h, :], pos[:, :], slope, None, ALU.mult).then_inc(step, 1)
                done[0] += 2
            dve.wait_ge(e_ready, 1)
            link(dve.tensor_scalar(w[:, :], e[:, :], 1.0, None, ALU.add))
            link(dve.scalar_tensor_tensor(out=t1[:, :], in0=w[:, :], scalar=-1.0, in1=e[:, :],
                                          op0=ALU.add, op1=ALU.subtract))
            link(dve.reciprocal(az[:, :], w[:, :]))
            link(dve.tensor_tensor(t1[:, :], t1[:, :], az[:, :], ALU.mult))
            dve.wait_ge(e_ready, 2)
            link(dve.tensor_tensor(t1[:, :], t1[:, :], lw[:, :], ALU.subtract))
            link(dve.scalar_tensor_tensor(out=t1[:, :], in0=z[:, :], scalar=0.0, in1=t1[:, :],
                                          op0=ALU.min, op1=ALU.add))
            link(dve.tensor_tensor_scan(c[:, :], t1[:, :], f32(zero[:, :]), 0.0, ALU.add, ALU.add))
            link(dve.tensor_copy(hi[:, :], c[:, :]))
            link(dve.tensor_tensor(lo[:, :], c[:, :], f32(hi[:, :]), ALU.subtract))
            link(dve.tensor_scalar(nhi[:, :], f32(hi[:, :]), -1.0, None, ALU.mult))
            link(dve.tensor_scalar(nlo[:, :], f32(lo[:, :]), -1.0, None, ALU.mult))
            assert done[0] == DVE_STEPS


        @block.scalar
        def _(act):
            act.wait_ge(step, 2)
            act.activation(e[:, :], az[:, :], ACT.Exp, scale=-1.0).then_inc(e_ready, 1)
            act.wait_ge(step, 3 + 2 * DIFF_HEADS)
            act.activation(lw[:, :], w[:, :], ACT.Ln).then_inc(e_ready, 1)

        @block.sync
        def _(sp):
            sp.dma_start(z[:, :], qkvT[QKV_TILES, 0:H, :]).then_inc(loaded, 16)
            sp.dma_start(b[:, :], b_forget.rearrange("o h -> h o")).then_inc(loaded, 16)
            sp.wait_ge(pos_ready, 3)
            sp.wait_ge(step, 2 + 2 * DIFF_HEADS)
            n = 0
            D4 = DIFF_HEADS
            for rows, k, src in ((q_rows, 0, down[0:1, :, :]), (k_rows, 2, up[0:1, :, :])):
                sp.dma_start(rows[H:H + D4, k, :].rearrange("(o h) n -> o h n", o=1), f32(src)).then_inc(stored, 16)
                n += 1
            for rows, k, src in ((q_rows, 1, zero), (q_rows, 2, ones), (q_rows, 3, ones), (q_rows, 4, zero),
                                 (q_rows, 5, zero), (k_rows, 0, ones), (k_rows, 1, ones), (k_rows, 3, zero),
                                 (k_rows, 4, ones), (k_rows, 5, ones)):
                sp.dma_start(rows[H:H + D4, k, :], f32(src[0:D4, :])).then_inc(stored, 16)
                n += 1
            for rows, k, src in ((q_rows, 2, ones), (q_rows, 3, ones), (q_rows, 4, zero), (q_rows, 5, zero),
                                 (k_rows, 0, ones), (k_rows, 1, ones), (k_rows, 4, ones), (k_rows, 5, ones)):
                sp.dma_start(rows[0:H, k, :], f32(src[:, :])).then_inc(stored, 16)
                n += 1
            sp.wait_ge(step, DVE_STEPS)
            for rows, k, src in ((q_rows, 0, hi), (q_rows, 1, lo), (k_rows, 2, nhi), (k_rows, 3, nlo)):
                sp.dma_start(rows[0:H, k, :], f32(src[:, :])).then_inc(stored, 16)
                n += 1
            sp.wait_ge(stored, 16 * n)


FOX, DIFF = 0, 1
RAW = 80
COMBOS = (80, 40)
BLOCKS = (8, 4)
STAT = 48
PRING, SRING = 4, 3
LAG = 2
NEAR = 4 * 4


def stat_chunks():
    return [(s, qt, ch) for s in range(2) for qt in range(RT) for ch in range(qt // 8 + 1)]


def raw_chunks(kind):
    if kind == FOX:
        return [(s, J, j) for s in range(2) for J in range(4) for j in range(4 * J + 4)]
    return [(s, J, j) for J in range(4) for j in range(4 * J + 4) for s in range(2)]


def on_pool(kind, m):
    return m % 2 == 0 if kind == FOX else m % 4 != 3


def lo_count(kind, m, pool):
    return sum(on_pool(kind, n) == pool for n in range(m + 1))


LO_TOTAL = [[lo_count(k, COMBOS[k] - 1, p) for k in (FOX, DIFF)] for p in (False, True)]


def plan(kind, with_stats):
    at = [[] for _ in range(RAW + 12)]
    if with_stats:
        at[0] += [("rows",), ("prep", 0)]
        at[8] += [("prep", 1)]
        first, per = 12, 26
        for g in range(STAT):
            s = g // 24
            t = first + s * (per + 4) + (g % 24) * per // 24
            at[t] += [("stat_scores", g)]
            at[t + 1] += [("stat_exp", g)]
        for s in range(2):
            t = first + s * (per + 4) + per + 1
            for n, what in enumerate(("stat_max", "stat_corr", "stat_sum", "stat_ln", "stat_shift",
                                      "stat_flip", "stat_rows")):
                at[t + n] += [(what, s)]
        for g in range(4):
            at[22 + 2 * g] += [("v_flip", g), ("v_split", g)]
    steps = []
    raws = raw_chunks(kind)
    combo_of = [c if kind == FOX else c // 2 for c in range(RAW)]
    pv_at, block_end = {}, {}
    lag = LAG if kind == FOX else 2 * LAG
    for c in range(RAW):
        if kind == FOX or c % 2:
            pv_at.setdefault(c + lag, []).append(combo_of[c])
    seen = 0
    for t in range(RAW + 12):
        if t < RAW:
            steps.append(("scores", t))
        for m in pv_at.get(t, []):
            steps.append(("pv", m))
            s, J, j = raws[m if kind == FOX else 2 * m]
            if j == 4 * J + 3:
                b = seen
                seen += 1
                at[min(t + 1, RAW + 11)].insert(0, ("o_first", b))
                if kind == DIFF:
                    at[min(t + 4, RAW + 11)].append(("o_var", b))
                    at[min(t + 6, RAW + 11)].append(("o_norm", b))
        if t < RAW:
            steps.append(("exp", t))
            if kind == FOX or t % 2:
                steps += [("split", combo_of[t])]
        steps += at[t]
    if with_stats:
        steps.append(("load_next",))
    return steps


def attend(nc, qkvT, q_rows, k_rows, lams, g_subln, mixT):
    with ExitStack() as ctx:
        r = Room(nc, ctx, "at")
        q1 = r.sb("q1", [P, 2, 2, S], F32R)
        k1 = r.sb("k1", [P, 2, 2, S], F32R)
        q2 = r.sb("q2", [P, 2, 2, S], F32R)
        k2 = r.sb("k2", [P, 2, 2, S], F32R)
        vals = r.sb("vals", [P, 2, RT, 256], F32R)
        stage_a = r.sb("stage_a", [P, S])
        stage_b = r.sb("stage_b", [P, S])
        probs = r.sb("probs", [P, PRING, 512])
        p_hi = r.sb("p_hi", [P, SRING, 512], F32R)
        p_lo = r.sb("p_lo", [P, SRING, 512], F32R)
        o_sb = r.sb("o_sb", [P, 2, 512])
        o_half = r.sb("o_half", [P, 512])
        var = o_half
        ident_r = r.sb("ident_r", [P, P], F32R)
        ident = f32(ident_r[:, :])
        mask_q = r.sb("mask_q", [P, P], F32R)
        mask_k = r.sb("mask_k", [P, P], F32R)
        made = o_half[:, 0:3 * P].rearrange("p (a n) -> p a n", n=P)
        mean = r.sb("mean", [P, P])
        power = r.sb("power", [P, 1])
        nmax = r.sb("nmax", [P, 2, 2, 2, RT])
        rsum = r.sb("rsum", [P, 2, 2, 2, RT])
        top = r.sb("top", [P, RT])
        corr = r.sb("corr", [P, 2, RT])
        total = r.sb("total", [P, RT])
        logsum = r.sb("logsum", [P, RT])
        shift = r.sb("shift", [P, 2 * RT], F32R)
        shiftT = r.sb("shiftT", [2 * RT, 2, P], F32R)
        lam_in = probs[:, 0, 0:4 * HD].rearrange("p (a d) -> p a d", d=HD)
        lam_s = r.sb("lam_s", [P, 4])
        nlam = r.sb("nlam", [P, 1])
        gsub = r.sb("gsub", [P, 1])
        ps_stat = r.ps("ps_stat", [P, 2, 1024])
        ps_sc = r.ps("ps_sc", [P, 2, 512])
        ps_o = r.ps("ps_o", [P, 512])
        ps_x = r.ps("ps_x", [P, 512])

        const_loaded = r.sem("const_loaded")
        const_pool = r.sem("const_pool")
        const_dve = r.sem("const_dve")
        const_act = r.sem("const_act")
        a_loaded = r.sem("a_loaded")
        b_loaded = r.sem("b_loaded")
        rows_loaded = r.sem("rows_loaded")
        shift_loaded = [r.sem(f"shift_loaded{s}") for s in range(2)]
        hi_ready = r.sem("hi_ready")
        lo_ready = r.sem("lo_ready")
        x_ready = r.sem("x_ready")
        x_free = r.sem("x_free")
        v_hi_ready = r.sem("v_hi_ready")
        stat_scored = r.sem("stat_scored")
        stat_maxed = r.sem("stat_maxed")
        stat_exped = r.sem("stat_exped")
        stat_dve = r.sem("stat_dve")
        stat_act = r.sem("stat_act")
        scored = r.sem("scored")
        exped = r.sem("exped")
        combined = r.sem("combined")
        p_hi_ready = r.sem("p_hi_ready")
        p_lo_dve = r.sem("p_lo_dve")
        p_lo_pool = r.sem("p_lo_pool")
        p_used = r.sem("p_used")
        o_half_ready = r.sem("o_half_ready")
        o_free = r.sem("o_free")
        o_squared = r.sem("o_squared")
        var_ready = r.sem("var_ready")
        o_normed = r.sem("o_normed")
        o_stored = [r.sem(f"o_stored{s}") for s in range(2)]
        block = ctx.enter_context(nc.Block())

        plans = {(k, w): plan(k, w) for k in (FOX, DIFF) for w in (True, False)}
        opening = [("rows",), ("prep", 0), ("prep", 1)]
        for g in range(STAT):
            opening += [("stat_scores", g)] + ([("stat_exp", g - 1)] if g else [])
            if g == 26:
                opening += [(w, 0) for w in ("stat_max", "stat_corr", "stat_sum", "stat_ln", "stat_shift",
                                             "stat_flip", "stat_rows")]
        opening += [("stat_exp", STAT - 1)] + [("v_flip", 0), ("v_split", 0), ("v_flip", 1), ("v_split", 1),
                                               ("v_flip", 2), ("v_split", 2), ("v_flip", 3), ("v_split", 3)]
        opening += [(w, 1) for w in ("stat_max", "stat_corr", "stat_sum", "stat_ln", "stat_shift",
                                     "stat_flip", "stat_rows")] + [("load_next",)]
        stats, raws = stat_chunks(), [raw_chunks(FOX), raw_chunks(DIFF)]
        X_OPEN, X_FOX, X_DIFF = 6, 6, 10

        class Half:

            def __init__(self, kind, i, with_stats=True):
                self.kind, self.i, self.with_stats = kind, i, with_stats
                if kind is None:
                    self.n, self.prep_kind, self.prep_i, self.slot, self.x = 0, FOX, 0, 0, 0
                    self.raw = 0
                    self.steps = opening
                    return
                self.n = 2 * i + 1 + kind
                self.prep_kind = DIFF if kind == FOX else FOX
                self.prep_i = i if kind == FOX else i + 1
                self.slot = 1 - kind
                self.raw = 2 * RAW * i + RAW * kind
                self.combo = sum(COMBOS) * i + COMBOS[FOX] * kind
                self.block = sum(BLOCKS) * i + BLOCKS[FOX] * kind
                self.x = (X_FOX + X_DIFF) * i + X_OPEN + X_FOX * kind
                self.steps = plans[kind, with_stats]
                self.shift_value = 32 * (2 * i + kind) + 32
                self.xpos = {}
                for st in self.steps:
                    if st[0] in ("v_flip", "stat_flip", "o_var"):
                        self.xpos[st] = len(self.xpos)

            def lo_value(self, m, pool):
                i, kind = self.i, self.kind
                both = sum(LO_TOTAL[pool])
                if m < 0:
                    m += COMBOS[1 - kind]
                    if kind == DIFF:
                        return i * both + (4 + lo_count(FOX, m, pool))
                    return i * both + (4 + LO_TOTAL[pool][FOX] + lo_count(DIFF, m, pool) - both)
                before = LO_TOTAL[pool][FOX] if kind == DIFF else 0
                return i * both + (4 + before + lo_count(kind, m, pool))

        open_x = {}
        for st in opening:
            if st[0] in ("v_flip", "stat_flip"):
                open_x[st] = len(open_x)

        def xpos(h, st):
            return (open_x if h.kind is None else h.xpos)[st]

        def halves(eng, emit):
            emit(Half(None, 0))
            with eng.Fori(0, DIFF_HEADS - 1) as i:
                emit(Half(FOX, i))
                emit(Half(DIFF, i))
            emit(Half(FOX, DIFF_HEADS - 1))
            emit(Half(DIFF, DIFF_HEADS - 1, with_stats=False))

        def width(J, j):
            return max(0, j - 4 * J) * P

        def block_of(kind, m):
            s, J, j = raws[kind][m if kind == FOX else 2 * m]
            return s, J, j

        def block_last(kind, b):
            ends = [m for m in range(COMBOS[kind]) if block_of(kind, m)[2] == 4 * block_of(kind, m)[1] + 3]
            return ends[b]

        @block.sync
        def _(sp):
            for n, v in enumerate(lams):
                sp.dma_start(lam_in[:, n, :], v[0:1, :].to_broadcast([P, HD])).then_inc(const_loaded, 16)
            sp.dma_start(gsub[:, :], g_subln.rearrange("o d -> d o")).then_inc(const_loaded, 16)

            def load_qk(kind, i, s, n, which, wait=True):
                first = 0 if kind == FOX else 12
                for z in range(2):
                    dst, sem, base = (stage_a, a_loaded, first) if which == 0 else (stage_b, b_loaded, first + 4)
                    sp.dma_start(dst[z * 64:(z + 1) * 64, :],
                                 qkvT[bass.ds(i + base, 1), s * 64:(s + 1) * 64, :]
                                 .rearrange("o p n -> (o p) n")).then_inc(sem, 16)

            def emit(h):
                if h.kind is None:
                    load_qk(FOX, 0, 0, 0, 0)
                    load_qk(FOX, 0, 0, 0, 1)
                for st in h.steps:
                    op = st[0]
                    if op == "rows":
                        if h.kind is not None:
                            sp.wait_ge(scored, h.raw + 1)
                        else:
                            sp.wait_ge(const_pool, 7)
                        head = h.prep_i if h.prep_kind == FOX else h.prep_i + FOX_HEADS
                        for s in range(2):
                            for dst, src in ((q2, q_rows), (k2, k_rows)):
                                at = 2 * h.prep_i + s if h.prep_kind == FOX else head
                                sp.dma_start(f32(dst[0:6, h.slot, s, :]),
                                             src[bass.ds(at, 1), :, :].rearrange("o r n -> (o r) n"))\
                                  .then_inc(rows_loaded, 16)
                    elif op == "prep" and st[1] == 0:
                        sp.wait_ge(lo_ready, 4 * h.n + 1)
                        load_qk(h.prep_kind, h.prep_i, 1, h.n, 0)
                        sp.wait_ge(lo_ready, 4 * h.n + 2)
                        load_qk(h.prep_kind, h.prep_i, 1, h.n, 1)
                    elif op == "prep":
                        sp.wait_ge(lo_ready, 4 * h.n + 3)
                        base = 8 if h.prep_kind == FOX else 20
                        for z in range(2):
                            sp.dma_start(stage_a[z * 64:(z + 1) * 64, :],
                                         qkvT[bass.ds(h.prep_i + base, 1), z * 64:(z + 1) * 64, :]
                                         .rearrange("o p n -> (o p) n")).then_inc(a_loaded, 16)
                    elif op == "load_next":
                        if h.kind == FOX and not isinstance(h.i, int):
                            kind, i = FOX, h.i + 1
                        elif h.kind == FOX:
                            continue
                        elif h.kind == DIFF:
                            kind, i = DIFF, h.i + 1
                        else:
                            kind, i = DIFF, 0
                        sp.wait_ge(x_ready, h.x + xpos(h, ("v_flip", 3)) + 1)
                        load_qk(kind, i, 0, None, 0)
                        sp.wait_ge(lo_ready, 4 * h.n + 4)
                        load_qk(kind, i, 0, None, 1)
                    elif op == "stat_rows":
                        s = st[1]
                        sp.wait_ge(stat_dve, 8 * (2 * h.n + s) + 8)
                        for z in range(2):
                            sp.dma_start(f32(q2[4 + z:5 + z, h.slot, s, :].rearrange("o (t q) -> o t q", q=P)),
                                         f32(shiftT[z * RT:(z + 1) * RT, s, :])).then_inc(shift_loaded[s], 16)
                    elif op == "o_first" and h.kind == FOX:
                        b = st[1]
                        s, J, _ = block_of(FOX, block_last(FOX, b))
                        sp.wait_ge(o_free, h.block + b + 2)
                        sp.dma_start(mixT[bass.ds(h.i, 1), s * 64:(s + 1) * 64, J * 512:(J + 1) * 512]
                                     .rearrange("o p n -> (o p) n"), o_sb[0:64, b % 2, :])\
                          .then_inc(o_stored[b % 2], 16)
                    elif op == "o_norm":
                        b = st[1]
                        sp.wait_ge(o_normed, BLOCKS[DIFF] * h.i + b + 2)
                        sp.dma_start(mixT[bass.ds(h.i + 4, 1), :, b * 512:(b + 1) * 512]
                                     .rearrange("o p n -> (o p) n"), o_sb[:, b % 2, :])\
                          .then_inc(o_stored[b % 2], 16)
            halves(sp, emit)
            for s in range(2):
                sp.wait_ge(o_stored[s], 16 * (1 + sum(BLOCKS) * DIFF_HEADS // 2))

        @block.gpsimd
        def _(pool):
            pool.sem_inc(p_lo_pool, 4)
            pool.memset(power[:, :], -0.5).then_inc(const_pool, 1)
            pool.memset(mean[:, :], 1.0 / P).then_inc(const_pool, 1)
            pool.memset(made[:, :, :], 0.0).then_inc(const_pool, 1)
            pool.memset(nmax[:, :, :, 1, :], -MASKED).then_inc(const_pool, 1)
            pool.memset(rsum[:, :, :, 1, :], 0.0).then_inc(const_pool, 1)
            for t in (q2, k2):
                pool.memset(f32(t[0:64, :, :, :]), 0.0).then_inc(const_pool, 1)
            pool.wait_ge(const_pool, 3)
            for n, (compare, fill, step, mult) in enumerate(((ALU.not_equal, 1.0, -1, 1),
                                                             (ALU.is_ge, MASKED, -1, 1),
                                                             (ALU.is_ge, MASKED, 1, -1))):
                pool.affine_select(out=made[:, n, :], in_=made[:, n, :], compare_op=compare, fill=fill,
                                   base=0, pattern=[[step, P]], channel_multiplier=mult).then_inc(const_pool, 1)

            def emit(h):
                split_last, prep_last = None, None
                for st in h.steps:
                    if st[0] == "split" and on_pool(h.kind, st[1]) or st[0] == "o_var":
                        if prep_last is not None:
                            pool.wait_ge(lo_ready, 2 * (2 * h.n + prep_last) + 2)
                            prep_last = None
                    if st[0] == "prep":
                        if split_last is not None:
                            pool.wait_ge(p_lo_pool, h.lo_value(split_last, True))
                        prep_last = st[1]
                    elif st[0] == "split" and on_pool(h.kind, st[1]):
                        split_last = st[1]
                    if st[0] == "prep":
                        s = st[1]
                        base = 3 * (2 * h.n + s)
                        if s == 0 and h.kind is not None:
                            pool.wait_ge(p_lo_pool, h.lo_value(split_last if split_last is not None else -1, True))
                        pool.wait_ge(hi_ready, base + 2)
                        pool.tensor_tensor(q1[64:P, h.slot, s, :], stage_a[64:P, :], f32(q2[64:P, h.slot, s, :]),
                                           ALU.subtract).then_inc(lo_ready, 1)
                        pool.wait_ge(hi_ready, base + 3)
                        pool.tensor_tensor(k2[64:P, h.slot, s, :], stage_b[64:P, :], f32(k1[64:P, h.slot, s, :]),
                                           ALU.subtract).then_inc(lo_ready, 1)
                    elif st[0] == "split" and on_pool(h.kind, st[1]):
                        m = st[1]
                        _, J, j = block_of(h.kind, m)
                        off = width(J, j)
                        c = m if h.kind == FOX else 2 * m
                        ring = (m + COMBOS[FOX] * h.kind) % SRING
                        pool.wait_ge(p_hi_ready, h.combo + m + 1)
                        pool.tensor_tensor(p_lo[:, ring, off:512], probs[:, c % PRING, off:512],
                                           f32(p_hi[:, ring, off:512]), ALU.subtract).then_inc(p_lo_pool, 1)
                    elif st[0] == "o_var":
                        pool.wait_ge(x_free, h.x + xpos(h, st) + 1)
                        pool.tensor_tensor(var[:, :], var[:, :], power[:, 0:1].to_broadcast([P, 512]),
                                           ALU.pow).then_inc(var_ready, 1)
            halves(pool, emit)

        @block.scalar
        def _(act):
            act.sem_inc(exped, 2)
            act.wait_ge(const_dve, 5)
            act.activation(lam_s[:, 2:4], lam_s[:, 0:2], ACT.Exp).then_inc(const_act, 1)

            def emit(h):
                for st in h.steps:
                    op = st[0]
                    if op == "stat_exp":
                        g = st[1]
                        s, qt, ch = stats[g]
                        n = min(1024, P * (qt + 1) - 1024 * ch)
                        act.wait_ge(stat_maxed, STAT * h.n + g + 1)
                        act.activation(ps_stat[:, g % 2, 0:n], ps_stat[:, g % 2, 0:n], ACT.Exp,
                                       bias=nmax[:, h.slot, s, ch, qt:qt + 1],
                                       accum_out=rsum[:, h.slot, s, ch, qt:qt + 1]).then_inc(stat_exped, 1)
                    elif op == "stat_corr":
                        act.wait_ge(stat_dve, 8 * (2 * h.n + st[1]) + 2)
                        act.activation(corr[:, :, :], corr[:, :, :], ACT.Exp).then_inc(stat_act, 1)
                    elif op == "stat_ln":
                        act.wait_ge(stat_dve, 8 * (2 * h.n + st[1]) + 4)
                        act.activation(logsum[:, :], total[:, :], ACT.Ln).then_inc(stat_act, 1)
                    elif op == "v_split":
                        g = st[1]
                        act.wait_ge(x_ready, h.x + xpos(h, ("v_flip", g)) + 1)
                        src = ps_x[:, :].rearrange("p (t v) -> p t v", v=P)
                        if h.prep_kind == FOX:
                            for s in range(2):
                                last = act.activation(vals[:, h.slot, 4 * g:4 * g + 4, s * P:s * P + 64],
                                                      src[:, :, s * 64:(s + 1) * 64], ACT.Copy)
                            last.then_inc(v_hi_ready, 1)
                        else:
                            act.activation(vals[:, h.slot, 4 * g:4 * g + 4, 0:P], src, ACT.Copy)\
                               .then_inc(v_hi_ready, 1)
                    elif op == "exp":
                        c = st[1]
                        _, J, j = raws[h.kind][c]
                        off = width(J, j)
                        act.wait_ge(scored, h.raw + c + 2)
                        m = (c - PRING) if h.kind == FOX else (c - PRING) // 2
                        if m < 0:
                            m = -(-(PRING - c) // 2) * -1 if h.kind == FOX else c - PRING
                            pool = on_pool(1 - h.kind, m + COMBOS[1 - h.kind])
                        else:
                            pool = on_pool(h.kind, m)
                        act.wait_ge(p_lo_pool if pool else p_lo_dve, h.lo_value(m, pool))
                        act.activation(probs[:, c % PRING, off:512], ps_sc[:, c % 2, off:512], ACT.Exp)\
                           .then_inc(exped, 1)
                    elif op == "o_first" and h.kind == FOX:
                        b = st[1]
                        act.wait_ge(p_used, h.combo + block_last(FOX, b) + 1 + SRING)
                        act.wait_ge(o_free, h.block + b + 1)
                        if b == 0:
                            act.wait_ge(o_normed, BLOCKS[DIFF] * h.i + 1)
                        act.activation(o_half[0:64, :], ps_o[64:P, :], ACT.Copy).then_inc(o_half_ready, 1)
                    elif op == "o_first":
                        b = st[1]
                        act.wait_ge(o_free, h.block + b + 2)
                        if b:
                            act.wait_ge(o_normed, BLOCKS[DIFF] * h.i + b + 1)
                        act.activation(o_half[:, :], o_sb[:, b % 2, :], ACT.Square).then_inc(o_squared, 1)
            halves(act, emit)

        @block.vector
        def _(dve):
            dve.sem_inc(p_lo_dve, 4)
            dve.sem_inc(o_free, 1)
            dve.sem_inc(o_normed, 1)
            for s in range(2):
                dve.sem_inc(o_stored[s], 16)
            dve.wait_ge(const_pool, 10)
            for n, t in enumerate((ident_r, mask_q, mask_k)):
                dve.tensor_copy(t[:, :], made[:, n, :]).then_inc(const_dve, 1)
            dve.wait_ge(const_loaded, 80)
            lam_v = lam_in[:, :, :].rearrange("p (a b) d -> p a b d", b=2)
            dve.tensor_tensor(lam_v[:, :, 0, :], lam_v[:, :, 0, :], lam_v[:, :, 1, :], ALU.mult)\
               .then_inc(const_dve, 1)
            dve.wait_ge(const_dve, 4)
            dve.tensor_reduce(lam_s[:, 0:2], lam_v[:, :, 0, :], AX.X, ALU.add).then_inc(const_dve, 1)
            dve.wait_ge(const_act, 1)
            dve.tensor_tensor(nlam[:, :], lam_s[:, 3:4], lam_s[:, 2:3], ALU.subtract).then_inc(const_dve, 1)
            dve.wait_ge(const_dve, 6)
            dve.tensor_scalar(nlam[:, :], nlam[:, :], LAM_INIT, None, ALU.subtract).then_inc(const_dve, 1)
            dve.tensor_scalar(gsub[:, :], gsub[:, :], 1.0 - LAM_INIT, None, ALU.mult).then_inc(const_dve, 1)
            dve.wait_ge(const_dve, 8)

            def emit(h):
                for st in h.steps:
                    op = st[0]
                    if op == "prep":
                        s = st[1]
                        base = 3 * (2 * h.n + s)
                        dve.wait_ge(a_loaded, 32 * (3 * h.n + s + 1))
                        if h.kind is not None:
                            dve.wait_ge(scored, h.raw + 1)
                        dve.tensor_copy(q1[:, h.slot, s, :], stage_a[:, :]).then_inc(hi_ready, 1)
                        dve.wait_ge(hi_ready, base + 1)
                        dve.tensor_copy(q2[64:P, h.slot, s, :], f32(q1[64:P, h.slot, s, :])).then_inc(hi_ready, 1)
                        dve.wait_ge(b_loaded, 32 * (2 * h.n + s + 1))
                        dve.tensor_copy(k1[:, h.slot, s, :], stage_b[:, :]).then_inc(hi_ready, 1)
                    elif op == "stat_exp":
                        g = st[1]
                        s, qt, ch = stats[g]
                        n = min(1024, P * (qt + 1) - 1024 * ch)
                        dve.wait_ge(stat_scored, STAT * h.n + g + 1)
                        dve.tensor_reduce(nmax[:, h.slot, s, ch, qt:qt + 1], ps_stat[:, g % 2, 0:n], AX.X,
                                          ALU.max, negate=True).then_inc(stat_maxed, 1)
                    elif op.startswith("stat_") and op not in ("stat_scores", "stat_rows"):
                        s = st[1]
                        base = 8 * (2 * h.n + s)
                        act_base = 2 * (2 * h.n + s)
                        nm, rs = nmax[:, h.slot, s], rsum[:, h.slot, s]
                        if op == "stat_max":
                            dve.wait_ge(stat_exped, STAT * h.n + 24 * (s + 1))
                            dve.tensor_tensor(top[:, :], nm[:, 0, :], nm[:, 1, :], ALU.min).then_inc(stat_dve, 1)
                            dve.wait_ge(stat_dve, base + 1)
                            dve.tensor_tensor(corr[:, :, :], top[:, :].unsqueeze(1).to_broadcast([P, 2, RT]), nm,
                                              ALU.subtract).then_inc(stat_dve, 1)
                        elif op == "stat_sum":
                            dve.wait_ge(stat_act, act_base + 1)
                            dve.tensor_tensor(corr[:, :, :], corr[:, :, :], rs, ALU.mult).then_inc(stat_dve, 1)
                            dve.wait_ge(stat_dve, base + 3)
                            dve.tensor_tensor(total[:, :], corr[:, 0, :], corr[:, 1, :], ALU.add)\
                               .then_inc(stat_dve, 1)
                        elif op == "stat_shift":
                            dve.wait_ge(stat_act, act_base + 2)
                            dve.tensor_tensor(total[:, :], top[:, :], logsum[:, :], ALU.subtract)\
                               .then_inc(stat_dve, 1)
                            dve.wait_ge(stat_dve, base + 5)
                            dve.tensor_copy(shift[:, 0:RT], total[:, :]).then_inc(stat_dve, 1)
                            dve.wait_ge(stat_dve, base + 6)
                            dve.tensor_tensor(shift[:, RT:2 * RT], total[:, :], f32(shift[:, 0:RT]),
                                              ALU.subtract).then_inc(stat_dve, 1)
                        elif op == "stat_flip":
                            dve.wait_ge(x_ready, h.x + xpos(h, st) + 1)
                            if h.kind is not None:
                                dve.wait_ge(shift_loaded[s], 32 * h.n)
                            dve.tensor_copy(shiftT[:, s, :], ps_x[0:2 * RT, 0:P]).then_inc(stat_dve, 1)
                            dve.wait_ge(stat_dve, base + 8)
                            dve.sem_inc(x_free, 1)
                    elif op == "v_split":
                        g = st[1]
                        dve.wait_ge(v_hi_ready, 4 * h.n + g + 1)
                        src = ps_x[:, :].rearrange("p (t v) -> p t v", v=P)
                        t4 = slice(4 * g, 4 * g + 4)
                        if h.prep_kind == FOX:
                            for s in range(2):
                                last = dve.tensor_tensor(vals[:, h.slot, t4, s * P + 64:(s + 1) * P],
                                                         src[:, :, s * 64:(s + 1) * 64],
                                                         f32(vals[:, h.slot, t4, s * P:s * P + 64]), ALU.subtract)
                        else:
                            last = dve.tensor_tensor(vals[:, h.slot, t4, P:2 * P], src,
                                                     f32(vals[:, h.slot, t4, 0:P]), ALU.subtract)
                        last.then_inc(x_free, 1)
                    elif op == "split":
                        m = st[1]
                        _, J, j = block_of(h.kind, m)
                        off = width(J, j)
                        c = m if h.kind == FOX else 2 * m
                        ring = (m + COMBOS[FOX] * h.kind) % SRING
                        if h.kind == FOX:
                            dve.wait_ge(exped, h.raw + c + 3)
                        else:
                            dve.wait_ge(exped, h.raw + c + 4)
                            dve.scalar_tensor_tensor(out=probs[:, c % PRING, off:512],
                                                     in0=probs[:, (c + 1) % PRING, off:512], scalar=nlam[:, :],
                                                     in1=probs[:, c % PRING, off:512],
                                                     op0=ALU.mult, op1=ALU.add).then_inc(combined, 1)
                            dve.wait_ge(combined, COMBOS[DIFF] * h.i + m + 1)
                        dve.wait_ge(p_used, h.combo + m + 1)
                        dve.tensor_copy(p_hi[:, ring, off:512], probs[:, c % PRING, off:512])\
                           .then_inc(p_hi_ready, 1)
                        if not on_pool(h.kind, m):
                            dve.wait_ge(p_hi_ready, h.combo + m + 1)
                            dve.tensor_tensor(p_lo[:, ring, off:512], probs[:, c % PRING, off:512],
                                              f32(p_hi[:, ring, off:512]), ALU.subtract).then_inc(p_lo_dve, 1)
                    elif op == "o_first":
                        b = st[1]
                        dve.wait_ge(o_stored[b % 2], 8 * sum(BLOCKS) * h.i
                                    + (16 * (b // 2 + 1) + 8 * BLOCKS[FOX] * h.kind))
                        if h.kind == FOX:
                            dve.wait_ge(o_half_ready, BLOCKS[FOX] * h.i + b + 1)
                            dve.tensor_tensor(o_sb[0:64, b % 2, :], ps_o[0:64, :], o_half[0:64, :], ALU.add)\
                               .then_inc(o_free, 1)
                        else:
                            dve.wait_ge(p_used, h.combo + block_last(DIFF, b) + 1 + SRING)
                            dve.tensor_copy(o_sb[:, b % 2, :], ps_o[:, :]).then_inc(o_free, 1)
                    elif op == "o_var":
                        dve.wait_ge(x_ready, h.x + xpos(h, st) + 1)
                        dve.tensor_scalar(var[:, :], ps_x[:, :], EPS, None, ALU.add).then_inc(x_free, 1)
                    elif op == "o_norm":
                        b = st[1]
                        dve.wait_ge(var_ready, BLOCKS[DIFF] * h.i + b + 1)
                        dve.scalar_tensor_tensor(out=o_sb[:, b % 2, :], in0=o_sb[:, b % 2, :], scalar=gsub[:, :],
                                                 in1=var[:, :], op0=ALU.mult, op1=ALU.mult)\
                           .then_inc(o_normed, 1)
            halves(dve, emit)

        @block.tensor
        def _(pe):
            pe.sem_inc(scored, 1)
            pe.sem_inc(p_used, SRING)
            pe.wait_ge(const_dve, 3)

            def claim_x(h, st):
                if h.kind is not None or xpos(h, st):
                    pe.wait_ge(x_free, h.x + xpos(h, st))

            def emit(h):
                for st in h.steps:
                    op = st[0]
                    if op == "stat_scores":
                        g = st[1]
                        s, qt, ch = stats[g]
                        if g % 24 == 0:
                            pe.wait_ge(lo_ready, 2 * (2 * h.n + s + 1))
                            pe.wait_ge(rows_loaded, 64 * (h.n + 1))
                        if h.kind is not None or g > 1:
                            pe.wait_ge(stat_exped, STAT * h.n + g - 1)
                        n = P * (qt + 1) - 1024 * ch
                        q = slice(qt * P, (qt + 1) * P)
                        last = None
                        for w0 in range(0, min(n, 1024), 512):
                            w1 = min(n, w0 + 512)
                            out = ps_stat[:, g % 2, w0:w1]
                            keys = slice(1024 * ch + w0, 1024 * ch + w1)
                            pe.matmul(out, q2[:, h.slot, s, q], k2[:, h.slot, s, keys], start=True, stop=False)
                            if w1 == n:
                                pe.matmul(ps_stat[:, g % 2, n - P:n], ident_r[:, :], mask_q[:, :],
                                          start=False, stop=False)
                            last = pe.matmul(out, q1[:, h.slot, s, q], k1[:, h.slot, s, keys],
                                             start=False, stop=True)
                        last.then_inc(stat_scored, 1)
                    elif op == "stat_flip":
                        s = st[1]
                        pe.wait_ge(stat_dve, 8 * (2 * h.n + s) + 7)
                        claim_x(h, st)
                        pe.transpose(ps_x[0:2 * RT, 0:P], f32(shift[:, :]), ident).then_inc(x_ready, 1)
                    elif op == "v_flip":
                        g = st[1]
                        pe.wait_ge(a_loaded, 32 * (3 * h.n + 3))
                        claim_x(h, st)
                        for t in range(4):
                            last = pe.transpose(ps_x[:, t * P:(t + 1) * P],
                                                stage_a[:, (4 * g + t) * P:(4 * g + t + 1) * P], ident)
                        last.then_inc(x_ready, 1)
                    elif op == "scores":
                        c = st[1]
                        s, J, j = raws[h.kind][c]
                        slot = h.kind
                        off = width(J, j)
                        if c == 0 or (c == 1 and h.kind == DIFF) or (h.kind == FOX and c == RAW // 2):
                            pe.wait_ge(shift_loaded[s], h.shift_value)
                        pe.wait_ge(exped, h.raw + c + 1)
                        out = ps_sc[:, c % 2, off:512]
                        keys = slice(j * P, (j + 1) * P)
                        qs = slice(J * 512 + off, (J + 1) * 512)
                        pe.matmul(out, k2[:, slot, s, keys], q2[:, slot, s, qs], start=True, stop=False)
                        if j >= 4 * J:
                            pe.matmul(ps_sc[:, c % 2, off:off + P], ident_r[:, :], mask_k[:, :],
                                      start=False, stop=False)
                        pe.matmul(out, k1[:, slot, s, keys], q1[:, slot, s, qs], start=False, stop=True)\
                          .then_inc(scored, 1)
                    elif op == "pv":
                        m = st[1]
                        s, J, j = block_of(h.kind, m)
                        off = width(J, j)
                        slot = h.kind
                        ring = (m + COMBOS[FOX] * h.kind) % SRING
                        pool = on_pool(h.kind, m)
                        pe.wait_ge(p_lo_pool if pool else p_lo_dve, h.lo_value(m, pool))
                        out = ps_o[:, off:512]
                        if j == 0:
                            b = (4 * s + J) if h.kind == FOX else J
                            pe.wait_ge(o_free, h.block + b + 1)
                        end = j == 4 * J + 3
                        if h.kind == FOX:
                            v = vals[:, slot, j, s * P:(s + 1) * P]
                            pe.matmul(out, v, p_hi[:, ring, off:512], start=(j == 0), stop=False)
                            pe.matmul(out, v, p_lo[:, ring, off:512], start=False, stop=end).then_inc(p_used, 1)
                        else:
                            v_hi, v_lo = vals[:, slot, j, 0:P], vals[:, slot, j, P:2 * P]
                            pe.matmul(out, v_hi, p_hi[:, ring, off:512], start=(j == 0), stop=False)
                            pe.matmul(out, v_lo, p_hi[:, ring, off:512], start=False, stop=False)
                            pe.matmul(out, v_hi, p_lo[:, ring, off:512], start=False, stop=end)\
                              .then_inc(p_used, 1)
                    elif op == "o_var":
                        b = st[1]
                        pe.wait_ge(o_squared, BLOCKS[DIFF] * h.i + b + 1)
                        claim_x(h, st)
                        pe.matmul(ps_x[:, :], mean[:, :], o_half[:, :], start=True, stop=True).then_inc(x_ready, 1)
            halves(pe, emit)


def mix_out(nc, mixT, w_out, x, g_post_mix, g_pre_mlp, x2, h2T):
    with ExitStack() as ctx:
        r = Room(nc, ctx, "mo")
        w_raw = r.sb("w_raw", [P, 2, D])
        w_hi = r.sb("w_hi", [P, KT, D], F32R)
        w_lo = r.sb("w_lo", [P, KT, D], F32R)
        m_raw = r.sb("m_raw", [P, 2, KT, P])
        m_hi = r.sb("m_hi", [P, 2, KT, P], F32R)
        m_lo = r.sb("m_lo", [P, 2, KT, P], F32R)
        xin = r.sb("xin", [P, 2, D])
        y = r.sb("y", [P, 2, D])
        xn = r.sb("xn", [P, 2, D])
        h_hi = r.sb("h_hi", [P, 2, KT, P], F32R)
        h_lo = r.sb("h_lo", [P, 2, KT, P], F32R)
        g_post = r.sb("g_post", [P, D])
        g_pre = r.sb("g_pre", [P, D])
        ident = r.sb("ident", [P, P])
        power = r.sb("power", [P, 1])
        eps = r.sb("eps", [P, 1])
        ss = r.sb("ss", [P, 2, RT])
        rstd = r.sb("rstd", [P, 2, RT])
        acc = r.ps("acc", [P, 2, D])
        flip = r.ps("flip", [P, 2, D])
        const_ready = r.sem("const_ready")
        gains_loaded = r.sem("gains_loaded")
        w_loaded = [r.sem(f"w_loaded{s}") for s in range(2)]
        w_hi_ready = r.sem("w_hi_ready")
        w_ready = r.sem("w_ready")
        m_loaded = [r.sem(f"m_loaded{s}") for s in range(2)]
        x_loaded = [r.sem(f"x_loaded{s}") for s in range(2)]
        m_hi_ready = r.sem("m_hi_ready")
        m_ready = r.sem("m_ready")
        multiplied = r.sem("multiplied")
        ss_ready = r.sem("ss_ready")
        rstd_step = r.sem("rstd_step")
        y_step = r.sem("y_step")
        xn_ready = r.sem("xn_ready")
        flipped = r.sem("flipped")
        h_hi_ready = r.sem("h_hi_ready")
        h_ready = r.sem("h_ready")
        stored = [r.sem(f"stored{s}") for s in range(2)]
        block = ctx.enter_context(nc.Block())
        LAST = RT // 2

        @block.sync
        def _(sp):
            for s in range(2):
                sp.dma_start(w_raw[:, s, :], w_out[0, s * P:(s + 1) * P, :]).then_inc(w_loaded[s], 16)
            sp.dma_start(m_raw[:, 0], mixT[:, :, 0:P].rearrange("k p n -> p k n")).then_inc(m_loaded[0], 16)
            for k in range(2, KT):
                sp.wait_ge(w_ready, k - 1)
                sp.dma_start(w_raw[:, k % 2, :], w_out[0, k * P:(k + 1) * P, :]).then_inc(w_loaded[k % 2], 16)
            sp.dma_start(g_post[:, :], g_post_mix[0:1, :].to_broadcast([P, D])).then_inc(gains_loaded, 16)
            sp.dma_start(g_pre[:, :], g_pre_mlp[0:1, :].to_broadcast([P, D])).then_inc(gains_loaded, 16)
            sp.dma_start(xin[:, 0, :], x[0, 0:P, :]).then_inc(x_loaded[0], 16)
            sp.dma_start(m_raw[:, 1], mixT[:, :, P:2 * P].rearrange("k p n -> p k n")).then_inc(m_loaded[1], 16)
            sp.dma_start(xin[:, 1, :], x[0, P:2 * P, :]).then_inc(x_loaded[1], 16)
            with sp.Fori(0, LAST - 1) as i:
                for s in range(2):
                    t = 2 * i + s + 2
                    sp.wait_ge(m_ready, t + 1)
                    sp.dma_start(m_raw[:, s], mixT[:, :, bass.ts(t, P)].rearrange("k p n -> p k n"))\
                      .then_inc(m_loaded[s], 16)
                    sp.wait_ge(y_step, 2 * (t - 1))
                    sp.dma_start(xin[:, s, :], x[0, bass.ts(t, P), :]).then_inc(x_loaded[s], 16)

        @block.gpsimd
        def _(pool):
            pool.memset(ident[:, :], 0.0).then_inc(const_ready, 1)
            pool.memset(power[:, :], -0.5).then_inc(const_ready, 1)
            pool.memset(eps[:, :], EPS).then_inc(const_ready, 1)
            pool.wait_ge(const_ready, 1)
            pool.affine_select(out=ident[:, :], in_=ident[:, :], compare_op=ALU.not_equal, fill=1.0,
                               base=0, pattern=[[-1, P]], channel_multiplier=1).then_inc(const_ready, 1)
            pool.wait_ge(const_ready, 4)
            with pool.Fori(0, RT) as t:
                for n in range(2):
                    pool.wait_ge(ss_ready, 2 * t + n + 1)
                    pool.tensor_tensor(ss[:, n, bass.ds(t, 1)], ss[:, n, bass.ds(t, 1)], eps[:, :], ALU.add)\
                        .then_inc(rstd_step, 1)
                    pool.wait_ge(rstd_step, 4 * t + 2 * n + 1)
                    pool.tensor_tensor(rstd[:, n, bass.ds(t, 1)], ss[:, n, bass.ds(t, 1)], power[:, :],
                                       ALU.pow).then_inc(rstd_step, 1)

        @block.scalar
        def _(act):
            for s in range(2):
                act.sem_inc(stored[s], 48)

            def tile(i, s, t):
                act.wait_ge(multiplied, t + 3)
                act.wait_ge(xn_ready, t + 1)
                act.wait_ge(flipped, t + 1)
                act.activation(xn[:, s, :], acc[:, s, :], ACT.Square, scale=ROOT, accum_out=ss[:, 0, bass.ds(t, 1)])\
                   .then_inc(ss_ready, 1)
                act.wait_ge(y_step, 2 * t + 2)
                act.activation(xn[:, s, :], y[:, s, :], ACT.Square, scale=ROOT, accum_out=ss[:, 1, bass.ds(t, 1)])\
                   .then_inc(ss_ready, 1)
                act.dma_start(x2[bass.ts(t, P), :], y[:, s, :]).then_inc(stored[s], 16)

            def keep(i, s, t):
                act.wait_ge(flipped, t + 3)
                act.wait_ge(stored[s], 16 * (3 * i + 4))
                act.activation(h_hi[:, s], flip[:, s, :].rearrange("p (k r) -> p k r", r=P), ACT.Copy)\
                   .then_inc(h_hi_ready, 1)
                act.wait_ge(h_ready, t + 3)
                for n, src in enumerate((h_hi, h_lo)):
                    act.dma_start(h2T[n, :, :, bass.ts(t, P)].rearrange("k p n -> p k n"), f32(src[:, s]))\
                       .then_inc(stored[s], 16)
            act.sem_inc(flipped, 2)
            tile(0, 0, 0)
            with act.Fori(0, LAST - 1) as i:
                tile(i, 1, 2 * i + 1)
                keep(i, 0, 2 * i)
                tile(i + 1, 0, 2 * i + 2)
                keep(i, 1, 2 * i + 1)
            tile(LAST - 1, 1, RT - 1)
            keep(LAST - 1, 0, RT - 2)
            keep(LAST - 1, 1, RT - 1)
            for s in range(2):
                act.wait_ge(stored[s], 48 * (LAST + 1))

        @block.vector
        def _(dve):
            dve.sem_inc(m_ready, 2)
            dve.sem_inc(xn_ready, 2)
            dve.sem_inc(h_ready, 2)

            def split_mix(i, s, t):
                dve.wait_ge(m_loaded[s], 16 * (i + 1))
                dve.wait_ge(multiplied, t + 1)
                dve.tensor_copy(m_hi[:, s], m_raw[:, s]).then_inc(m_hi_ready, 1)
                dve.wait_ge(m_hi_ready, t + 1)
                dve.tensor_tensor(m_lo[:, s], m_raw[:, s], f32(m_hi[:, s]), ALU.subtract).then_inc(m_ready, 1)

            def norms(i, s, t):
                dve.wait_ge(rstd_step, 4 * t + 2)
                dve.wait_ge(stored[s], 48 * (i + 1))
                dve.scalar_tensor_tensor(out=y[:, s, :], in0=acc[:, s, :], scalar=rstd[:, 0, bass.ds(t, 1)],
                                         in1=g_post[:, :], op0=ALU.mult, op1=ALU.mult).then_inc(y_step, 1)
                dve.wait_ge(x_loaded[s], 16 * (i + 1))
                dve.wait_ge(y_step, 2 * t + 1)
                dve.tensor_tensor(y[:, s, :], y[:, s, :], xin[:, s, :], ALU.add).then_inc(y_step, 1)

            def pre_norm(i, s, t):
                dve.wait_ge(rstd_step, 4 * t + 4)
                dve.scalar_tensor_tensor(out=xn[:, s, :], in0=y[:, s, :], scalar=rstd[:, 1, bass.ds(t, 1)],
                                         in1=g_pre[:, :], op0=ALU.mult, op1=ALU.mult).then_inc(xn_ready, 1)

            def keep_lo(s, t):
                dve.wait_ge(h_hi_ready, t + 1)
                dve.tensor_tensor(h_lo[:, s], flip[:, s, :].rearrange("p (k r) -> p k r", r=P),
                                  f32(h_hi[:, s]), ALU.subtract).then_inc(h_ready, 1)

            for k in range(KT):
                dve.wait_ge(w_loaded[k % 2], 16 * (k // 2 + 1))
                dve.tensor_copy(w_hi[:, k, :], w_raw[:, k % 2, :]).then_inc(w_hi_ready, 1)
                dve.wait_ge(w_hi_ready, k + 1)
                dve.tensor_tensor(w_lo[:, k, :], w_raw[:, k % 2, :], f32(w_hi[:, k, :]), ALU.subtract)\
                   .then_inc(w_ready, 1)
            dve.wait_ge(gains_loaded, 32)
            split_mix(0, 0, 0)
            split_mix(0, 1, 1)
            norms(0, 0, 0)
            pre_norm(0, 0, 0)
            with dve.Fori(0, LAST - 1) as i:
                split_mix(i + 1, 0, 2 * i + 2)
                norms(i, 1, 2 * i + 1)
                keep_lo(0, 2 * i)
                pre_norm(i, 1, 2 * i + 1)
                split_mix(i + 1, 1, 2 * i + 3)
                norms(i + 1, 0, 2 * i + 2)
                keep_lo(1, 2 * i + 1)
                pre_norm(i + 1, 0, 2 * i + 2)
            norms(LAST - 1, 1, RT - 1)
            keep_lo(0, RT - 2)
            pre_norm(LAST - 1, 1, RT - 1)
            keep_lo(1, RT - 1)

        @block.tensor
        def _(pe):
            pe.sem_inc(multiplied, 2)

            def multiply(i, s, t):
                pe.wait_ge(m_ready, t + 3)
                if not isinstance(t, int) or t > 1:
                    pe.wait_ge(y_step, 2 * t - 3)
                for b in range(D // 512):
                    cols = slice(b * 512, (b + 1) * 512)
                    for k in range(KT):
                        pe.matmul(acc[:, s, cols], m_hi[:, s, k], w_hi[:, k, cols], start=(k == 0), stop=False)
                        pe.matmul(acc[:, s, cols], m_hi[:, s, k], w_lo[:, k, cols], start=False, stop=False)
                        last = pe.matmul(acc[:, s, cols], m_lo[:, s, k], w_hi[:, k, cols],
                                         start=False, stop=(k == KT - 1))
                last.then_inc(multiplied, 1)

            def transpose(s, t):
                pe.wait_ge(xn_ready, t + 3)
                pe.wait_ge(h_ready, t + 1)
                for k in range(KT):
                    last = pe.transpose(flip[:, s, k * P:(k + 1) * P], xn[:, s, k * P:(k + 1) * P], ident[:, :])
                last.then_inc(flipped, 1)
            pe.wait_ge(w_ready, KT)
            pe.wait_ge(const_ready, 4)
            multiply(0, 0, 0)
            multiply(0, 1, 1)
            transpose(0, 0)
            with pe.Fori(0, LAST - 1) as i:
                multiply(i, 0, 2 * i + 2)
                transpose(1, 2 * i + 1)
                multiply(i, 1, 2 * i + 3)
                transpose(0, 2 * i + 2)
            transpose(1, RT - 1)


def mlp(nc, h2T, w_up, w_down, x2, g_post_mlp, out):
    SW = S // 2
    ST = SW // P
    FC = 256
    FT = FC // P
    NC = DFF // FC
    RB = SW // 512
    UB = FT * RB
    YB = ST * D // 512
    with ExitStack() as ctx:
        r = Room(nc, ctx, "ml")
        h_hi = r.sb("h_hi", [P, KT, SW], F32R)
        h_lo = r.sb("h_lo", [P, KT, SW], F32R)
        y = r.sb("y", [P, ST, D])
        u_hi = r.sb("u_hi", [P, 2, FT, SW], F32R)
        u_lo = r.sb("u_lo", [P, 2, FT, SW], F32R)
        up_raw = r.sb("up_raw", [P, KT, FC])
        up_hi = r.sb("up_hi", [P, KT, FC], F32R)
        up_lo = r.sb("up_lo", [P, KT, FC], F32R)
        dn_raw = r.sb("dn_raw", [P, FT, D])
        dn_hi = r.sb("dn_hi", [P, FT, D], F32R)
        dn_lo = r.sb("dn_lo", [P, FT, D], F32R)
        relu = r.sb("relu", [P, 2, 512])
        gain = r.sb("gain", [P, D])
        xres = r.sb("xres", [P, D])
        junk = r.sb("junk", [P, D])
        power = r.sb("power", [P, 1])
        ss = r.sb("ss", [P, 2 * ST])
        rstd = r.sb("rstd", [P, 2 * ST])
        ps_u = r.ps("ps_u", [P, 4, 512])
        ps_y = r.ps("ps_y", [P, 4, 512])
        const_ready = r.sem("const_ready")
        gain_loaded = r.sem("gain_loaded")
        h_loaded = r.sem("h_loaded")
        up_loaded = r.sem("up_loaded")
        dn_loaded = r.sem("dn_loaded")
        up_split = r.sem("up_split")
        dn_split = r.sem("dn_split")
        up_done = r.sem("up_done")
        dn_done = r.sem("dn_done")
        relued = r.sem("relued")
        u_step = r.sem("u_step")
        y_added = r.sem("y_added")
        y_cleared = r.sem("y_cleared")
        ss_ready = r.sem("ss_ready")
        rstd_step = r.sem("rstd_step")
        x_loaded = r.sem("x_loaded")
        y_final = r.sem("y_final")
        stored = r.sem("stored")
        block = ctx.enter_context(nc.Block())
        up_v = w_up.rearrange("o (k p) f -> p (o k) f", p=P)
        dn_v = w_down.rearrange("o (k p) d -> p (o k) d", p=P)

        def chunks(eng, up, down):
            def sweep(w):
                up(w, 0, 0)
                with eng.Fori(0, NC // 2 - 1) as i:
                    up(w, 2 * i + 1, 1)
                    down(w, 2 * i, 0)
                    up(w, 2 * i + 2, 0)
                    down(w, 2 * i + 1, 1)
                up(w, NC - 1, 1)
                down(w, NC - 2, 0)
                down(w, NC - 1, 1)
            return sweep

        @block.sync
        def _(sp):
            sp.dma_start(gain[:, :], g_post_mlp[0:1, :].to_broadcast([P, D])).then_inc(gain_loaded, 16)

            def up(w, c, s):
                n = w * NC + c
                if isinstance(c, int) and c == 0:
                    if w:
                        sp.wait_ge(up_done, UB + UB * NC * w)
                    for k in range(KT):
                        for z, dst in enumerate((h_hi, h_lo)):
                            sp.dma_start(f32(dst[:, k, :]), h2T[z, k, :, w * SW:(w + 1) * SW]).then_inc(h_loaded, 16)
                sp.wait_ge(up_split, 2 * n + 2)
                sp.dma_start(up_raw[:, :, :], up_v[:, :, bass.ds(c * FC, FC)]).then_inc(up_loaded, 16)

            def down(w, c, s):
                n = w * NC + c
                sp.wait_ge(dn_split, 2 * n + 2)
                sp.dma_start(dn_raw[:, :, :], dn_v[:, bass.ds(c * FT, FT), :]).then_inc(dn_loaded, 16)
            sweep = chunks(sp, up, down)
            for w in range(2):
                sweep(w)
                for t in range(ST):
                    n = w * ST + t
                    if n:
                        sp.wait_ge(y_final, 2 * n)
                    sp.dma_start(xres[:, :], x2[n * P:(n + 1) * P, :]).then_inc(x_loaded, 16)
                    sp.wait_ge(y_final, 2 * n + 2)
                    sp.dma_start(out[0, n * P:(n + 1) * P, :], y[:, t, :]).then_inc(stored, 16)
            sp.wait_ge(stored, 16 * 2 * ST)

        @block.gpsimd
        def _(pool):
            pool.memset(power[:, :], -0.5).then_inc(const_ready, 1)
            pool.wait_ge(const_ready, 1)
            for w in range(2):
                if w:
                    pool.wait_ge(stored, 16 * ST)
                pool.memset(y[:, :, :], 0.0).then_inc(y_cleared, 1)
                for t in range(ST):
                    n = w * ST + t
                    pool.wait_ge(ss_ready, n + 1)
                    pool.tensor_scalar(ss[:, n:n + 1], ss[:, n:n + 1], EPS, None, ALU.add)\
                        .then_inc(rstd_step, 1)
                    pool.wait_ge(rstd_step, 2 * n + 1)
                    pool.tensor_tensor(rstd[:, n:n + 1], ss[:, n:n + 1], power[:, :], ALU.pow)\
                        .then_inc(rstd_step, 1)

        @block.scalar
        def _(act):
            act.sem_inc(relued, 4)

            def up(w, c, s):
                n = w * NC + c
                for b in range(UB):
                    g = n * UB + b
                    act.wait_ge(up_done, g + 1 + UB)
                    act.wait_ge(u_step, 3 * g + 3)
                    act.activation(relu[:, b % 2, :], ps_u[:, b % 4, :], ACT.Relu).then_inc(relued, 1)

            def down(w, c, s):
                pass
            sweep = chunks(act, up, down)
            for w in range(2):
                sweep(w)
                act.wait_ge(y_added, 4 + YB * NC * (w + 1))
                for t in range(ST):
                    n = w * ST + t
                    if n:
                        act.wait_ge(ss_ready, n)
                    act.activation(junk[:, :], y[:, t, :], ACT.Square, scale=ROOT, accum_out=ss[:, n:n + 1])\
                       .then_inc(ss_ready, 1)

        @block.vector
        def _(dve):
            dve.sem_inc(up_split, 2)
            dve.sem_inc(dn_split, 2)
            dve.sem_inc(u_step, 6)
            dve.sem_inc(y_added, 4)
            dve.wait_ge(gain_loaded, 16)

            def split(n, raw, hi, lo, loaded, sem):
                dve.wait_ge(loaded, 16 * (n + 1))
                dve.tensor_copy(hi[:, :, :], raw[:, :, :]).then_inc(sem, 1)
                dve.wait_ge(sem, 2 * n + 3)
                dve.tensor_tensor(lo[:, :, :], raw[:, :, :], f32(hi[:, :, :]), ALU.subtract).then_inc(sem, 1)

            def up(w, c, s):
                n = w * NC + c
                dve.wait_ge(up_done, UB * n + UB)
                split(n, up_raw, up_hi, up_lo, up_loaded, up_split)
                for b in range(UB):
                    g = n * UB + b
                    f, rb = b // RB, b % RB
                    rows = slice(rb * 512, (rb + 1) * 512)
                    dve.wait_ge(relued, g + 5)
                    if b == 0:
                        dve.wait_ge(dn_done, YB * n + 1)
                    dve.tensor_tensor(relu[:, b % 2, :], relu[:, b % 2, :], relu[:, b % 2, :], ALU.mult)\
                       .then_inc(u_step, 1)
                    dve.wait_ge(u_step, 3 * g + 7)
                    dve.tensor_copy(u_hi[:, s, f, rows], relu[:, b % 2, :]).then_inc(u_step, 1)
                    dve.wait_ge(u_step, 3 * g + 8)
                    dve.tensor_tensor(u_lo[:, s, f, rows], relu[:, b % 2, :], f32(u_hi[:, s, f, rows]),
                                      ALU.subtract).then_inc(u_step, 1)

            def down(w, c, s):
                n = w * NC + c
                dve.wait_ge(dn_done, YB * n + 2 * YB)
                split(n, dn_raw, dn_hi, dn_lo, dn_loaded, dn_split)
                if isinstance(c, int) and c == 0 or not isinstance(c, int):
                    dve.wait_ge(y_cleared, w + 1)
                for b in range(YB):
                    g = n * YB + b
                    t, half = b // 2, b % 2
                    cols = slice(half * 512, (half + 1) * 512)
                    dve.wait_ge(dn_done, g + 1 + 2 * YB)
                    dve.wait_ge(y_added, g + 4)
                    dve.tensor_tensor(y[:, t, cols], y[:, t, cols], ps_y[:, b % 4, :], ALU.add)\
                       .then_inc(y_added, 1)
            sweep = chunks(dve, up, down)
            for w in range(2):
                sweep(w)
                for t in range(ST):
                    n = w * ST + t
                    dve.wait_ge(rstd_step, 2 * n + 2)
                    dve.scalar_tensor_tensor(out=y[:, t, :], in0=y[:, t, :], scalar=rstd[:, n:n + 1],
                                             in1=gain[:, :], op0=ALU.mult, op1=ALU.mult).then_inc(y_final, 1)
                    dve.wait_ge(x_loaded, 16 * (n + 1))
                    dve.wait_ge(y_final, 2 * n + 1)
                    dve.tensor_tensor(y[:, t, :], y[:, t, :], xres[:, :], ALU.add).then_inc(y_final, 1)

        @block.tensor
        def _(pe):
            pe.sem_inc(up_done, UB)
            pe.sem_inc(dn_done, 2 * YB)

            def up(w, c, s):
                n = w * NC + c
                if isinstance(c, int) and c == 0:
                    pe.wait_ge(h_loaded, 16 * 2 * KT * (w + 1))
                pe.wait_ge(up_split, 2 * n + 4)
                for b in range(UB):
                    g = n * UB + b
                    f, rb = b // RB, b % RB
                    rows = slice(rb * 512, (rb + 1) * 512)
                    cols = slice(f * P, (f + 1) * P)
                    pe.wait_ge(relued, g + 1)
                    for k in range(KT):
                        pe.matmul(ps_u[:, b % 4, :], up_hi[:, k, cols], h_hi[:, k, rows],
                                  start=(k == 0), stop=False)
                        pe.matmul(ps_u[:, b % 4, :], up_hi[:, k, cols], h_lo[:, k, rows], start=False, stop=False)
                        last = pe.matmul(ps_u[:, b % 4, :], up_lo[:, k, cols], h_hi[:, k, rows],
                                         start=False, stop=(k == KT - 1))
                    last.then_inc(up_done, 1)

            def down(w, c, s):
                n = w * NC + c
                pe.wait_ge(dn_split, 2 * n + 4)
                pe.wait_ge(u_step, 6 + 3 * UB * (n + 1))
                for b in range(YB):
                    g = n * YB + b
                    t, half = b // 2, b % 2
                    cols = slice(half * 512, (half + 1) * 512)
                    rows = slice(t * P, (t + 1) * P)
                    pe.wait_ge(y_added, g + 1)
                    for f in range(FT):
                        pe.matmul(ps_y[:, b % 4, :], u_hi[:, s, f, rows], dn_hi[:, f, cols],
                                  start=(f == 0), stop=False)
                        pe.matmul(ps_y[:, b % 4, :], u_hi[:, s, f, rows], dn_lo[:, f, cols],
                                  start=False, stop=False)
                        last = pe.matmul(ps_y[:, b % 4, :], u_lo[:, s, f, rows], dn_hi[:, f, cols],
                                         start=False, stop=(f == FT - 1))
                    last.then_inc(dn_done, 1)
            sweep = chunks(pe, up, down)
            for w in range(2):
                sweep(w)


def hybrid_block(nc, x, g_pre_mix, w_in, b_forget, lambda_q1, lambda_k1, lambda_q2, lambda_k2,
                 g_subln, w_out, g_post_mix, g_pre_mlp, w_up, w_down, g_post_mlp, out):
    qkvT = nc.dram_tensor("qkvT", [QKV_TILES + 1, P, S], F32).ap()
    q_rows = nc.dram_tensor("q_rows", [FOX_HEADS + DIFF_HEADS, 6, S], F32).ap()
    k_rows = nc.dram_tensor("k_rows", [FOX_HEADS + DIFF_HEADS, 6, S], F32).ap()
    mixT = nc.dram_tensor("mixT", [KT, P, S], F32).ap()
    x2 = nc.dram_tensor("x2", [S, D], F32).ap()
    h2T = nc.dram_tensor("h2T", [2, KT, P, S], F32).ap()
    project(nc, x, g_pre_mix, w_in, qkvT)
    decay(nc, qkvT, b_forget, q_rows, k_rows)
    attend(nc, qkvT, q_rows, k_rows, (lambda_q1, lambda_k1, lambda_q2, lambda_k2), g_subln, mixT)
    mix_out(nc, mixT, w_out, x, g_post_mix, g_pre_mlp, x2, h2T)
    mlp(nc, h2T, w_up, w_down, x2, g_post_mlp, out)


_INS = ["x", "g_pre_mix", "w_in", "b_forget", "lambda_q1", "lambda_k1", "lambda_q2", "lambda_k2",
        "g_subln", "w_out", "g_post_mix", "g_pre_mlp", "w_up", "w_down", "g_post_mlp"]


def kernel(**inputs):
    import numpy as _np
    import concourse.bacc as _bacc
    from concourse import mybir as _mybir
    from concourse.bass_utils import run_bass_kernel_spmd as _run

    nc = _bacc.Bacc("TRN2", target_bir_lowering=False, num_devices=1)
    arrays, args = {}, []
    for name in _INS:
        a = _np.ascontiguousarray(inputs[name])
        arrays[f"in_{name}_dram"] = a
        args.append(nc.dram_tensor(f"in_{name}_dram", a.shape, _mybir.dt.from_np(a.dtype), kind="ExternalInput").ap())
    args.append(nc.dram_tensor("out_0_dram", (1, S, D), _mybir.dt.float32, kind="ExternalOutput").ap())
    hybrid_block(nc, *args)
    r = _run(nc, [arrays], core_ids=[0])
    return r.results[0]["out_0_dram"]
```

```python
from contextlib import ExitStack

import concourse.bass as bass
from concourse import mybir

F32 = mybir.dt.float32
F32R = mybir.dt.float32r
ALU = mybir.AluOpType
ACT = mybir.ActivationFunctionType
AX = mybir.AxisListType

P = 128
D = 1024
S = 2048
KT = D // P
RT = S // P
HD = 64
DFF = 4 * D
EPS = 1e-6
FOX_HEADS = 8
DIFF_HEADS = 4
LAM_INIT = 0.2
LOGIT_COL = 3 * FOX_HEADS * HD
QKV_TILES = 24
ROOT = D ** -0.5
MASKED = -float(2 ** 100)


def f32(ap):
    return ap.bitcast(F32)


class Room:

    def __init__(self, nc, ctx, stage):
        self.nc, self.ctx, self.stage = nc, ctx, stage

    def sb(self, name, shape, dt=F32):
        return self.ctx.enter_context(self.nc.sbuf_tensor(f"{self.stage}_{name}", shape, dt))

    def ps(self, name, shape):
        return self.ctx.enter_context(self.nc.psum_tensor(f"{self.stage}_{name}", shape, F32))

    def sem(self, name):
        return self.ctx.enter_context(self.nc.semaphore(f"{self.stage}_{name}"))


def project(nc, x, g_pre_mix, w_in, qkvT):
    with ExitStack() as ctx:
        r = Room(nc, ctx, "pj")
        ident = r.sb("ident", [P, P])
        gain = r.sb("gain", [P, D])
        xin = r.sb("xin", [P, 2, D])
        xn = r.sb("xn", [P, 2, D])
        ss = r.sb("ss", [P, RT])
        ms = r.sb("ms", [P, RT])
        rstd = r.sb("rstd", [P, RT])
        power = r.sb("power", [P, 1])
        eps = r.sb("eps", [P, 1])
        h_hi = r.sb("h_hi", [P, KT, S], F32R)
        h_lo = r.sb("h_lo", [P, KT, S], F32R)
        w_raw = r.sb("w_raw", [P, 2, KT, P])
        w_hi = r.sb("w_hi", [P, 2, KT, P], F32R)
        w_lo = r.sb("w_lo", [P, 2, KT, P], F32R)
        qscale = r.sb("qscale", [P, QKV_TILES + 1])
        proj_sb = r.sb("proj_sb", [P, 2, S])
        acc = r.ps("acc", [P, 2, S])
        x_loaded = [r.sem(f"x_loaded{s}") for s in range(2)]
        gain_loaded = r.sem("gain_loaded")
        const_ready = r.sem("const_ready")
        ss_ready = r.sem("ss_ready")
        rstd_step = r.sem("rstd_step")
        xn_ready = r.sem("xn_ready")
        xT_ready = r.sem("xT_ready")
        h_hi_ready = r.sem("h_hi_ready")
        h_ready = r.sem("h_ready")
        w_loaded = [r.sem(f"w_loaded{s}") for s in range(2)]
        w_hi_ready = r.sem("w_hi_ready")
        w_ready = r.sem("w_ready")
        proj_done = r.sem("proj_done")
        evacuated = r.sem("evacuated")
        stored = [r.sem(f"stored{s}") for s in range(2)]
        block = ctx.enter_context(nc.Block())
        w_v = w_in.rearrange("o (t p) c -> p (o t) c", p=P)
        half = QKV_TILES // 2
        gap = FOX_HEADS

        def column_tiles(eng, step):
            for lo, shift in ((0, 0), (half // 2, gap)):
                with eng.Fori(lo, lo + half // 2) as i:
                    for s in range(2):
                        step(i, s, 2 * i + s, i * (2 * P) + (s * P + shift))
            step(half, 0, QKV_TILES, LOGIT_COL)

        @block.sync
        def _(sp):
            sp.dma_start(gain[:, :], g_pre_mix[0:1, :].to_broadcast([P, D])).then_inc(gain_loaded, 16)
            for t in range(2):
                sp.dma_start(xin[:, t, :], x[0, t * P:(t + 1) * P, :]).then_inc(x_loaded[t], 16)
            with sp.Fori(0, RT // 2 - 1) as i:
                for s in range(2):
                    sp.wait_ge(xn_ready, 2 * i + s + 1)
                    sp.dma_start(xin[:, s, :], x[0, bass.ts(2 * i + (s + 2), P), :]).then_inc(x_loaded[s], 16)

            def load(i, s, ct, col):
                sp.wait_ge(w_ready, ct + 1)
                sp.dma_start(w_raw[:, s], w_v[:, :, bass.ds(col, P)]).then_inc(w_loaded[s], 16)
            column_tiles(sp, load)

        @block.gpsimd
        def _(pool):
            pool.memset(ident[:, :], 0.0).then_inc(const_ready, 1)
            pool.memset(power[:, :], -0.5).then_inc(const_ready, 1)
            pool.memset(eps[:, :], EPS).then_inc(const_ready, 1)
            pool.wait_ge(const_ready, 1)
            pool.affine_select(out=ident[:, :], in_=ident[:, :], compare_op=ALU.not_equal, fill=1.0,
                               base=0, pattern=[[-1, P]], channel_multiplier=1).then_inc(const_ready, 1)
            pool.memset(qscale[:, :], 1.0).then_inc(const_ready, 1)
            pool.wait_ge(const_ready, 5)
            for c in (0, half):
                pool.memset(qscale[:, c:c + 4], HD ** -0.5).then_inc(const_ready, 1)
            with pool.Fori(0, RT) as t:
                pool.wait_ge(ss_ready, t + 1)
                pool.tensor_tensor(ms[:, bass.ds(t, 1)], ss[:, bass.ds(t, 1)], eps[:, :], ALU.add)\
                    .then_inc(rstd_step, 1)
                pool.wait_ge(rstd_step, 2 * t + 1)
                pool.tensor_tensor(rstd[:, bass.ds(t, 1)], ms[:, bass.ds(t, 1)], power[:, :],
                                   ALU.pow).then_inc(rstd_step, 1)

        @block.scalar
        def _(act):
            act.sem_inc(evacuated, 2)
            for s in range(2):
                act.sem_inc(stored[s], 16)

            def square(i, s, t):
                act.wait_ge(x_loaded[s], 16 * (i + 1))
                act.activation(xn[:, s, :], xin[:, s, :], ACT.Square, scale=ROOT,
                               accum_out=ss[:, bass.ds(t, 1)]).then_inc(ss_ready, 1)

            def keep_hi(s, t):
                act.wait_ge(xT_ready, t + 1)
                act.activation(h_hi[:, :, bass.ts(t, P)], acc[:, s, 0:D].rearrange("p (k r) -> p k r", r=P),
                               ACT.Copy).then_inc(h_hi_ready, 1)

            for t in range(2):
                square(0, t, t)
            with act.Fori(0, RT // 2 - 1) as i:
                for s in range(2):
                    keep_hi(s, 2 * i + s)
                    square(i + 1, s, 2 * i + (s + 2))
            for s in range(2):
                keep_hi(s, RT - 2 + s)

            def evacuate(i, s, ct, col):
                act.wait_ge(proj_done, ct + 3)
                act.wait_ge(stored[s], 16 * (i + 1))
                act.activation(proj_sb[:, s, :], acc[:, s, :], ACT.Copy,
                               scale=qscale[:, bass.ds(ct, 1)]).then_inc(evacuated, 1)
                act.wait_ge(evacuated, ct + 3)
                act.dma_start(qkvT[bass.ds(ct, 1), :, :].rearrange("o p n -> (o p) n"),
                              proj_sb[:, s, :]).then_inc(stored[s], 16)
            act.wait_ge(const_ready, 7)
            column_tiles(act, evacuate)
            act.wait_ge(stored[0], 16 * (half + 2))
            act.wait_ge(stored[1], 16 * (half + 1))

        @block.vector
        def _(dve):
            dve.sem_inc(w_ready, 2)

            def normalise(s, t):
                dve.wait_ge(rstd_step, 2 * t + 2)
                dve.scalar_tensor_tensor(out=xn[:, s, :], in0=xin[:, s, :], scalar=rstd[:, bass.ds(t, 1)],
                                         in1=gain[:, :], op0=ALU.mult, op1=ALU.mult).then_inc(xn_ready, 1)

            def keep_lo(s, t):
                dve.wait_ge(h_hi_ready, t + 1)
                dve.tensor_tensor(h_lo[:, :, bass.ts(t, P)], acc[:, s, 0:D].rearrange("p (k r) -> p k r", r=P),
                                  f32(h_hi[:, :, bass.ts(t, P)]), ALU.subtract).then_inc(h_ready, 1)

            dve.wait_ge(gain_loaded, 16)
            for t in range(2):
                normalise(t, t)
            with dve.Fori(0, RT // 2 - 1) as i:
                for s in range(2):
                    keep_lo(s, 2 * i + s)
                    normalise(s, 2 * i + (s + 2))
            for s in range(2):
                keep_lo(s, RT - 2 + s)

            def split(i, s, ct, col):
                dve.wait_ge(w_loaded[s], 16 * (i + 1))
                dve.wait_ge(proj_done, ct + 1)
                dve.tensor_copy(w_hi[:, s], w_raw[:, s]).then_inc(w_hi_ready, 1)
                dve.wait_ge(w_hi_ready, ct + 1)
                dve.tensor_tensor(w_lo[:, s], w_raw[:, s], f32(w_hi[:, s]), ALU.subtract).then_inc(w_ready, 1)
            column_tiles(dve, split)

        @block.tensor
        def _(pe):
            pe.sem_inc(proj_done, 2)
            pe.wait_ge(const_ready, 4)

            def transpose(s, t):
                pe.wait_ge(xn_ready, t + 1)
                for k in range(KT):
                    last = pe.transpose(acc[:, s, k * P:(k + 1) * P], xn[:, s, k * P:(k + 1) * P], ident[:, :])
                last.then_inc(xT_ready, 1)
            for t in range(2):
                transpose(t, t)
            with pe.Fori(0, RT // 2 - 1) as i:
                for s in range(2):
                    pe.wait_ge(h_ready, 2 * i + s + 1)
                    transpose(s, 2 * i + (s + 2))
            pe.wait_ge(h_ready, RT)

            def multiply(i, s, ct, col):
                pe.wait_ge(w_ready, ct + 3)
                pe.wait_ge(evacuated, ct + 1)
                for b in range(S // 512):
                    rows = slice(b * 512, (b + 1) * 512)
                    for k in range(KT):
                        pe.matmul(acc[:, s, rows], w_hi[:, s, k], h_hi[:, k, rows], start=(k == 0), stop=False)
                        pe.matmul(acc[:, s, rows], w_hi[:, s, k], h_lo[:, k, rows], start=False, stop=False)
                        last = pe.matmul(acc[:, s, rows], w_lo[:, s, k], h_hi[:, k, rows],
                                         start=False, stop=(k == KT - 1))
                last.then_inc(proj_done, 1)
            column_tiles(pe, multiply)


def decay(nc, qkvT, b_forget, q_rows, k_rows):
    with ExitStack() as ctx:
        r = Room(nc, ctx, "dc")
        H = FOX_HEADS
        z = r.sb("z", [H, S])
        b = r.sb("b", [H, 1])
        az = r.sb("az", [H, S])
        e = r.sb("e", [H, S])
        w = r.sb("w", [H, S])
        lw = r.sb("lw", [H, S])
        t1 = r.sb("t1", [H, S])
        c = r.sb("c", [H, S])
        hi = r.sb("hi", [H, S], F32R)
        lo = r.sb("lo", [H, S], F32R)
        nhi = r.sb("nhi", [H, S], F32R)
        nlo = r.sb("nlo", [H, S], F32R)
        ones = r.sb("ones", [H, S], F32R)
        zero = r.sb("zero", [H, S], F32R)
        pos = r.sb("pos", [1, S])
        up = r.sb("up", [1, DIFF_HEADS, S], F32R)
        down = r.sb("down", [1, DIFF_HEADS, S], F32R)
        loaded = r.sem("loaded")
        pos_ready = r.sem("pos_ready")
        step = r.sem("step")
        e_ready = r.sem("e_ready")
        stored = r.sem("stored")
        DVE_STEPS = 2 + 2 * DIFF_HEADS + 11
        block = ctx.enter_context(nc.Block())

        @block.gpsimd
        def _(pool):
            pool.iota(pos[:, :], pattern=[[1, S]], base=0, channel_multiplier=0,
                      allow_small_or_imprecise_dtypes=True).then_inc(pos_ready, 1)
            pool.memset(f32(ones[:, :]), 1.0).then_inc(pos_ready, 1)
            pool.memset(f32(zero[:, :]), 0.0).then_inc(pos_ready, 1)

        @block.vector
        def _(dve):
            done = [0]

            def link(ins):
                done[0] += 1
                ins.then_inc(step, 1)
                dve.wait_ge(step, done[0])
            dve.wait_ge(loaded, 32)
            link(dve.tensor_scalar(z[:, :], z[:, :], b[:, :], None, ALU.add))
            link(dve.scalar_tensor_tensor(out=az[:, :], in0=z[:, :], scalar=-1.0, in1=z[:, :],
                                          op0=ALU.mult, op1=ALU.max))
            dve.wait_ge(pos_ready, 3)
            for h in range(DIFF_HEADS):
                slope = 2.0 ** (-8.0 * (h + 1) / DIFF_HEADS)
                dve.tensor_scalar(down[:, h, :], pos[:, :], -slope, None, ALU.mult).then_inc(step, 1)
                dve.tensor_scalar(up[:, h, :], pos[:, :], slope, None, ALU.mult).then_inc(step, 1)
                done[0] += 2
            dve.wait_ge(e_ready, 1)
            link(dve.tensor_scalar(w[:, :], e[:, :], 1.0, None, ALU.add))
            link(dve.scalar_tensor_tensor(out=t1[:, :], in0=w[:, :], scalar=-1.0, in1=e[:, :],
                                          op0=ALU.add, op1=ALU.subtract))
            link(dve.reciprocal(az[:, :], w[:, :]))
            link(dve.tensor_tensor(t1[:, :], t1[:, :], az[:, :], ALU.mult))
            dve.wait_ge(e_ready, 2)
            link(dve.tensor_tensor(t1[:, :], t1[:, :], lw[:, :], ALU.subtract))
            link(dve.scalar_tensor_tensor(out=t1[:, :], in0=z[:, :], scalar=0.0, in1=t1[:, :],
                                          op0=ALU.min, op1=ALU.add))
            link(dve.tensor_tensor_scan(c[:, :], t1[:, :], f32(zero[:, :]), 0.0, ALU.add, ALU.add))
            link(dve.tensor_copy(hi[:, :], c[:, :]))
            link(dve.tensor_tensor(lo[:, :], c[:, :], f32(hi[:, :]), ALU.subtract))
            link(dve.tensor_scalar(nhi[:, :], f32(hi[:, :]), -1.0, None, ALU.mult))
            link(dve.tensor_scalar(nlo[:, :], f32(lo[:, :]), -1.0, None, ALU.mult))
            assert done[0] == DVE_STEPS


        @block.scalar
        def _(act):
            act.preload_act_table_set("natural_log_exp_and_others")
            act.wait_ge(step, 2)
            act.activation(e[:, :], az[:, :], ACT.Exp, scale=-1.0).then_inc(e_ready, 1)
            act.wait_ge(step, 3 + 2 * DIFF_HEADS)
            act.activation(lw[:, :], w[:, :], ACT.Ln).then_inc(e_ready, 1)

        @block.sync
        def _(sp):
            sp.dma_start(z[:, :], qkvT[QKV_TILES, 0:H, :]).then_inc(loaded, 16)
            sp.dma_start(b[:, :], b_forget.rearrange("o h -> h o")).then_inc(loaded, 16)
            sp.wait_ge(pos_ready, 3)
            sp.wait_ge(step, 2 + 2 * DIFF_HEADS)
            n = 0
            D4 = DIFF_HEADS
            for rows, k, src in ((q_rows, 0, down[0:1, :, :]), (k_rows, 2, up[0:1, :, :])):
                sp.dma_start(rows[H:H + D4, k, :].rearrange("(o h) n -> o h n", o=1), f32(src)).then_inc(stored, 16)
                n += 1
            for rows, k, src in ((q_rows, 1, zero), (q_rows, 2, ones), (q_rows, 3, ones), (q_rows, 4, zero),
                                 (q_rows, 5, zero), (k_rows, 0, ones), (k_rows, 1, ones), (k_rows, 3, zero),
                                 (k_rows, 4, ones), (k_rows, 5, ones)):
                sp.dma_start(rows[H:H + D4, k, :], f32(src[0:D4, :])).then_inc(stored, 16)
                n += 1
            for rows, k, src in ((q_rows, 2, ones), (q_rows, 3, ones), (q_rows, 4, zero), (q_rows, 5, zero),
                                 (k_rows, 0, ones), (k_rows, 1, ones), (k_rows, 4, ones), (k_rows, 5, ones)):
                sp.dma_start(rows[0:H, k, :], f32(src[:, :])).then_inc(stored, 16)
                n += 1
            sp.wait_ge(step, DVE_STEPS)
            for rows, k, src in ((q_rows, 0, hi), (q_rows, 1, lo), (k_rows, 2, nhi), (k_rows, 3, nlo)):
                sp.dma_start(rows[0:H, k, :], f32(src[:, :])).then_inc(stored, 16)
                n += 1
            sp.wait_ge(stored, 16 * n)


FOX, DIFF = 0, 1
RAW = 80
COMBOS = (80, 40)
BLOCKS = (8, 4)
STAT = 80
STAT_RING = 3
STAGES = 5
PIECES = [(w, s, p) for s in range(2) for p in range(4) for w in "qk"]
PIECES = PIECES[:8] + [("v", 0, 0), ("v", 0, 1)] + PIECES[8:] + [("v", 0, 2), ("v", 0, 3)]
PRING, SRING = 4, 4
LAG = (3, 4)
TAIL = 12


def stat_chunks():
    return [(s, qt, ch) for s in range(2) for qt in range(RT) for ch in range(qt // 4 + 1)]


def stat_width(qt, ch):
    return min(512, P * (qt + 1) - 512 * ch)


def raw_chunks(kind):
    if kind == FOX:
        return [(s, J, j) for s in range(2) for J in range(4) for j in range(4 * J + 4)]
    return [(s, J, j) for J in range(4) for j in range(4 * J + 4) for s in range(2)]


def on_pool(kind, m):
    return m % 2 == 0 if kind == FOX else m % 4 != 3


def lo_count(kind, m, pool):
    return sum(on_pool(kind, n) == pool for n in range(m + 1))


LO_TOTAL = [[lo_count(k, COMBOS[k] - 1, p) for k in (FOX, DIFF)] for p in (False, True)]
STAT_STEPS = ("stat_top", "stat_corr", "stat_sum", "stat_ln", "stat_shift", "stat_flip", "stat_rows")


def plan(kind, with_stats=True):
    raws = RAW if kind is not None else 0
    size = (RAW if raws else 62) + TAIL
    early = [[] for _ in range(size)]
    late = [[] for _ in range(size)]
    if with_stats:
        late[0].append(("rows",))
        starts, span = ((4, 40), 30) if raws else ((1, 29), 26)
        prep_at = ((0, 2, 7, 14), (26, 30, 40, 47)) if raws else ((0, 1, 4, 10), (20, 24, 30, 36))
        v_at = (20, 23, 54, 58) if raws else (16, 18, 44, 48)
        for s in range(2):
            for p in range(4):
                late[prep_at[s][p]].append(("prep", s, p))
        for g in range(4):
            late[v_at[g]].append(("v_flip", g))
            late[v_at[g] + 1].append(("v_split", g))
        at, done = [], 0
        chunks = stat_chunks()
        total = sum(stat_width(qt, ch) for _, qt, ch in chunks) // 2
        for g, (s, qt, ch) in enumerate(chunks):
            if g % (STAT // 2) == 0:
                done = 0
            t = starts[s] + span * done // total
            if g >= STAT_RING:
                t = max(t, at[g - STAT_RING] + 2)
            at.append(t)
            done += stat_width(qt, ch)
            late[t].append(("stat_scores", g))
            late[t + 1].append(("stat_max", g))
            early[t + 2].append(("stat_exp", g))
        for s in range(2):
            t = at[STAT // 2 * (s + 1) - 1] + 3
            for n, what in enumerate(STAT_STEPS):
                late[t + n].append((what, s))
    split_at, pv_at = {}, {}
    for c in range(raws):
        if kind == FOX or c % 2:
            m = c if kind == FOX else c // 2
            split_at[c + 1] = m
            pv_at[c + LAG[kind]] = m
    steps, blocks = [], 0
    for t in range(size):
        if t < raws:
            steps.append(("scores", t))
        if t in pv_at:
            m = pv_at[t]
            steps.append(("pv", m))
            s, J, j = raw_chunks(kind)[m if kind == FOX else 2 * m]
            if j == 4 * J + 3:
                uses = (("o_first", 1),) if kind == FOX else (("o_first", 1), ("o_var", 2), ("o_pow", 3),
                                                               ("o_bcast", 5), ("o_norm", 6))
                for what, n in uses:
                    late[min(t + n, size - 1)].append((what, blocks))
                blocks += 1
        steps += early[t]
        if t < raws:
            steps.append(("exp", t))
        steps += [st for st in late[t] if st[0] == "stat_max"]
        if t in split_at:
            steps.append(("split", split_at[t]))
        steps += [st for st in late[t] if st[0] != "stat_max"]
    out, used = [], 0
    for st in steps:
        out.append(st)
        for _ in range({"prep": 2, "v_flip": 1}.get(st[0], 0)):
            assert PIECES[used][0] in ("qk" if st[0] == "prep" else "v")
            out.append(("load", used + STAGES))
            used += 1
    return out


def attend(nc, qkvT, q_rows, k_rows, lams, g_subln, mixT):
    with ExitStack() as ctx:
        r = Room(nc, ctx, "at")
        q1 = r.sb("q1", [P, 2, 2, S], F32R)
        k1 = r.sb("k1", [P, 2, 2, S], F32R)
        q2 = r.sb("q2", [P, 2, 2, S], F32R)
        k2 = r.sb("k2", [P, 2, 2, S], F32R)
        vals = r.sb("vals", [P, 2, RT, 256], F32R)
        stage = r.sb("stage", [P, STAGES, 512])
        probs = r.sb("probs", [P, PRING, 512])
        p_hi = r.sb("p_hi", [P, SRING, 512], F32R)
        p_lo = r.sb("p_lo", [P, SRING, 512], F32R)
        o_sb = r.sb("o_sb", [P, 2, 512])
        o_half = r.sb("o_half", [P, 512])
        ident_r = r.sb("ident_r", [P, P], F32R)
        ident = f32(ident_r[:, :])
        mask_q = r.sb("mask_q", [P, P], F32R)
        mask_k = r.sb("mask_k", [P, P], F32R)
        made = o_half[:, 0:3 * P].rearrange("p (a n) -> p a n", n=P)
        mean = r.sb("mean", [P, 1])
        power = r.sb("power", [P, 4])
        var = r.sb("var", [P, 4])
        rstd = r.sb("rstd", [P, 4])
        nmax = r.sb("nmax", [P, 2, 2, 4, RT])
        rsum = r.sb("rsum", [P, 2, 2, 4, RT])
        top = r.sb("top", [P, RT])
        corr = r.sb("corr", [P, 4, RT])
        total = r.sb("total", [P, RT])
        logsum = r.sb("logsum", [P, RT])
        shift = r.sb("shift", [P, 2 * RT], F32R)
        shiftT = r.sb("shiftT", [2 * RT, 2, P], F32R)
        lam_in = probs[:, 0, 0:4 * HD].rearrange("p (a d) -> p a d", d=HD)
        lam_s = r.sb("lam_s", [P, 4])
        nlam = r.sb("nlam", [P, 1])
        gsub = r.sb("gsub", [P, 1])
        ps_stat = r.ps("ps_stat", [P, STAT_RING, 512])
        ps_sc = r.ps("ps_sc", [P, 2, 512])
        ps_o = r.ps("ps_o", [P, 2, 512])
        ps_x = r.ps("ps_x", [P, 512])

        const_loaded = r.sem("const_loaded")
        const_pool = r.sem("const_pool")
        const_dve = r.sem("const_dve")
        const_act = r.sem("const_act")
        staged = [r.sem(f"staged{n}") for n in range(STAGES)]
        rows_loaded = r.sem("rows_loaded")
        shift_loaded = [r.sem(f"shift_loaded{s}") for s in range(2)]
        hi_ready = r.sem("hi_ready")
        lo_ready = r.sem("lo_ready")
        x_ready = r.sem("x_ready")
        x_free = r.sem("x_free")
        v_hi_ready = r.sem("v_hi_ready")
        stat_scored = r.sem("stat_scored")
        stat_maxed = r.sem("stat_maxed")
        stat_exped = r.sem("stat_exped")
        stat_dve = r.sem("stat_dve")
        stat_act = r.sem("stat_act")
        scored = r.sem("scored")
        exped = r.sem("exped")
        combined = r.sem("combined")
        p_hi_ready = r.sem("p_hi_ready")
        p_lo_dve = r.sem("p_lo_dve")
        p_lo_pool = r.sem("p_lo_pool")
        p_used = r.sem("p_used")
        o_half_ready = r.sem("o_half_ready")
        o_free = r.sem("o_free")
        o_squared = r.sem("o_squared")
        o_pow = r.sem("o_pow")
        o_stored = [r.sem(f"o_stored{s}") for s in range(2)]
        block = ctx.enter_context(nc.Block())

        plans = {None: plan(None), FOX: plan(FOX), DIFF: plan(DIFF)}
        last_plan = plan(DIFF, with_stats=False)
        stats, raws = stat_chunks(), [raw_chunks(FOX), raw_chunks(DIFF)]
        X_USES = ("v_flip", "stat_flip", "o_var", "o_bcast")
        X_OPEN, X_FOX, X_DIFF = (sum(st[0] in X_USES for st in plans[k]) for k in (None, FOX, DIFF))

        class Half:

            def __init__(self, kind, i, steps=None):
                self.kind, self.i = kind, i
                self.steps = plans[kind] if steps is None else steps
                self.xpos = {}
                for st in self.steps:
                    if st[0] in X_USES:
                        self.xpos[st] = len(self.xpos)
                if kind is None:
                    self.n, self.prep_kind, self.prep_i, self.slot = 0, FOX, 0, 0
                    self.x = self.raw = 0
                    return
                self.n = 2 * i + 1 + kind
                self.prep_kind = DIFF if kind == FOX else FOX
                self.prep_i = i if kind == FOX else i + 1
                self.slot = 1 - kind
                self.raw = 2 * RAW * i + RAW * kind
                self.combo = sum(COMBOS) * i + COMBOS[FOX] * kind
                self.block = sum(BLOCKS) * i + BLOCKS[FOX] * kind
                self.x = (X_FOX + X_DIFF) * i + X_OPEN + X_FOX * kind
                self.shift_value = 32 * (2 * i + kind) + 32

            def x_value(self, st):
                return self.x + (self.xpos[st] + 1)

            def lo_value(self, m, pool):
                both = sum(LO_TOTAL[pool])
                if m < 0:
                    m += COMBOS[1 - self.kind]
                    if self.kind == DIFF:
                        return self.i * both + (4 + lo_count(FOX, m, pool))
                    return self.i * both + (4 + LO_TOTAL[pool][FOX] + lo_count(DIFF, m, pool) - both)
                before = LO_TOTAL[pool][FOX] if self.kind == DIFF else 0
                return self.i * both + (4 + before + lo_count(self.kind, m, pool))

        def halves(eng, emit):
            emit(Half(None, 0))
            with eng.Fori(0, DIFF_HEADS - 1) as i:
                emit(Half(FOX, i))
                emit(Half(DIFF, i))
            emit(Half(FOX, DIFF_HEADS - 1))
            emit(Half(DIFF, DIFF_HEADS - 1, last_plan))

        def width(J, j):
            return max(0, j - 4 * J) * P

        def block_of(kind, m):
            return raws[kind][m if kind == FOX else 2 * m]

        def block_last(kind, b):
            ends = [m for m in range(COMBOS[kind]) if block_of(kind, m)[2] == 4 * block_of(kind, m)[1] + 3]
            return ends[b]

        def block_number(kind, m):
            s, J, _ = block_of(kind, m)
            return 4 * s + J if kind == FOX else J

        def staged_value(n, idx):
            return 128 * n + 32 * (idx // STAGES + 1)

        def piece_index(what, s, p):
            return PIECES.index((what, s, p))

        @block.sync
        def _(sp):
            def load(kind, i, idx):
                what, s, p = PIECES[idx]
                base = (0 if kind == FOX else 12) + {"q": 0, "k": 4, "v": 8}[what]
                for z in range(2):
                    rows = slice(z * 64, (z + 1) * 64) if what == "v" else slice(s * 64, (s + 1) * 64)
                    sp.dma_start(stage[z * 64:(z + 1) * 64, idx % STAGES, :],
                                 qkvT[bass.ds(i + base, 1), rows, p * 512:(p + 1) * 512]
                                 .rearrange("o p n -> (o p) n")).then_inc(staged[idx % STAGES], 16)

            for idx in range(STAGES):
                load(FOX, 0, idx)
            for n, v in enumerate(lams):
                sp.dma_start(lam_in[:, n, :], v[0:1, :].to_broadcast([P, HD])).then_inc(const_loaded, 16)
            sp.dma_start(gsub[:, :], g_subln.rearrange("o d -> d o")).then_inc(const_loaded, 16)

            def emit(h):
                for st in h.steps:
                    op = st[0]
                    if op == "rows":
                        if h.kind is not None:
                            sp.wait_ge(scored, h.raw + 1)
                        else:
                            sp.wait_ge(const_pool, 4)
                            sp.wait_ge(const_dve, 2)
                        for s in range(2):
                            at = 2 * h.prep_i + s if h.prep_kind == FOX else h.prep_i + FOX_HEADS
                            for dst, src in ((q2, q_rows), (k2, k_rows)):
                                sp.dma_start(f32(dst[0:6, h.slot, s, :]),
                                             src[bass.ds(at, 1), :, :].rearrange("o r n -> (o r) n"))\
                                  .then_inc(rows_loaded, 16)
                    elif op == "load":
                        idx = st[1]
                        if idx >= 20 and h.kind == FOX and isinstance(h.i, int):
                            continue
                        what, s, p = PIECES[idx - STAGES]
                        if what == "v":
                            sp.wait_ge(x_ready, h.x_value(("v_flip", p)))
                        else:
                            sp.wait_ge(lo_ready, 16 * h.n + (8 * s + 2 * p + (2 if what == "k" else 1)))
                        if idx < 20:
                            load(h.prep_kind, h.prep_i, idx)
                        elif h.kind is None:
                            load(DIFF, 0, idx - 20)
                        else:
                            load(h.kind, h.i + 1, idx - 20)
                    elif op == "stat_rows":
                        s = st[1]
                        sp.wait_ge(x_free, h.x_value(("stat_flip", s)))
                        for z in range(2):
                            sp.dma_start(f32(q2[4 + z:5 + z, h.slot, s, :].rearrange("o (t q) -> o t q", q=P)),
                                         f32(shiftT[z * RT:(z + 1) * RT, s, :])).then_inc(shift_loaded[s], 16)
                    elif op == "o_first" and h.kind == FOX:
                        b = st[1]
                        s, J, _ = block_of(FOX, block_last(FOX, b))
                        sp.wait_ge(o_free, h.block + b + 3)
                        sp.dma_start(mixT[bass.ds(h.i, 1), s * 64:(s + 1) * 64, J * 512:(J + 1) * 512]
                                     .rearrange("o p n -> (o p) n"), o_sb[0:64, b % 2, :])\
                          .then_inc(o_stored[b % 2], 16)
                    elif op == "o_norm":
                        b = st[1]
                        sp.wait_ge(x_free, h.x_value(("o_bcast", b)))
                        sp.dma_start(mixT[bass.ds(h.i + 4, 1), :, b * 512:(b + 1) * 512]
                                     .rearrange("o p n -> (o p) n"), o_sb[:, b % 2, :])\
                          .then_inc(o_stored[b % 2], 16)
            halves(sp, emit)
            for s in range(2):
                sp.wait_ge(o_stored[s], 16 * (1 + sum(BLOCKS) * DIFF_HEADS // 2))

        @block.gpsimd
        def _(pool):
            pool.sem_inc(p_lo_pool, 4)
            pool.sem_inc(o_pow, 1)
            pool.memset(made[:, :, :], 0.0).then_inc(const_pool, 1)
            pool.memset(nmax[:, :, :, :, :], -MASKED).then_inc(const_pool, 1)
            pool.memset(rsum[:, :, :, :, :], 0.0).then_inc(const_pool, 1)
            pool.memset(f32(q2[0:64, 0, :, :]), 0.0).then_inc(const_pool, 1)
            pool.memset(mean[:, :], 1.0 / P).then_inc(const_pool, 1)
            pool.memset(power[:, :], -0.5).then_inc(const_pool, 1)
            pool.wait_ge(const_pool, 6)
            for n, (compare, fill, step, mult) in enumerate(((ALU.not_equal, 1.0, -1, 1),
                                                             (ALU.is_ge, MASKED, -1, 1),
                                                             (ALU.is_ge, MASKED, 1, -1))):
                pool.affine_select(out=made[:, n, :], in_=made[:, n, :], compare_op=compare, fill=fill,
                                   base=0, pattern=[[step, P]], channel_multiplier=mult).then_inc(const_pool, 1)
            pool.wait_ge(const_pool, 9)

            def emit(h):
                full, narrow = h.kind is not None, None
                split_last = -1
                for st in h.steps:
                    op = st[0]
                    if op == "prep":
                        _, s, p = st
                        base = 24 * h.n + (12 * s + 3 * p)
                        cols = slice(p * 512, (p + 1) * 512)
                        if full:
                            pool.wait_ge(p_lo_pool, h.lo_value(split_last, True))
                            pool.wait_ge(o_pow, BLOCKS[DIFF] * h.i + 1)
                            full = False
                        pool.wait_ge(hi_ready, base + 2)
                        pool.tensor_tensor(q1[64:P, h.slot, s, cols], stage[64:P, piece_index("q", s, p) % STAGES, :],
                                           f32(q2[64:P, h.slot, s, cols]), ALU.subtract).then_inc(lo_ready, 1)
                        pool.wait_ge(hi_ready, base + 3)
                        pool.tensor_tensor(k2[64:P, h.slot, s, cols], stage[64:P, piece_index("k", s, p) % STAGES, :],
                                           f32(k1[64:P, h.slot, s, cols]), ALU.subtract).then_inc(lo_ready, 1)
                        narrow = 16 * h.n + (8 * s + 2 * p + 2)
                    elif (op == "split" and on_pool(h.kind, st[1])) or op == "o_pow":
                        if narrow is not None:
                            pool.wait_ge(lo_ready, narrow)
                            narrow = None
                        full = True
                        if op == "o_pow":
                            pool.wait_ge(x_free, h.x_value(("o_var", st[1])))
                            pool.tensor_tensor(rstd[:, :], var[:, :], power[:, :], ALU.pow).then_inc(o_pow, 1)
                            if h.steps is not last_plan:
                                pool.wait_ge(o_pow, BLOCKS[DIFF] * h.i + (st[1] + 2))
                            continue
                        m = split_last = st[1]
                        _, J, j = block_of(h.kind, m)
                        off = width(J, j)
                        c = m if h.kind == FOX else 2 * m
                        pool.wait_ge(p_hi_ready, h.combo + m + 1)
                        pool.tensor_tensor(p_lo[:, m % SRING, off:512], probs[:, c % PRING, off:512],
                                           f32(p_hi[:, m % SRING, off:512]), ALU.subtract).then_inc(p_lo_pool, 1)
            halves(pool, emit)

        @block.scalar
        def _(act):
            act.sem_inc(exped, 2)
            act.preload_act_table_set("natural_log_exp_and_others")
            act.wait_ge(const_dve, 8)
            act.activation(lam_s[:, 2:4], lam_s[:, 0:2], ACT.Exp).then_inc(const_act, 1)

            def emit(h):
                for st in h.steps:
                    op = st[0]
                    if op == "stat_exp":
                        g = st[1]
                        s, qt, ch = stats[g]
                        n = stat_width(qt, ch)
                        act.wait_ge(stat_maxed, STAT * h.n + g + 1)
                        act.activation(ps_stat[:, g % STAT_RING, 0:n], ps_stat[:, g % STAT_RING, 0:n], ACT.Exp,
                                       bias=nmax[:, h.slot, s, ch, qt:qt + 1],
                                       accum_out=rsum[:, h.slot, s, ch, qt:qt + 1]).then_inc(stat_exped, 1)
                    elif op == "stat_corr":
                        act.wait_ge(stat_dve, 7 * (2 * h.n + st[1]) + 2)
                        act.activation(corr[:, :, :], corr[:, :, :], ACT.Exp).then_inc(stat_act, 1)
                    elif op == "stat_ln":
                        act.wait_ge(stat_dve, 7 * (2 * h.n + st[1]) + 4)
                        act.activation(logsum[:, :], total[:, :], ACT.Ln).then_inc(stat_act, 1)
                    elif op == "v_split":
                        g = st[1]
                        act.wait_ge(x_ready, h.x_value(("v_flip", g)))
                        src = ps_x[:, :].rearrange("p (t v) -> p t v", v=P)
                        if h.prep_kind == FOX:
                            for s in range(2):
                                last = act.activation(vals[:, h.slot, 4 * g:4 * g + 4, s * P:s * P + 64],
                                                      src[:, :, s * 64:(s + 1) * 64], ACT.Copy)
                            last.then_inc(v_hi_ready, 1)
                        else:
                            act.activation(vals[:, h.slot, 4 * g:4 * g + 4, 0:P], src, ACT.Copy)\
                               .then_inc(v_hi_ready, 1)
                    elif op == "exp":
                        c = st[1]
                        _, J, j = raws[h.kind][c]
                        off = width(J, j)
                        act.wait_ge(scored, h.raw + c + 2)
                        if c >= PRING:
                            m = c - PRING if h.kind == FOX else (c - PRING) // 2
                            pool = on_pool(h.kind, m)
                        else:
                            m = -((PRING - c + 1) // 2) if h.kind == FOX else c - PRING
                            pool = on_pool(1 - h.kind, m + COMBOS[1 - h.kind])
                        act.wait_ge(p_lo_pool if pool else p_lo_dve, h.lo_value(m, pool))
                        act.activation(probs[:, c % PRING, off:512], ps_sc[:, c % 2, off:512], ACT.Exp)\
                           .then_inc(exped, 1)
                    elif op == "o_first" and h.kind == FOX:
                        b = st[1]
                        act.wait_ge(p_used, h.combo + block_last(FOX, b) + 1 + SRING)
                        act.wait_ge(o_free, h.block + b + 2)
                        if b == 0:
                            act.wait_ge(x_ready, h.x)
                        act.activation(o_half[0:64, :], ps_o[64:P, b % 2, :], ACT.Copy).then_inc(o_half_ready, 1)
                    elif op == "o_first":
                        b = st[1]
                        act.wait_ge(o_free, h.block + b + 3)
                        if b:
                            act.wait_ge(x_ready, h.x_value(("o_var", b - 1)))
                        act.activation(o_half[:, :], o_sb[:, b % 2, :], ACT.Square).then_inc(o_squared, 1)
            halves(act, emit)

        @block.vector
        def _(dve):
            dve.sem_inc(p_lo_dve, 4)
            dve.sem_inc(o_free, 2)
            for s in range(2):
                dve.sem_inc(o_stored[s], 16)
            dve.memset(f32(k2[0:64, 0, :, :]), 0.0).then_inc(const_dve, 1)
            dve.memset(f32(q2[0:64, 1, :, :]), 0.0).then_inc(const_dve, 1)
            dve.memset(f32(k2[0:64, 1, :, :]), 0.0).then_inc(const_dve, 1)
            dve.wait_ge(const_pool, 9)
            for n, t in enumerate((ident_r, mask_q, mask_k)):
                dve.tensor_copy(t[:, :], made[:, n, :]).then_inc(const_dve, 1)
            dve.wait_ge(const_loaded, 80)
            lam_v = lam_in[:, :, :].rearrange("p (a b) d -> p a b d", b=2)
            dve.tensor_tensor(lam_v[:, :, 0, :], lam_v[:, :, 0, :], lam_v[:, :, 1, :], ALU.mult)\
               .then_inc(const_dve, 1)
            dve.wait_ge(const_dve, 7)
            dve.tensor_reduce(lam_s[:, 0:2], lam_v[:, :, 0, :], AX.X, ALU.add).then_inc(const_dve, 1)
            dve.wait_ge(const_act, 1)
            dve.tensor_tensor(nlam[:, :], lam_s[:, 3:4], lam_s[:, 2:3], ALU.subtract).then_inc(const_dve, 1)
            dve.wait_ge(const_dve, 9)
            dve.tensor_scalar(nlam[:, :], nlam[:, :], LAM_INIT, None, ALU.subtract).then_inc(const_dve, 1)
            dve.tensor_scalar(gsub[:, :], gsub[:, :], 1.0 - LAM_INIT, None, ALU.mult).then_inc(const_dve, 1)
            dve.wait_ge(const_dve, 11)

            def emit(h):
                for st in h.steps:
                    op = st[0]
                    if op == "prep":
                        _, s, p = st
                        base = 24 * h.n + (12 * s + 3 * p)
                        cols = slice(p * 512, (p + 1) * 512)
                        q_at, k_at = piece_index("q", s, p), piece_index("k", s, p)
                        if h.kind is not None and (s, p) == (0, 0):
                            dve.wait_ge(scored, h.raw + 1)
                        dve.wait_ge(staged[q_at % STAGES], staged_value(h.n, q_at))
                        dve.tensor_copy(q1[:, h.slot, s, cols], stage[:, q_at % STAGES, :]).then_inc(hi_ready, 1)
                        dve.wait_ge(hi_ready, base + 1)
                        dve.tensor_copy(q2[64:P, h.slot, s, cols], f32(q1[64:P, h.slot, s, cols]))\
                           .then_inc(hi_ready, 1)
                        dve.wait_ge(staged[k_at % STAGES], staged_value(h.n, k_at))
                        dve.tensor_copy(k1[:, h.slot, s, cols], stage[:, k_at % STAGES, :]).then_inc(hi_ready, 1)
                    elif op == "stat_max":
                        g = st[1]
                        s, qt, ch = stats[g]
                        dve.wait_ge(stat_scored, STAT * h.n + g + 1)
                        dve.tensor_reduce(nmax[:, h.slot, s, ch, qt:qt + 1],
                                          ps_stat[:, g % STAT_RING, 0:stat_width(qt, ch)], AX.X,
                                          ALU.max, negate=True).then_inc(stat_maxed, 1)
                    elif op in STAT_STEPS:
                        s = st[1]
                        base = 7 * (2 * h.n + s)
                        act_base = 2 * (2 * h.n + s)
                        nm, rs = nmax[:, h.slot, s], rsum[:, h.slot, s]
                        if op == "stat_top":
                            dve.wait_ge(stat_exped, STAT * h.n + STAT // 2 * (s + 1))
                            dve.tensor_reduce(top[:, :], nm.rearrange("p c t -> p t c"), AX.X, ALU.min)\
                               .then_inc(stat_dve, 1)
                            dve.wait_ge(stat_dve, base + 1)
                            dve.tensor_tensor(corr[:, :, :], top[:, :].unsqueeze(1).to_broadcast([P, 4, RT]), nm,
                                              ALU.subtract).then_inc(stat_dve, 1)
                        elif op == "stat_sum":
                            dve.wait_ge(stat_act, act_base + 1)
                            dve.tensor_tensor(corr[:, :, :], corr[:, :, :], rs, ALU.mult).then_inc(stat_dve, 1)
                            dve.wait_ge(stat_dve, base + 3)
                            dve.tensor_reduce(total[:, :], corr[:, :, :].rearrange("p c t -> p t c"), AX.X, ALU.add)\
                               .then_inc(stat_dve, 1)
                        elif op == "stat_shift":
                            dve.wait_ge(stat_act, act_base + 2)
                            dve.tensor_tensor(total[:, :], top[:, :], logsum[:, :], ALU.subtract)\
                               .then_inc(stat_dve, 1)
                            dve.wait_ge(stat_dve, base + 5)
                            dve.tensor_copy(shift[:, 0:RT], total[:, :]).then_inc(stat_dve, 1)
                            dve.wait_ge(stat_dve, base + 6)
                            dve.tensor_tensor(shift[:, RT:2 * RT], total[:, :], f32(shift[:, 0:RT]),
                                              ALU.subtract).then_inc(stat_dve, 1)
                        elif op == "stat_flip":
                            dve.wait_ge(x_ready, h.x_value(st))
                            if h.kind is not None:
                                dve.wait_ge(shift_loaded[s], 32 * h.n)
                            dve.tensor_copy(shiftT[:, s, :], ps_x[0:2 * RT, 0:P]).then_inc(x_free, 1)
                    elif op == "v_split":
                        g = st[1]
                        dve.wait_ge(v_hi_ready, 4 * h.n + g + 1)
                        src = ps_x[:, :].rearrange("p (t v) -> p t v", v=P)
                        t4 = slice(4 * g, 4 * g + 4)
                        if h.prep_kind == FOX:
                            for s in range(2):
                                last = dve.tensor_tensor(vals[:, h.slot, t4, s * P + 64:(s + 1) * P],
                                                         src[:, :, s * 64:(s + 1) * 64],
                                                         f32(vals[:, h.slot, t4, s * P:s * P + 64]), ALU.subtract)
                        else:
                            last = dve.tensor_tensor(vals[:, h.slot, t4, P:2 * P], src,
                                                     f32(vals[:, h.slot, t4, 0:P]), ALU.subtract)
                        last.then_inc(x_free, 1)
                    elif op == "split":
                        m = st[1]
                        _, J, j = block_of(h.kind, m)
                        off = width(J, j)
                        c = m if h.kind == FOX else 2 * m
                        if h.kind == FOX:
                            dve.wait_ge(exped, h.raw + c + 3)
                        else:
                            dve.wait_ge(exped, h.raw + c + 4)
                            dve.scalar_tensor_tensor(out=probs[:, c % PRING, off:512],
                                                     in0=probs[:, (c + 1) % PRING, off:512], scalar=nlam[:, :],
                                                     in1=probs[:, c % PRING, off:512],
                                                     op0=ALU.mult, op1=ALU.add).then_inc(combined, 1)
                            dve.wait_ge(combined, COMBOS[DIFF] * h.i + m + 1)
                        dve.wait_ge(p_used, h.combo + m + 1)
                        dve.tensor_copy(p_hi[:, m % SRING, off:512], probs[:, c % PRING, off:512])\
                           .then_inc(p_hi_ready, 1)
                        if not on_pool(h.kind, m):
                            dve.wait_ge(p_hi_ready, h.combo + m + 1)
                            dve.tensor_tensor(p_lo[:, m % SRING, off:512], probs[:, c % PRING, off:512],
                                              f32(p_hi[:, m % SRING, off:512]), ALU.subtract).then_inc(p_lo_dve, 1)
                    elif op == "o_first":
                        b = st[1]
                        dve.wait_ge(o_stored[b % 2], 8 * sum(BLOCKS) * h.i
                                    + (16 * (b // 2 + 1) + 8 * BLOCKS[FOX] * h.kind))
                        if h.kind == FOX:
                            dve.wait_ge(o_half_ready, BLOCKS[FOX] * h.i + b + 1)
                            dve.tensor_tensor(o_sb[0:64, b % 2, :], ps_o[0:64, b % 2, :], o_half[0:64, :], ALU.add)\
                               .then_inc(o_free, 1)
                        else:
                            dve.wait_ge(p_used, h.combo + block_last(DIFF, b) + 1 + SRING)
                            dve.tensor_copy(o_sb[:, b % 2, :], ps_o[:, b % 2, :]).then_inc(o_free, 1)
                    elif op == "o_var":
                        dve.wait_ge(x_ready, h.x_value(st))
                        dve.tensor_scalar(var[:, :], ps_x[:, 0:4], EPS, None, ALU.add).then_inc(x_free, 1)
                    elif op == "o_norm":
                        b = st[1]
                        dve.wait_ge(x_ready, h.x_value(("o_bcast", b)))
                        dve.scalar_tensor_tensor(out=o_sb[:, b % 2, :], in0=o_sb[:, b % 2, :], scalar=gsub[:, :],
                                                 in1=ps_x[:, :], op0=ALU.mult, op1=ALU.mult)\
                           .then_inc(x_free, 1)
            halves(dve, emit)

        @block.tensor
        def _(pe):
            pe.sem_inc(scored, 1)
            pe.sem_inc(p_used, SRING)
            pe.wait_ge(const_dve, 6)

            def claim_x(h, st):
                if h.kind is not None or h.xpos[st]:
                    pe.wait_ge(x_free, h.x + h.xpos[st])

            def emit(h):
                for st in h.steps:
                    op = st[0]
                    if op == "stat_scores":
                        g = st[1]
                        s, qt, ch = stats[g]
                        if qt % 4 == 0 and ch == 0:
                            pe.wait_ge(lo_ready, 16 * h.n + (8 * s + 2 * (qt // 4) + 2))
                        if g == 0:
                            pe.wait_ge(rows_loaded, 64 * (h.n + 1))
                        if h.kind is not None or g >= STAT_RING:
                            pe.wait_ge(stat_exped, STAT * h.n + g + 1 - STAT_RING)
                        n = stat_width(qt, ch)
                        q = slice(qt * P, (qt + 1) * P)
                        keys = slice(512 * ch, 512 * ch + n)
                        out = ps_stat[:, g % STAT_RING, 0:n]
                        pe.matmul(out, q2[:, h.slot, s, q], k2[:, h.slot, s, keys], start=True, stop=False)
                        if ch == qt // 4:
                            pe.matmul(ps_stat[:, g % STAT_RING, n - P:n], ident_r[:, :], mask_q[:, :],
                                      start=False, stop=False)
                        pe.matmul(out, q1[:, h.slot, s, q], k1[:, h.slot, s, keys], start=False, stop=True)\
                          .then_inc(stat_scored, 1)
                    elif op == "stat_flip":
                        s = st[1]
                        pe.wait_ge(stat_dve, 7 * (2 * h.n + s) + 7)
                        claim_x(h, st)
                        pe.transpose(ps_x[0:2 * RT, 0:P], f32(shift[:, :]), ident).then_inc(x_ready, 1)
                    elif op == "v_flip":
                        g = st[1]
                        idx = piece_index("v", 0, g)
                        pe.wait_ge(staged[idx % STAGES], staged_value(h.n, idx))
                        claim_x(h, st)
                        for t in range(4):
                            last = pe.transpose(ps_x[:, t * P:(t + 1) * P],
                                                stage[:, idx % STAGES, t * P:(t + 1) * P], ident)
                        last.then_inc(x_ready, 1)
                    elif op == "scores":
                        c = st[1]
                        s, J, j = raws[h.kind][c]
                        slot = h.kind
                        off = width(J, j)
                        if c == 0 or (c == 1 and h.kind == DIFF) or (h.kind == FOX and c == RAW // 2):
                            pe.wait_ge(shift_loaded[s], h.shift_value)
                        pe.wait_ge(exped, h.raw + c + 1)
                        out = ps_sc[:, c % 2, off:512]
                        keys = slice(j * P, (j + 1) * P)
                        qs = slice(J * 512 + off, (J + 1) * 512)
                        pe.matmul(out, k2[:, slot, s, keys], q2[:, slot, s, qs], start=True, stop=False)
                        if j >= 4 * J:
                            pe.matmul(ps_sc[:, c % 2, off:off + P], ident_r[:, :], mask_k[:, :],
                                      start=False, stop=False)
                        pe.matmul(out, k1[:, slot, s, keys], q1[:, slot, s, qs], start=False, stop=True)\
                          .then_inc(scored, 1)
                    elif op == "pv":
                        m = st[1]
                        s, J, j = block_of(h.kind, m)
                        off = width(J, j)
                        slot, ring = h.kind, m % SRING
                        pool = on_pool(h.kind, m)
                        b = block_number(h.kind, m)
                        pe.wait_ge(p_lo_pool if pool else p_lo_dve, h.lo_value(m, pool))
                        if j == 0:
                            pe.wait_ge(o_free, h.block + b + 1)
                        out = ps_o[:, b % 2, off:512]
                        end = j == 4 * J + 3
                        if h.kind == FOX:
                            v = vals[:, slot, j, s * P:(s + 1) * P]
                            pe.matmul(out, v, p_hi[:, ring, off:512], start=(j == 0), stop=False)
                            pe.matmul(out, v, p_lo[:, ring, off:512], start=False, stop=end).then_inc(p_used, 1)
                        else:
                            v_hi, v_lo = vals[:, slot, j, 0:P], vals[:, slot, j, P:2 * P]
                            pe.matmul(out, v_hi, p_hi[:, ring, off:512], start=(j == 0), stop=False)
                            pe.matmul(out, v_lo, p_hi[:, ring, off:512], start=False, stop=False)
                            pe.matmul(out, v_hi, p_lo[:, ring, off:512], start=False, stop=end)\
                              .then_inc(p_used, 1)
                    elif op == "o_var":
                        b = st[1]
                        pe.wait_ge(o_squared, BLOCKS[DIFF] * h.i + b + 1)
                        claim_x(h, st)
                        for t in range(4):
                            last = pe.matmul(ps_x[:, t:t + 1], o_half[:, t * P:(t + 1) * P], mean[:, :],
                                             start=True, stop=True)
                        last.then_inc(x_ready, 1)
                    elif op == "o_bcast":
                        b = st[1]
                        pe.wait_ge(o_pow, BLOCKS[DIFF] * h.i + b + 2)
                        claim_x(h, st)
                        for t in range(4):
                            last = pe.matmul(ps_x[:, t * P:(t + 1) * P], rstd[:, t:t + 1].to_broadcast([P, P]), ident,
                                             start=True, stop=True)
                        last.then_inc(x_ready, 1)
            halves(pe, emit)


def mix_out(nc, mixT, w_out, x, g_post_mix, g_pre_mlp, x2, h2T):
    with ExitStack() as ctx:
        r = Room(nc, ctx, "mo")
        w_raw = r.sb("w_raw", [P, 2, D])
        w_hi = r.sb("w_hi", [P, KT, D], F32R)
        w_lo = r.sb("w_lo", [P, KT, D], F32R)
        m_raw = r.sb("m_raw", [P, 2, KT, P])
        m_hi = r.sb("m_hi", [P, 2, KT, P], F32R)
        m_lo = r.sb("m_lo", [P, 2, KT, P], F32R)
        xin = r.sb("xin", [P, 2, D])
        y = r.sb("y", [P, 2, D])
        xn = r.sb("xn", [P, 2, D])
        h_hi = r.sb("h_hi", [P, 2, KT, P], F32R)
        h_lo = r.sb("h_lo", [P, 2, KT, P], F32R)
        g_post = r.sb("g_post", [P, D])
        g_pre = r.sb("g_pre", [P, D])
        ident = r.sb("ident", [P, P])
        power = r.sb("power", [P, 1])
        eps = r.sb("eps", [P, 1])
        ss = r.sb("ss", [P, 2, RT])
        rstd = r.sb("rstd", [P, 2, RT])
        acc = r.ps("acc", [P, 2, D])
        flip = r.ps("flip", [P, 2, D])
        const_ready = r.sem("const_ready")
        gains_loaded = r.sem("gains_loaded")
        w_loaded = [r.sem(f"w_loaded{s}") for s in range(2)]
        w_hi_ready = r.sem("w_hi_ready")
        w_ready = r.sem("w_ready")
        m_loaded = [r.sem(f"m_loaded{s}") for s in range(2)]
        x_loaded = [r.sem(f"x_loaded{s}") for s in range(2)]
        m_hi_ready = r.sem("m_hi_ready")
        m_ready = r.sem("m_ready")
        multiplied = r.sem("multiplied")
        ss_ready = r.sem("ss_ready")
        rstd_step = r.sem("rstd_step")
        y_step = r.sem("y_step")
        xn_ready = r.sem("xn_ready")
        flipped = r.sem("flipped")
        h_hi_ready = r.sem("h_hi_ready")
        h_ready = r.sem("h_ready")
        stored = [r.sem(f"stored{s}") for s in range(2)]
        block = ctx.enter_context(nc.Block())
        LAST = RT // 2

        @block.sync
        def _(sp):
            sp.dma_start(m_raw[:, 0], mixT[:, :, 0:P].rearrange("k p n -> p k n")).then_inc(m_loaded[0], 16)
            for s in range(2):
                sp.dma_start(w_raw[:, s, :], w_out[0, s * P:(s + 1) * P, :]).then_inc(w_loaded[s], 16)
            for k in range(2, KT):
                sp.wait_ge(w_ready, k - 1)
                sp.dma_start(w_raw[:, k % 2, :], w_out[0, k * P:(k + 1) * P, :]).then_inc(w_loaded[k % 2], 16)
            sp.dma_start(g_post[:, :], g_post_mix[0:1, :].to_broadcast([P, D])).then_inc(gains_loaded, 16)
            sp.dma_start(g_pre[:, :], g_pre_mlp[0:1, :].to_broadcast([P, D])).then_inc(gains_loaded, 16)
            sp.dma_start(xin[:, 0, :], x[0, 0:P, :]).then_inc(x_loaded[0], 16)
            sp.dma_start(m_raw[:, 1], mixT[:, :, P:2 * P].rearrange("k p n -> p k n")).then_inc(m_loaded[1], 16)
            sp.dma_start(xin[:, 1, :], x[0, P:2 * P, :]).then_inc(x_loaded[1], 16)
            with sp.Fori(0, LAST - 1) as i:
                for s in range(2):
                    t = 2 * i + s + 2
                    sp.wait_ge(m_ready, t + 1)
                    sp.dma_start(m_raw[:, s], mixT[:, :, bass.ts(t, P)].rearrange("k p n -> p k n"))\
                      .then_inc(m_loaded[s], 16)
                    sp.wait_ge(y_step, 2 * (t - 1))
                    sp.dma_start(xin[:, s, :], x[0, bass.ts(t, P), :]).then_inc(x_loaded[s], 16)

        @block.gpsimd
        def _(pool):
            pool.memset(ident[:, :], 0.0).then_inc(const_ready, 1)
            pool.memset(power[:, :], -0.5).then_inc(const_ready, 1)
            pool.memset(eps[:, :], EPS).then_inc(const_ready, 1)
            pool.wait_ge(const_ready, 1)
            pool.affine_select(out=ident[:, :], in_=ident[:, :], compare_op=ALU.not_equal, fill=1.0,
                               base=0, pattern=[[-1, P]], channel_multiplier=1).then_inc(const_ready, 1)
            pool.wait_ge(const_ready, 4)
            with pool.Fori(0, RT) as t:
                for n in range(2):
                    pool.wait_ge(ss_ready, 2 * t + n + 1)
                    pool.tensor_tensor(ss[:, n, bass.ds(t, 1)], ss[:, n, bass.ds(t, 1)], eps[:, :], ALU.add)\
                        .then_inc(rstd_step, 1)
                    pool.wait_ge(rstd_step, 4 * t + 2 * n + 1)
                    pool.tensor_tensor(rstd[:, n, bass.ds(t, 1)], ss[:, n, bass.ds(t, 1)], power[:, :],
                                       ALU.pow).then_inc(rstd_step, 1)

        @block.scalar
        def _(act):
            for s in range(2):
                act.sem_inc(stored[s], 48)

            def tile(i, s, t):
                act.wait_ge(multiplied, t + 3)
                act.wait_ge(xn_ready, t + 1)
                act.wait_ge(flipped, t + 1)
                act.activation(xn[:, s, :], acc[:, s, :], ACT.Square, scale=ROOT, accum_out=ss[:, 0, bass.ds(t, 1)])\
                   .then_inc(ss_ready, 1)
                act.wait_ge(y_step, 2 * t + 2)
                act.activation(xn[:, s, :], y[:, s, :], ACT.Square, scale=ROOT, accum_out=ss[:, 1, bass.ds(t, 1)])\
                   .then_inc(ss_ready, 1)
                act.dma_start(x2[bass.ts(t, P), :], y[:, s, :]).then_inc(stored[s], 16)

            def keep(i, s, t):
                act.wait_ge(flipped, t + 3)
                act.wait_ge(stored[s], 16 * (3 * i + 4))
                act.activation(h_hi[:, s], flip[:, s, :].rearrange("p (k r) -> p k r", r=P), ACT.Copy)\
                   .then_inc(h_hi_ready, 1)
                act.wait_ge(h_ready, t + 3)
                for n, src in enumerate((h_hi, h_lo)):
                    act.dma_start(h2T[n, :, :, bass.ts(t, P)].rearrange("k p n -> p k n"), f32(src[:, s]))\
                       .then_inc(stored[s], 16)
            act.sem_inc(flipped, 2)
            tile(0, 0, 0)
            with act.Fori(0, LAST - 1) as i:
                tile(i, 1, 2 * i + 1)
                keep(i, 0, 2 * i)
                tile(i + 1, 0, 2 * i + 2)
                keep(i, 1, 2 * i + 1)
            tile(LAST - 1, 1, RT - 1)
            keep(LAST - 1, 0, RT - 2)
            keep(LAST - 1, 1, RT - 1)
            for s in range(2):
                act.wait_ge(stored[s], 48 * (LAST + 1))

        @block.vector
        def _(dve):
            dve.sem_inc(m_ready, 2)
            dve.sem_inc(xn_ready, 2)
            dve.sem_inc(h_ready, 2)

            def split_mix(i, s, t):
                dve.wait_ge(m_loaded[s], 16 * (i + 1))
                dve.wait_ge(multiplied, t + 1)
                dve.tensor_copy(m_hi[:, s], m_raw[:, s]).then_inc(m_hi_ready, 1)
                dve.wait_ge(m_hi_ready, t + 1)
                dve.tensor_tensor(m_lo[:, s], m_raw[:, s], f32(m_hi[:, s]), ALU.subtract).then_inc(m_ready, 1)

            def norms(i, s, t):
                dve.wait_ge(rstd_step, 4 * t + 2)
                dve.wait_ge(stored[s], 48 * (i + 1))
                dve.scalar_tensor_tensor(out=y[:, s, :], in0=acc[:, s, :], scalar=rstd[:, 0, bass.ds(t, 1)],
                                         in1=g_post[:, :], op0=ALU.mult, op1=ALU.mult).then_inc(y_step, 1)
                dve.wait_ge(x_loaded[s], 16 * (i + 1))
                dve.wait_ge(y_step, 2 * t + 1)
                dve.tensor_tensor(y[:, s, :], y[:, s, :], xin[:, s, :], ALU.add).then_inc(y_step, 1)

            def pre_norm(i, s, t):
                dve.wait_ge(rstd_step, 4 * t + 4)
                dve.scalar_tensor_tensor(out=xn[:, s, :], in0=y[:, s, :], scalar=rstd[:, 1, bass.ds(t, 1)],
                                         in1=g_pre[:, :], op0=ALU.mult, op1=ALU.mult).then_inc(xn_ready, 1)

            def keep_lo(s, t):
                dve.wait_ge(h_hi_ready, t + 1)
                dve.tensor_tensor(h_lo[:, s], flip[:, s, :].rearrange("p (k r) -> p k r", r=P),
                                  f32(h_hi[:, s]), ALU.subtract).then_inc(h_ready, 1)

            split_mix(0, 0, 0)
            for k in range(KT):
                dve.wait_ge(w_loaded[k % 2], 16 * (k // 2 + 1))
                dve.tensor_copy(w_hi[:, k, :], w_raw[:, k % 2, :]).then_inc(w_hi_ready, 1)
                dve.wait_ge(w_hi_ready, k + 1)
                dve.tensor_tensor(w_lo[:, k, :], w_raw[:, k % 2, :], f32(w_hi[:, k, :]), ALU.subtract)\
                   .then_inc(w_ready, 1)
            dve.wait_ge(gains_loaded, 32)
            split_mix(0, 1, 1)
            norms(0, 0, 0)
            pre_norm(0, 0, 0)
            with dve.Fori(0, LAST - 1) as i:
                split_mix(i + 1, 0, 2 * i + 2)
                norms(i, 1, 2 * i + 1)
                keep_lo(0, 2 * i)
                pre_norm(i, 1, 2 * i + 1)
                split_mix(i + 1, 1, 2 * i + 3)
                norms(i + 1, 0, 2 * i + 2)
                keep_lo(1, 2 * i + 1)
                pre_norm(i + 1, 0, 2 * i + 2)
            norms(LAST - 1, 1, RT - 1)
            keep_lo(0, RT - 2)
            pre_norm(LAST - 1, 1, RT - 1)
            keep_lo(1, RT - 1)

        @block.tensor
        def _(pe):
            pe.sem_inc(multiplied, 2)

            def multiply(i, s, t):
                pe.wait_ge(m_ready, t + 3)
                if not isinstance(t, int) or t > 1:
                    pe.wait_ge(y_step, 2 * t - 3)
                for b in range(D // 512):
                    cols = slice(b * 512, (b + 1) * 512)
                    for k in range(KT):
                        if isinstance(t, int) and t == 0 and b == 0:
                            pe.wait_ge(w_ready, k + 1)
                        pe.matmul(acc[:, s, cols], m_hi[:, s, k], w_hi[:, k, cols], start=(k == 0), stop=False)
                        pe.matmul(acc[:, s, cols], m_hi[:, s, k], w_lo[:, k, cols], start=False, stop=False)
                        last = pe.matmul(acc[:, s, cols], m_lo[:, s, k], w_hi[:, k, cols],
                                         start=False, stop=(k == KT - 1))
                last.then_inc(multiplied, 1)

            def transpose(s, t):
                pe.wait_ge(xn_ready, t + 3)
                pe.wait_ge(h_ready, t + 1)
                for k in range(KT):
                    last = pe.transpose(flip[:, s, k * P:(k + 1) * P], xn[:, s, k * P:(k + 1) * P], ident[:, :])
                last.then_inc(flipped, 1)
            pe.wait_ge(const_ready, 4)
            multiply(0, 0, 0)
            multiply(0, 1, 1)
            transpose(0, 0)
            with pe.Fori(0, LAST - 1) as i:
                multiply(i, 0, 2 * i + 2)
                transpose(1, 2 * i + 1)
                multiply(i, 1, 2 * i + 3)
                transpose(0, 2 * i + 2)
            transpose(1, RT - 1)


def mlp(nc, h2T, w_up, w_down, x2, g_post_mlp, out):
    SW = S // 2
    ST = SW // P
    FC = 256
    FT = FC // P
    NC = DFF // FC
    RB = SW // 512
    UB = FT * RB
    YB = ST * D // 512
    with ExitStack() as ctx:
        r = Room(nc, ctx, "ml")
        h_hi = r.sb("h_hi", [P, KT, SW], F32R)
        h_lo = r.sb("h_lo", [P, KT, SW], F32R)
        y = r.sb("y", [P, ST, D])
        u_hi = r.sb("u_hi", [P, 2, FT, SW], F32R)
        u_lo = r.sb("u_lo", [P, 2, FT, SW], F32R)
        up_raw = r.sb("up_raw", [P, KT, FC])
        up_hi = r.sb("up_hi", [P, KT, FC], F32R)
        up_lo = r.sb("up_lo", [P, KT, FC], F32R)
        dn_raw = r.sb("dn_raw", [P, FT, D])
        dn_hi = r.sb("dn_hi", [P, FT, D], F32R)
        dn_lo = r.sb("dn_lo", [P, FT, D], F32R)
        relu = r.sb("relu", [P, 2, 512])
        gain = r.sb("gain", [P, D])
        xres = r.sb("xres", [P, 2, D])
        junk = r.sb("junk", [P, D])
        power = r.sb("power", [P, 1])
        ss = r.sb("ss", [P, 2 * ST])
        rstd = r.sb("rstd", [P, 2 * ST])
        ps_u = r.ps("ps_u", [P, 4, 512])
        ps_y = r.ps("ps_y", [P, 4, 512])
        const_ready = r.sem("const_ready")
        gain_loaded = r.sem("gain_loaded")
        h_loaded = r.sem("h_loaded")
        up_loaded = r.sem("up_loaded")
        dn_loaded = r.sem("dn_loaded")
        up_split = r.sem("up_split")
        dn_split = r.sem("dn_split")
        up_done = r.sem("up_done")
        dn_done = r.sem("dn_done")
        relued = r.sem("relued")
        u_step = r.sem("u_step")
        y_added = r.sem("y_added")
        y_cleared = r.sem("y_cleared")
        ss_ready = r.sem("ss_ready")
        rstd_step = r.sem("rstd_step")
        x_loaded = [r.sem(f"x_loaded{s}") for s in range(2)]
        y_final = r.sem("y_final")
        stored = r.sem("stored")
        block = ctx.enter_context(nc.Block())
        up_v = w_up.rearrange("o (k p) f -> p (o k) f", p=P)
        dn_v = w_down.rearrange("o (k p) d -> p (o k) d", p=P)

        def sweeps(eng, up, down, tail=None):
            up(0, 0, 0)
            for w in range(2):
                with eng.Fori(0, NC // 2 - 1) as i:
                    up(w, 2 * i + 1, 1)
                    down(w, 2 * i, 0)
                    up(w, 2 * i + 2, 0)
                    down(w, 2 * i + 1, 1)
                up(w, NC - 1, 1)
                down(w, NC - 2, 0)
                down(w, NC - 1, 1)
                if w == 0:
                    up(1, 0, 0)
                if tail:
                    tail(w)

        def first(c):
            return isinstance(c, int) and c == 0

        @block.sync
        def _(sp):
            sp.dma_start(gain[:, :], g_post_mlp[0:1, :].to_broadcast([P, D])).then_inc(gain_loaded, 16)

            def load_up(n, c):
                sp.wait_ge(up_split, 2 * n + 2)
                sp.dma_start(up_raw[:, :, :], up_v[:, :, bass.ds(c * FC, FC)]).then_inc(up_loaded, 16)

            def up(w, c, s):
                n = w * NC + c
                if not isinstance(c, int) or c < NC - 1:
                    load_up(n + 1, c + 1)
                elif w == 0:
                    load_up(n + 1, 0)
                if first(c):
                    if w:
                        sp.wait_ge(up_done, UB + UB * NC * w)
                    for k in range(KT):
                        for z, dst in enumerate((h_hi, h_lo)):
                            sp.dma_start(f32(dst[:, k, :]), h2T[z, k, :, w * SW:(w + 1) * SW])\
                              .then_inc(h_loaded, 16)

            def down(w, c, s):
                n = w * NC + c
                sp.wait_ge(dn_split, 2 * n + 2)
                sp.dma_start(dn_raw[:, :, :], dn_v[:, bass.ds(c * FT, FT), :]).then_inc(dn_loaded, 16)

            def tail(w):
                def load(n):
                    if n > 1:
                        sp.wait_ge(y_final, 2 * n - 2)
                    sp.dma_start(xres[:, n % 2, :], x2[n * P:(n + 1) * P, :]).then_inc(x_loaded[n % 2], 16)
                load(w * ST)
                for t in range(ST):
                    n = w * ST + t
                    if t < ST - 1:
                        load(n + 1)
                    sp.wait_ge(y_final, 2 * n + 2)
                    sp.dma_start(out[0, n * P:(n + 1) * P, :], y[:, t, :]).then_inc(stored, 16)
            load_up(0, 0)
            sweeps(sp, up, down, tail)
            sp.wait_ge(stored, 16 * 2 * ST)

        @block.gpsimd
        def _(pool):
            pool.memset(power[:, :], -0.5).then_inc(const_ready, 1)
            pool.wait_ge(const_ready, 1)
            for w in range(2):
                if w:
                    pool.wait_ge(stored, 16 * ST)
                pool.memset(y[:, :, :], 0.0).then_inc(y_cleared, 1)
                for t in range(ST):
                    n = w * ST + t
                    pool.wait_ge(ss_ready, n + 1)
                    pool.tensor_scalar(ss[:, n:n + 1], ss[:, n:n + 1], EPS, None, ALU.add)\
                        .then_inc(rstd_step, 1)
                    pool.wait_ge(rstd_step, 2 * n + 1)
                    pool.tensor_tensor(rstd[:, n:n + 1], ss[:, n:n + 1], power[:, :], ALU.pow)\
                        .then_inc(rstd_step, 1)

        @block.scalar
        def _(act):
            act.sem_inc(relued, 4)

            def up(w, c, s):
                n = w * NC + c
                for b in range(UB):
                    g = n * UB + b
                    act.wait_ge(up_done, g + 1 + UB)
                    act.wait_ge(u_step, 3 * g + 3)
                    act.activation(relu[:, b % 2, :], ps_u[:, b % 4, :], ACT.Relu).then_inc(relued, 1)

            def down(w, c, s):
                pass

            def tail(w):
                act.wait_ge(y_added, 4 + YB * NC * (w + 1))
                for t in range(ST):
                    n = w * ST + t
                    if n:
                        act.wait_ge(ss_ready, n)
                    act.activation(junk[:, :], y[:, t, :], ACT.Square, scale=ROOT, accum_out=ss[:, n:n + 1])\
                       .then_inc(ss_ready, 1)
            sweeps(act, up, down, tail)

        @block.vector
        def _(dve):
            dve.sem_inc(up_split, 2)
            dve.sem_inc(dn_split, 2)
            dve.sem_inc(u_step, 6)
            dve.sem_inc(y_added, 4)
            dve.wait_ge(gain_loaded, 16)

            def split(n, raw, hi, lo, loaded, sem):
                dve.wait_ge(loaded, 16 * (n + 1))
                dve.tensor_copy(hi[:, :, :], raw[:, :, :]).then_inc(sem, 1)
                dve.wait_ge(sem, 2 * n + 3)
                dve.tensor_tensor(lo[:, :, :], raw[:, :, :], f32(hi[:, :, :]), ALU.subtract).then_inc(sem, 1)

            def split_up(n):
                dve.wait_ge(up_done, UB * n + UB)
                split(n, up_raw, up_hi, up_lo, up_loaded, up_split)

            def split_down(n):
                dve.wait_ge(dn_done, YB * n + YB)
                split(n, dn_raw, dn_hi, dn_lo, dn_loaded, dn_split)

            def up(w, c, s):
                n = w * NC + c
                if not first(c):
                    split_down(n - 1)
                for b in range(UB):
                    g = n * UB + b
                    f, rb = b // RB, b % RB
                    rows = slice(rb * 512, (rb + 1) * 512)
                    dve.wait_ge(relued, g + 5)
                    if b == 0:
                        dve.wait_ge(dn_done, YB * n + 1)
                    dve.tensor_tensor(relu[:, b % 2, :], relu[:, b % 2, :], relu[:, b % 2, :], ALU.mult)\
                       .then_inc(u_step, 1)
                    dve.wait_ge(u_step, 3 * g + 7)
                    dve.tensor_copy(u_hi[:, s, f, rows], relu[:, b % 2, :]).then_inc(u_step, 1)
                    dve.wait_ge(u_step, 3 * g + 8)
                    dve.tensor_tensor(u_lo[:, s, f, rows], relu[:, b % 2, :], f32(u_hi[:, s, f, rows]),
                                      ALU.subtract).then_inc(u_step, 1)
                if first(c):
                    split_up(n + 1)

            def down(w, c, s):
                n = w * NC + c
                last_two = isinstance(c, int) and c - (NC - 2)
                if last_two == 1 and isinstance(c, int):
                    split_down(n)
                elif not isinstance(c, int) or w == 0:
                    split_up(n + 2)
                if not isinstance(c, int):
                    dve.wait_ge(y_cleared, w + 1)
                for b in range(YB):
                    g = n * YB + b
                    t, half = b // 2, b % 2
                    cols = slice(half * 512, (half + 1) * 512)
                    dve.wait_ge(dn_done, g + 1 + 2 * YB)
                    dve.wait_ge(y_added, g + 4)
                    dve.tensor_tensor(y[:, t, cols], y[:, t, cols], ps_y[:, b % 4, :], ALU.add)\
                       .then_inc(y_added, 1)

            def tail(w):
                for t in range(ST):
                    n = w * ST + t
                    dve.wait_ge(rstd_step, 2 * n + 2)
                    dve.scalar_tensor_tensor(out=y[:, t, :], in0=y[:, t, :], scalar=rstd[:, n:n + 1],
                                             in1=gain[:, :], op0=ALU.mult, op1=ALU.mult).then_inc(y_final, 1)
                    dve.wait_ge(x_loaded[n % 2], 16 * (n // 2 + 1))
                    dve.wait_ge(y_final, 2 * n + 1)
                    dve.tensor_tensor(y[:, t, :], y[:, t, :], xres[:, n % 2, :], ALU.add).then_inc(y_final, 1)
            split_up(0)
            sweeps(dve, up, down, tail)

        @block.tensor
        def _(pe):
            pe.sem_inc(up_done, UB)
            pe.sem_inc(dn_done, 2 * YB)

            def up(w, c, s):
                n = w * NC + c
                if isinstance(c, int) and c == 0:
                    pe.wait_ge(h_loaded, 16 * 2 * KT * (w + 1))
                pe.wait_ge(up_split, 2 * n + 4)
                for b in range(UB):
                    g = n * UB + b
                    f, rb = b // RB, b % RB
                    rows = slice(rb * 512, (rb + 1) * 512)
                    cols = slice(f * P, (f + 1) * P)
                    pe.wait_ge(relued, g + 1)
                    for k in range(KT):
                        pe.matmul(ps_u[:, b % 4, :], up_hi[:, k, cols], h_hi[:, k, rows],
                                  start=(k == 0), stop=False)
                        pe.matmul(ps_u[:, b % 4, :], up_hi[:, k, cols], h_lo[:, k, rows], start=False, stop=False)
                        last = pe.matmul(ps_u[:, b % 4, :], up_lo[:, k, cols], h_hi[:, k, rows],
                                         start=False, stop=(k == KT - 1))
                    last.then_inc(up_done, 1)

            def down(w, c, s):
                n = w * NC + c
                pe.wait_ge(dn_split, 2 * n + 4)
                pe.wait_ge(u_step, 6 + 3 * UB * (n + 1))
                for b in range(YB):
                    g = n * YB + b
                    t, half = b // 2, b % 2
                    cols = slice(half * 512, (half + 1) * 512)
                    rows = slice(t * P, (t + 1) * P)
                    pe.wait_ge(y_added, g + 1)
                    for f in range(FT):
                        pe.matmul(ps_y[:, b % 4, :], u_hi[:, s, f, rows], dn_hi[:, f, cols],
                                  start=(f == 0), stop=False)
                        pe.matmul(ps_y[:, b % 4, :], u_hi[:, s, f, rows], dn_lo[:, f, cols],
                                  start=False, stop=False)
                        last = pe.matmul(ps_y[:, b % 4, :], u_lo[:, s, f, rows], dn_hi[:, f, cols],
                                         start=False, stop=(f == FT - 1))
                    last.then_inc(dn_done, 1)
            sweeps(pe, up, down)


def hybrid_block(nc, x, g_pre_mix, w_in, b_forget, lambda_q1, lambda_k1, lambda_q2, lambda_k2,
                 g_subln, w_out, g_post_mix, g_pre_mlp, w_up, w_down, g_post_mlp, out):
    qkvT = nc.dram_tensor("qkvT", [QKV_TILES + 1, P, S], F32).ap()
    q_rows = nc.dram_tensor("q_rows", [FOX_HEADS + DIFF_HEADS, 6, S], F32).ap()
    k_rows = nc.dram_tensor("k_rows", [FOX_HEADS + DIFF_HEADS, 6, S], F32).ap()
    mixT = nc.dram_tensor("mixT", [KT, P, S], F32).ap()
    x2 = nc.dram_tensor("x2", [S, D], F32).ap()
    h2T = nc.dram_tensor("h2T", [2, KT, P, S], F32).ap()
    project(nc, x, g_pre_mix, w_in, qkvT)
    decay(nc, qkvT, b_forget, q_rows, k_rows)
    attend(nc, qkvT, q_rows, k_rows, (lambda_q1, lambda_k1, lambda_q2, lambda_k2), g_subln, mixT)
    mix_out(nc, mixT, w_out, x, g_post_mix, g_pre_mlp, x2, h2T)
    mlp(nc, h2T, w_up, w_down, x2, g_post_mlp, out)


_INS = ["x", "g_pre_mix", "w_in", "b_forget", "lambda_q1", "lambda_k1", "lambda_q2", "lambda_k2",
        "g_subln", "w_out", "g_post_mix", "g_pre_mlp", "w_up", "w_down", "g_post_mlp"]


def kernel(**inputs):
    import numpy as _np
    import concourse.bacc as _bacc
    from concourse import mybir as _mybir
    from concourse.bass_utils import run_bass_kernel_spmd as _run

    nc = _bacc.Bacc("TRN2", target_bir_lowering=False, num_devices=1)
    arrays, args = {}, []
    for name in _INS:
        a = _np.ascontiguousarray(inputs[name])
        arrays[f"in_{name}_dram"] = a
        args.append(nc.dram_tensor(f"in_{name}_dram", a.shape, _mybir.dt.from_np(a.dtype), kind="ExternalInput").ap())
    args.append(nc.dram_tensor("out_0_dram", (1, S, D), _mybir.dt.float32, kind="ExternalOutput").ap())
    hybrid_block(nc, *args)
    r = _run(nc, [arrays], core_ids=[0])
    return r.results[0]["out_0_dram"]
```

```python
from contextlib import ExitStack

import concourse.bass as bass
from concourse import mybir

F32 = mybir.dt.float32
F32R = mybir.dt.float32r
ALU = mybir.AluOpType
ACT = mybir.ActivationFunctionType
AX = mybir.AxisListType

P = 128
D = 1024
S = 2048
KT = D // P
RT = S // P
HD = 64
DFF = 4 * D
EPS = 1e-6
FOX_HEADS = 8
DIFF_HEADS = 4
LAM_INIT = 0.2
LOGIT_COL = 3 * FOX_HEADS * HD
QKV_TILES = 24
ROOT = D ** -0.5
MASKED = -float(2 ** 100)


def f32(ap):
    return ap.bitcast(F32)


class Room:

    def __init__(self, nc, ctx, stage):
        self.nc, self.ctx, self.stage = nc, ctx, stage

    def sb(self, name, shape, dt=F32):
        return self.ctx.enter_context(self.nc.sbuf_tensor(f"{self.stage}_{name}", shape, dt))

    def ps(self, name, shape):
        return self.ctx.enter_context(self.nc.psum_tensor(f"{self.stage}_{name}", shape, F32))

    def sem(self, name):
        return self.ctx.enter_context(self.nc.semaphore(f"{self.stage}_{name}"))


def project(nc, x, g_pre_mix, w_in, b_forget, qkvT, q_rows, k_rows):
    H = FOX_HEADS
    SEGS = P // H
    SEG = S // SEGS
    log_sig = nc.dram_tensor("log_sig", [H, S], F32).ap()
    cum = nc.dram_tensor("cum", [H, S], F32).ap()
    with ExitStack() as ctx:
        r = Room(nc, ctx, "pj")
        ident = r.sb("ident", [P, P])
        gain_junk = r.sb("gain_junk", [P, 2, D])
        gain, junk = gain_junk[:, 0], gain_junk[:, 1]
        xn = r.sb("xn", [P, 2, D])
        ss = r.sb("ss", [P, RT])
        ms = r.sb("ms", [P, RT])
        rstd = r.sb("rstd", [P, RT])
        power = r.sb("power", [P, 1])
        eps = r.sb("eps", [P, 1])
        h_hi = r.sb("h_hi", [P, KT, S], F32R)
        h_lo = r.sb("h_lo", [P, KT, S], F32R)
        w_raw = r.sb("w_raw", [P, 2, KT, P])
        w_hi = r.sb("w_hi", [P, 2, KT, P], F32R)
        w_lo = r.sb("w_lo", [P, 2, KT, P], F32R)
        qscale = r.sb("qscale", [P, QKV_TILES + 1])
        proj_sb = r.sb("proj_sb", [P, 2, S])
        acc = r.ps("acc", [P, 2, S])
        b = r.sb("b", [P, 1])
        z, az, e, w, lw, t1, c = (r.sb(name, [P, SEG]) for name in ("z", "az", "e", "w", "lw", "t1", "c"))
        hi, lo, nhi, nlo = (r.sb(name, [P, SEG], F32R) for name in ("hi", "lo", "nhi", "nlo"))
        ones = r.sb("ones", [P, SEG])
        zeros = r.sb("zeros", [P, SEG])
        long_c = r.sb("long_c", [H, S])
        pos = r.sb("pos", [SEGS, SEG])
        down = r.sb("down", [SEGS, DIFF_HEADS, SEG])
        up = r.sb("up", [SEGS, DIFF_HEADS, SEG])
        x_loaded = [r.sem(f"x_loaded{s}") for s in range(4)]
        gain_loaded = r.sem("gain_loaded")
        const_ready = r.sem("const_ready")
        ss_ready = r.sem("ss_ready")
        rstd_step = r.sem("rstd_step")
        xn_ready = r.sem("xn_ready")
        xT_ready = r.sem("xT_ready")
        h_hi_ready = r.sem("h_hi_ready")
        h_ready = r.sem("h_ready")
        w_loaded = [r.sem(f"w_loaded{s}") for s in range(2)]
        w_hi_ready = r.sem("w_hi_ready")
        w_ready = r.sem("w_ready")
        proj_done = r.sem("proj_done")
        evacuated = r.sem("evacuated")
        stored = [r.sem(f"stored{s}") for s in range(2)]
        rows_ready = r.sem("rows_ready")
        z_loaded = r.sem("z_loaded")
        dc_step = r.sem("dc_step")
        e_ready = r.sem("e_ready")
        around = r.sem("around")
        rows_stored = r.sem("rows_stored")
        SIGMOID_STEPS = 8
        DC_STEPS = SIGMOID_STEPS + 5
        block = ctx.enter_context(nc.Block())
        w_v = w_in.rearrange("o (t p) c -> p (o t) c", p=P)
        half = QKV_TILES // 2
        gap = FOX_HEADS
        xin = [proj_sb[:, n // 2, n % 2 * D:(n % 2 + 1) * D] for n in range(4)]
        long_t = xn[0:H].rearrange("p s n -> p (s n)")
        long_zeros = gain_junk[0:H].rearrange("p s n -> p (s n)")

        def column_tiles(eng, step, pieces=()):
            quarter = half // 4
            for lo in range(0, half, quarter if pieces else 2 * quarter):
                shift = gap if lo >= half // 2 else 0
                with eng.Fori(lo, lo + (quarter if pieces else 2 * quarter)) as i:
                    for j in range(2):
                        step(i + j, 1 - j, 2 * i + (j + 1), 2 * i + j, i * (2 * P) + (j * P + shift))
                if pieces:
                    pieces[lo // quarter]()

        def nothing():
            pass

        def transposed(s):
            return acc[:, 1, s * D:(s + 1) * D].rearrange("p (k r) -> p k r", r=P)

        def segments(rows, h0, h1, k):
            return rows[k, h0:h1, :].rearrange("h (s j) -> (h s) j", j=SEG)

        @block.sync
        def _(sp):
            def load_x(s, t):
                sp.dma_start(xin[s], x[0, bass.ts(t, P), :]).then_inc(x_loaded[s], 16)

            def load(use, s, n, ct, col):
                sp.wait_ge(w_ready, n + 1)
                sp.dma_start(w_raw[:, s], w_v[:, :, bass.ds(col, P)]).then_inc(w_loaded[s], 16)
            load_x(0, 0)
            load_x(1, 1)
            sp.dma_start(gain, g_pre_mix[0:1, :].to_broadcast([P, D])).then_inc(gain_loaded, 16)
            load_x(2, 2)
            load_x(3, 3)
            load(0, 0, 0, QKV_TILES, LOGIT_COL)
            with sp.Fori(0, RT // 4 - 1) as g:
                for s in range(4):
                    sp.wait_ge(xn_ready, 4 * g + s + 1)
                    load_x(s, 4 * g + (s + 4))
            column_tiles(sp, load)

        @block.gpsimd
        def _(pool):
            pool.memset(ident[:, :], 0.0).then_inc(const_ready, 1)
            pool.memset(power[:, :], -0.5).then_inc(const_ready, 1)
            pool.memset(eps[:, :], EPS).then_inc(const_ready, 1)
            pool.wait_ge(const_ready, 1)
            pool.affine_select(out=ident[:, :], in_=ident[:, :], compare_op=ALU.not_equal, fill=1.0,
                               base=0, pattern=[[-1, P]], channel_multiplier=1).then_inc(const_ready, 1)
            pool.memset(qscale[:, :], 1.0).then_inc(const_ready, 1)
            pool.wait_ge(const_ready, 5)
            for first in (0, half):
                pool.memset(qscale[:, first:first + 4], HD ** -0.5).then_inc(const_ready, 1)
            with pool.Fori(0, RT) as t:
                pool.wait_ge(ss_ready, t + 1)
                pool.tensor_tensor(ms[:, bass.ds(t, 1)], ss[:, bass.ds(t, 1)], eps[:, :], ALU.add)\
                    .then_inc(rstd_step, 1)
                pool.wait_ge(rstd_step, 2 * t + 1)
                pool.tensor_tensor(rstd[:, bass.ds(t, 1)], ms[:, bass.ds(t, 1)], power[:, :],
                                   ALU.pow).then_inc(rstd_step, 1)
            D4 = DIFF_HEADS
            pool.iota(pos[:, :], pattern=[[1, SEG]], base=0, channel_multiplier=SEG,
                      allow_small_or_imprecise_dtypes=True).then_inc(rows_ready, 1)
            pool.wait_ge(rows_ready, 1)
            for h in range(D4):
                slope = 2.0 ** (-8.0 * (h + 1) / D4)
                pool.tensor_scalar(down[:, h, :], pos[:, :], -slope, None, ALU.mult).then_inc(rows_ready, 1)
                pool.tensor_scalar(up[:, h, :], pos[:, :], slope, None, ALU.mult).then_inc(rows_ready, 1)
            pool.wait_ge(rows_ready, 1 + 2 * D4)
            pool.memset(ones[:, :], 1.0).then_inc(rows_ready, 1)
            pool.memset(zeros[:, :], 0.0).then_inc(rows_ready, 1)
            pool.wait_ge(xn_ready, RT)
            pool.memset(long_zeros, 0.0).then_inc(rows_ready, 1)
            pool.wait_ge(rows_ready, 4 + 2 * D4)
            n = 0

            def store(rows, h0, h1, k, src):
                pool.dma_start(segments(rows, h0, h1, k), src).then_inc(rows_stored, 16)
                return 1
            for rows, k, src in ((q_rows, 0, down), (k_rows, 2, up)):
                pool.dma_start(rows[k, H:H + D4, :].rearrange("h (s j) -> s h j", j=SEG), src[:, :, :])\
                    .then_inc(rows_stored, 16)
                n += 1
            for rows, k, src in ((q_rows, 1, zeros), (q_rows, 2, ones), (q_rows, 3, ones), (q_rows, 4, zeros),
                                 (q_rows, 5, zeros), (k_rows, 0, ones), (k_rows, 1, ones), (k_rows, 3, zeros),
                                 (k_rows, 4, ones), (k_rows, 5, ones)):
                n += store(rows, H, H + D4, k, src[0:D4 * SEGS, :])
            for rows, k, src in ((q_rows, 2, ones), (q_rows, 3, ones), (q_rows, 4, zeros), (q_rows, 5, zeros),
                                 (k_rows, 0, ones), (k_rows, 1, ones), (k_rows, 4, ones), (k_rows, 5, ones)):
                n += store(rows, 0, H, k, src[:, :])
            for h in range(H):
                pool.dma_start(b[h * SEGS:(h + 1) * SEGS, :], b_forget[0:1, h:h + 1].to_broadcast([SEGS, 1]))\
                    .then_inc(z_loaded, 16)
            pool.wait_ge(stored[0], 32)
            pool.dma_start(z[:, :], qkvT[QKV_TILES, 0:H, :].rearrange("h (s j) -> (h s) j", j=SEG))\
                .then_inc(z_loaded, 16)
            pool.wait_ge(dc_step, SIGMOID_STEPS)
            pool.dma_start(log_sig.rearrange("h (s j) -> (h s) j", j=SEG), t1[:, :]).then_inc(around, 16)
            pool.wait_ge(around, 16)
            pool.dma_start(long_t, log_sig[:, :]).then_inc(around, 16)
            pool.wait_ge(dc_step, SIGMOID_STEPS + 1)
            pool.dma_start(cum[:, :], long_c[:, :]).then_inc(around, 16)
            pool.wait_ge(around, 48)
            pool.dma_start(c[:, :], cum.rearrange("h (s j) -> (h s) j", j=SEG)).then_inc(around, 16)
            pool.wait_ge(dc_step, DC_STEPS)
            for rows, k, src in ((q_rows, 0, hi), (q_rows, 1, lo), (k_rows, 2, nhi), (k_rows, 3, nlo)):
                n += store(rows, 0, H, k, f32(src[:, :]))
            pool.wait_ge(rows_stored, 16 * n)

        @block.scalar
        def _(act):
            act.sem_inc(evacuated, 2)
            for s in range(2):
                act.sem_inc(stored[s], 16)

            def square(use, s, t):
                act.wait_ge(x_loaded[s], 16 * (use + 1))
                if not isinstance(t, int) or t:
                    act.wait_ge(ss_ready, t)
                act.activation(junk, xin[s], ACT.Square, scale=ROOT,
                               accum_out=ss[:, bass.ds(t, 1)]).then_inc(ss_ready, 1)

            def keep_hi(s, t):
                act.wait_ge(xT_ready, t + 1)
                act.activation(h_hi[:, :, bass.ts(t, P)], transposed(s), ACT.Copy).then_inc(h_hi_ready, 1)

            for t in range(4):
                square(0, t, t)
            with act.Fori(0, RT // 4 - 1) as g:
                for s in range(4):
                    keep_hi(s % 2, 4 * g + s)
                    square(g + 1, s, 4 * g + (s + 4))
            for s in range(4):
                keep_hi(s % 2, RT - 4 + s)

            def evacuate(use, s, n, ct, col):
                act.wait_ge(proj_done, n + 3)
                act.wait_ge(stored[s], 16 * (use + 1))
                act.activation(proj_sb[:, s, :], acc[:, s, :], ACT.Copy,
                               scale=qscale[:, bass.ds(ct, 1)]).then_inc(evacuated, 1)
                act.wait_ge(evacuated, n + 3)
                act.dma_start(qkvT[bass.ds(ct, 1), :, :].rearrange("o p n -> (o p) n"),
                              proj_sb[:, s, :]).then_inc(stored[s], 16)

            def exp():
                act.wait_ge(dc_step, 2)
                act.activation(e[:, :], az[:, :], ACT.Exp, scale=-1.0).then_inc(e_ready, 1)

            def ln():
                act.wait_ge(dc_step, 3)
                act.activation(lw[:, :], w[:, :], ACT.Ln).then_inc(e_ready, 1)
            act.wait_ge(const_ready, 7)
            evacuate(0, 0, 0, QKV_TILES, LOGIT_COL)
            act.preload_act_table_set("natural_log_exp_and_others")
            column_tiles(act, evacuate, (exp, ln, nothing, nothing))
            act.wait_ge(stored[0], 16 * (half + 2))
            act.wait_ge(stored[1], 16 * (half + 1))

        @block.vector
        def _(dve):
            dve.sem_inc(w_ready, 2)

            def normalise(use, s, t):
                dve.wait_ge(rstd_step, 2 * t + 2)
                if not isinstance(t, int) or t > 1:
                    dve.wait_ge(xT_ready, t - 1)
                dve.scalar_tensor_tensor(out=xn[:, s % 2, :], in0=xin[s], scalar=rstd[:, bass.ds(t, 1)],
                                         in1=gain, op0=ALU.mult, op1=ALU.mult).then_inc(xn_ready, 1)

            def keep_lo(s, t):
                dve.wait_ge(h_hi_ready, t + 1)
                dve.tensor_tensor(h_lo[:, :, bass.ts(t, P)], transposed(s), f32(h_hi[:, :, bass.ts(t, P)]), ALU.subtract).then_inc(h_ready, 1)

            def split(use, s, n, ct, col):
                dve.wait_ge(w_loaded[s], 16 * (use + 1))
                dve.wait_ge(proj_done, n + 1)
                dve.tensor_copy(w_hi[:, s], w_raw[:, s]).then_inc(w_hi_ready, 1)
                dve.wait_ge(w_hi_ready, n + 1)
                dve.tensor_tensor(w_lo[:, s], w_raw[:, s], f32(w_hi[:, s]), ALU.subtract).then_inc(w_ready, 1)

            dve.wait_ge(gain_loaded, 16)
            for t in range(2):
                normalise(0, t, t)
            split(0, 0, 0, QKV_TILES, LOGIT_COL)
            with dve.Fori(0, RT // 4 - 1) as g:
                for s in range(4):
                    keep_lo(s % 2, 4 * g + s)
                    normalise(g + (s + 2) // 4, (s + 2) % 4, 4 * g + (s + 2))
            for s in range(4):
                keep_lo(s % 2, RT - 4 + s)
                if s < 2:
                    normalise(RT // 4 - 1, s + 2, RT - 2 + s)
            done = [0]

            def link(ins):
                done[0] += 1
                ins.then_inc(dc_step, 1)
                dve.wait_ge(dc_step, done[0])

            def magnitudes():
                dve.wait_ge(z_loaded, 16 * (H + 1))
                link(dve.tensor_scalar(z[:, :], z[:, :], b[:, :], None, ALU.add))
                link(dve.scalar_tensor_tensor(out=az[:, :], in0=z[:, :], scalar=-1.0, in1=z[:, :],
                                              op0=ALU.mult, op1=ALU.max))

            def corrections():
                dve.wait_ge(e_ready, 1)
                link(dve.tensor_scalar(w[:, :], e[:, :], 1.0, None, ALU.add))
                link(dve.scalar_tensor_tensor(out=t1[:, :], in0=w[:, :], scalar=-1.0, in1=e[:, :],
                                              op0=ALU.add, op1=ALU.subtract))
                link(dve.reciprocal(az[:, :], w[:, :]))
                link(dve.tensor_tensor(t1[:, :], t1[:, :], az[:, :], ALU.mult))

            def log_sigmoids():
                dve.wait_ge(e_ready, 2)
                link(dve.tensor_tensor(t1[:, :], t1[:, :], lw[:, :], ALU.subtract))
                link(dve.scalar_tensor_tensor(out=t1[:, :], in0=z[:, :], scalar=0.0, in1=t1[:, :],
                                              op0=ALU.min, op1=ALU.add))
                assert done[0] == SIGMOID_STEPS

            def sums():
                dve.wait_ge(rows_ready, 4 + 2 * DIFF_HEADS)
                dve.wait_ge(around, 32)
                link(dve.tensor_tensor_scan(long_c[:, :], long_t, long_zeros, 0.0, ALU.add, ALU.add))
                dve.wait_ge(around, 64)
                link(dve.tensor_copy(hi[:, :], c[:, :]))
                link(dve.tensor_tensor(lo[:, :], c[:, :], f32(hi[:, :]), ALU.subtract))
                link(dve.tensor_scalar(nhi[:, :], f32(hi[:, :]), -1.0, None, ALU.mult))
                link(dve.tensor_scalar(nlo[:, :], f32(lo[:, :]), -1.0, None, ALU.mult))
                assert done[0] == DC_STEPS
            column_tiles(dve, split, (magnitudes, corrections, log_sigmoids, sums))

        @block.tensor
        def _(pe):
            pe.sem_inc(proj_done, 2)
            pe.wait_ge(const_ready, 4)

            def transpose(s, t):
                pe.wait_ge(xn_ready, t + 1)
                if not isinstance(t, int) or t > 1:
                    pe.wait_ge(h_ready, t - 1)
                for k in range(KT):
                    last = pe.transpose(acc[:, 1, s * D + k * P:s * D + (k + 1) * P],
                                        xn[:, s, k * P:(k + 1) * P], ident[:, :])
                last.then_inc(xT_ready, 1)

            def products(s, rows):
                for k in range(KT):
                    pe.matmul(acc[:, s, rows], w_hi[:, s, k], h_hi[:, k, rows], start=(k == 0), stop=False)
                    pe.matmul(acc[:, s, rows], w_hi[:, s, k], h_lo[:, k, rows], start=False, stop=False)
                    last = pe.matmul(acc[:, s, rows], w_lo[:, s, k], h_hi[:, k, rows],
                                     start=False, stop=(k == KT - 1))
                return last

            for t in range(2):
                transpose(t, t)
            with pe.Fori(0, RT // 4 - 1) as g:
                for s in range(4):
                    transpose(s % 2, 4 * g + (s + 2))
                pe.wait_ge(w_ready, 3)
                pe.wait_ge(h_ready, 4 * g + 4)
                products(0, bass.ts(g, 512))
            for s in range(2):
                transpose(s, RT - 2 + s)
            pe.wait_ge(h_ready, RT)
            products(0, slice(S - 512, S)).then_inc(proj_done, 1)

            def multiply(use, s, n, ct, col):
                pe.wait_ge(w_ready, n + 3)
                pe.wait_ge(evacuated, n + 1)
                for rb in range(S // 512):
                    last = products(s, slice(rb * 512, (rb + 1) * 512))
                last.then_inc(proj_done, 1)
            column_tiles(pe, multiply)


FOX, DIFF = 0, 1
RAW = 80
COMBOS = (80, 40)
BLOCKS = (8, 4)
STAT = 80
RING = 4
X_USES = ("v_flip", "stat_flip", "o_var", "o_bcast")
READERS = {"stat_scores": "stat_exp", "v_flip": "v_split", "stat_flip": "stat_flip", "o_var": "o_var",
           "o_bcast": "o_norm"}
STAGES = 5
PIECES = [(w, s, p) for s in range(2) for p in range(4) for w in "qk"]
PIECES = PIECES[:8] + [("v", 0, 0), ("v", 0, 1)] + PIECES[8:] + [("v", 0, 2), ("v", 0, 3)]
SPACING = (4, 3)
PRING, SRING = 4, 4
LAG = (4, 4)
TAIL = 12


def stat_chunks():
    return [(s, qt, ch) for s in range(2) for qt in range(RT) for ch in range(qt // 4 + 1)]


def stat_width(qt, ch):
    return min(512, P * (qt + 1) - 512 * ch)


def raw_chunks(kind):
    if kind == FOX:
        return [(s, J, j) for s in range(2) for J in range(4) for j in range(4 * J + 4)]
    return [(s, J, j) for J in range(4) for j in range(4 * J + 4) for s in range(2)]


def on_pool(kind, m):
    return m % 4 != 3 if kind == FOX else True


def lo_count(kind, m, pool):
    return sum(on_pool(kind, n) == pool for n in range(m + 1))


LO_TOTAL = [[lo_count(k, COMBOS[k] - 1, p) for k in (FOX, DIFF)] for p in (False, True)]
STAT_STEPS = ("stat_top", "stat_corr", "stat_sum", "stat_ln", "stat_shift", "stat_flip", "stat_rows")


def plan(kind, with_stats=True):
    raws = RAW if kind is not None else 0
    size = (RAW if raws else 62) + TAIL
    early = [[] for _ in range(size)]
    late = [[] for _ in range(size)]
    if with_stats:
        late[0].append(("rows",))
        starts, span = ((2, 38), 34) if raws else ((1, 29), 26)
        prep_at = ((0, 2, 7, 14), (26, 30, 40, 47)) if raws else ((0, 1, 4, 10), (20, 24, 30, 36))
        v_at = (20, 23, 56, 61) if raws else (16, 18, 44, 48)
        for s in range(2):
            for p in range(4):
                late[prep_at[s][p]].append(("prep", s, p))
        for g in range(4):
            late[v_at[g]].append(("v_flip", g))
            late[v_at[g] + 1].append(("v_split", g))
        at, done = [], 0
        chunks = stat_chunks()
        total = sum(stat_width(qt, ch) for _, qt, ch in chunks) // 2
        for g, (s, qt, ch) in enumerate(chunks):
            if g % (STAT // 2) == 0:
                done = 0
            t = starts[s] + span * done // total
            if g >= SPACING[raws > 0]:
                t = max(t, at[g - SPACING[raws > 0]] + 2)
            at.append(t)
            done += stat_width(qt, ch)
            late[t].append(("stat_scores", g))
            late[t + 1].append(("stat_max", g))
            early[t + 2].append(("stat_exp", g))
        for s in range(2):
            t = at[STAT // 2 * (s + 1) - 1] + 3
            for n, what in enumerate(STAT_STEPS):
                late[t + n].append((what, s))
    split_at, pv_at = {}, {}
    for c in range(raws):
        if kind == FOX or c % 2:
            m = c if kind == FOX else c // 2
            split_at[c + 1] = m
            pv_at[c + LAG[kind]] = m
    steps, blocks = [], 0
    for t in range(size):
        if t < raws:
            steps.append(("scores", t))
        if t in pv_at:
            m = pv_at[t]
            steps.append(("pv", m))
            s, J, j = raw_chunks(kind)[m if kind == FOX else 2 * m]
            if j == 4 * J + 3:
                uses = (("o_first", 1),) if kind == FOX else (("o_first", 1), ("o_var", 3), ("o_pow", 4),
                                                               ("o_bcast", 7), ("o_norm", 9))
                for what, n in uses:
                    late[min(t + n, size - 1)].append((what, blocks))
                blocks += 1
        steps += early[t]
        if t < raws:
            steps.append(("exp", t))
        steps += [st for st in late[t] if st[0] == "stat_max"]
        if t in split_at:
            steps.append(("split", split_at[t]))
        steps += [st for st in late[t] if st[0] != "stat_max"]
    users = [st for st in steps if st[0] in READERS]
    for before, st in zip(users, users[RING:]):
        assert steps.index((READERS[before[0]],) + before[1:]) < steps.index(st), (before, st)
    out, used = [], 0
    for st in steps:
        out.append(st)
        for _ in range({"prep": 2, "v_flip": 1}.get(st[0], 0)):
            assert PIECES[used][0] in ("qk" if st[0] == "prep" else "v")
            out.append(("load", used + STAGES))
            used += 1
    return out


def attend(nc, qkvT, q_rows, k_rows, lams, g_subln, mixT):
    with ExitStack() as ctx:
        r = Room(nc, ctx, "at")
        q1 = r.sb("q1", [P, 2, 2, S], F32R)
        k1 = r.sb("k1", [P, 2, 2, S], F32R)
        q2 = r.sb("q2", [P, 2, 2, S], F32R)
        k2 = r.sb("k2", [P, 2, 2, S], F32R)
        vals = r.sb("vals", [P, 2, RT, 256], F32R)
        stage = r.sb("stage", [P, STAGES, 512])
        probs = r.sb("probs", [P, PRING, 512])
        p_hi = r.sb("p_hi", [P, SRING, 512], F32R)
        p_lo = r.sb("p_lo", [P, SRING, 512], F32R)
        o_sb = r.sb("o_sb", [P, 2, 512])
        o_half = r.sb("o_half", [P, 512])
        ident_r = r.sb("ident_r", [P, P], F32R)
        ident = f32(ident_r[:, :])
        mask_q = r.sb("mask_q", [P, P], F32R)
        mask_k = r.sb("mask_k", [P, P], F32R)
        made = o_half[:, 0:3 * P].rearrange("p (a n) -> p a n", n=P)
        mean = r.sb("mean", [P, 1])
        power = r.sb("power", [P, 4])
        var = r.sb("var", [P, 4])
        rstd = r.sb("rstd", [P, 4])
        nmax = r.sb("nmax", [P, 2, 2, 4, RT])
        rsum = r.sb("rsum", [P, 2, 2, 4, RT])
        top = r.sb("top", [P, RT])
        corr = r.sb("corr", [P, 4, RT])
        total = r.sb("total", [P, RT])
        logsum = r.sb("logsum", [P, RT])
        shift = r.sb("shift", [P, 2 * RT], F32R)
        shiftT = r.sb("shiftT", [2 * RT, 2, P], F32R)
        lam_in = probs[:, 0, 0:4 * HD].rearrange("p (a d) -> p a d", d=HD)
        lam_s = r.sb("lam_s", [P, 4])
        nlam = r.sb("nlam", [P, 1])
        gsub = r.sb("gsub", [P, 1])
        ps_ring = r.ps("ps_ring", [P, RING, 512])
        ps_sc = r.ps("ps_sc", [P, 2, 512])
        ps_o = r.ps("ps_o", [P, 2, 512])

        const_loaded = r.sem("const_loaded")
        const_pool = r.sem("const_pool")
        const_dve = r.sem("const_dve")
        const_act = r.sem("const_act")
        staged = [r.sem(f"staged{n}") for n in range(STAGES)]
        rows_loaded = r.sem("rows_loaded")
        shift_loaded = [r.sem(f"shift_loaded{s}") for s in range(2)]
        hi_ready = r.sem("hi_ready")
        lo_ready = r.sem("lo_ready")
        x_ready = r.sem("x_ready")
        x_free = r.sem("x_free")
        v_hi_ready = r.sem("v_hi_ready")
        stat_scored = r.sem("stat_scored")
        stat_maxed = r.sem("stat_maxed")
        stat_exped = r.sem("stat_exped")
        stat_dve = r.sem("stat_dve")
        stat_act = r.sem("stat_act")
        scored = r.sem("scored")
        exped = r.sem("exped")
        combined = r.sem("combined")
        p_hi_ready = r.sem("p_hi_ready")
        p_lo_dve = r.sem("p_lo_dve")
        p_lo_pool = r.sem("p_lo_pool")
        p_used = r.sem("p_used")
        o_half_ready = r.sem("o_half_ready")
        o_free = r.sem("o_free")
        o_squared = r.sem("o_squared")
        o_pow = r.sem("o_pow")
        o_stored = [r.sem(f"o_stored{s}") for s in range(2)]
        block = ctx.enter_context(nc.Block())

        plans = {None: plan(None), FOX: plan(FOX), DIFF: plan(DIFF)}
        last_plan = plan(DIFF, with_stats=False)
        stats, raws = stat_chunks(), [raw_chunks(FOX), raw_chunks(DIFF)]
        X_OPEN, X_FOX, X_DIFF = (sum(st[0] in X_USES for st in plans[k]) for k in (None, FOX, DIFF))

        class Half:

            def __init__(self, kind, i, steps=None):
                self.kind, self.i = kind, i
                self.steps = plans[kind] if steps is None else steps
                assert (2 * STAT + X_FOX + X_DIFF) % RING == 0
                base = {None: 0, FOX: STAT + X_OPEN, DIFF: 2 * STAT + X_OPEN + X_FOX}[kind]
                self.users = [st for st in self.steps if st[0] in READERS]
                self.banks = {st: (base + n) % RING for n, st in enumerate(self.users)}
                self.xpos = {}
                for st in self.steps:
                    if st[0] in X_USES:
                        self.xpos[st] = len(self.xpos)
                if kind is None:
                    self.n, self.prep_kind, self.prep_i, self.slot = 0, FOX, 0, 0
                    self.x = self.raw = 0
                    return
                self.n = 2 * i + 1 + kind
                self.prep_kind = DIFF if kind == FOX else FOX
                self.prep_i = i if kind == FOX else i + 1
                self.slot = 1 - kind
                self.raw = 2 * RAW * i + RAW * kind
                self.combo = sum(COMBOS) * i + COMBOS[FOX] * kind
                self.block = sum(BLOCKS) * i + BLOCKS[FOX] * kind
                self.x = (X_FOX + X_DIFF) * i + X_OPEN + X_FOX * kind
                self.shift_value = 32 * (2 * i + kind) + 32

            def x_value(self, st):
                return self.x + (self.xpos[st] + 1)

            def lo_value(self, m, pool):
                both = sum(LO_TOTAL[pool])
                if m < 0:
                    m += COMBOS[1 - self.kind]
                    if self.kind == DIFF:
                        return self.i * both + (4 + lo_count(FOX, m, pool))
                    return self.i * both + (4 + LO_TOTAL[pool][FOX] + lo_count(DIFF, m, pool) - both)
                before = LO_TOTAL[pool][FOX] if self.kind == DIFF else 0
                return self.i * both + (4 + before + lo_count(self.kind, m, pool))

        def bank(h, *st):
            return ps_ring[:, h.banks[st], :]

        def halves(eng, emit):
            emit(Half(None, 0))
            with eng.Fori(0, DIFF_HEADS - 1) as i:
                emit(Half(FOX, i))
                emit(Half(DIFF, i))
            emit(Half(FOX, DIFF_HEADS - 1))
            emit(Half(DIFF, DIFF_HEADS - 1, last_plan))

        def width(J, j):
            return max(0, j - 4 * J) * P

        def block_of(kind, m):
            return raws[kind][m if kind == FOX else 2 * m]

        def block_last(kind, b):
            ends = [m for m in range(COMBOS[kind]) if block_of(kind, m)[2] == 4 * block_of(kind, m)[1] + 3]
            return ends[b]

        def block_number(kind, m):
            s, J, _ = block_of(kind, m)
            return 4 * s + J if kind == FOX else J

        def staged_value(n, idx):
            return 128 * n + 32 * (idx // STAGES + 1)

        def piece_index(what, s, p):
            return PIECES.index((what, s, p))

        @block.sync
        def _(sp):
            def load(kind, i, idx):
                what, s, p = PIECES[idx]
                base = (0 if kind == FOX else 12) + {"q": 0, "k": 4, "v": 8}[what]
                for z in range(2):
                    rows = slice(z * 64, (z + 1) * 64) if what == "v" else slice(s * 64, (s + 1) * 64)
                    sp.dma_start(stage[z * 64:(z + 1) * 64, idx % STAGES, :],
                                 qkvT[bass.ds(i + base, 1), rows, p * 512:(p + 1) * 512]
                                 .rearrange("o p n -> (o p) n")).then_inc(staged[idx % STAGES], 16)

            def load_rows(kind, i):
                for s in range(2):
                    at = 2 * i + s if kind == FOX else i + FOX_HEADS
                    for dst, src in ((q2, q_rows), (k2, k_rows)):
                        sp.dma_start(f32(dst[0:6, kind, s, :]),
                                     src[:, bass.ds(at, 1), :].rearrange("r o n -> r (o n)"))\
                          .then_inc(rows_loaded, 16)

            for idx in range(2):
                load(FOX, 0, idx)
            sp.wait_ge(const_pool, 1)
            sp.wait_ge(const_dve, 1)
            load_rows(FOX, 0)
            for idx in range(2, STAGES):
                load(FOX, 0, idx)

            def emit(h):
                for st in h.steps:
                    op = st[0]
                    if op == "rows" and h.kind is not None:
                        sp.wait_ge(scored, h.raw + 1)
                        if h.kind == FOX:
                            sp.wait_ge(const_pool, 11)
                        load_rows(h.prep_kind, h.prep_i)
                    elif op == "load":
                        idx = st[1]
                        if idx >= 20 and h.kind == FOX and isinstance(h.i, int):
                            continue
                        what, s, p = PIECES[idx - STAGES]
                        if what == "v":
                            sp.wait_ge(x_ready, h.x_value(("v_flip", p)))
                        else:
                            sp.wait_ge(lo_ready, 16 * h.n + (8 * s + 2 * p + (2 if what == "k" else 1)))
                        if idx < 20:
                            load(h.prep_kind, h.prep_i, idx)
                        elif h.kind is None:
                            load(DIFF, 0, idx - 20)
                        else:
                            load(h.kind, h.i + 1, idx - 20)
                    elif op == "stat_rows":
                        s = st[1]
                        sp.wait_ge(x_free, h.x_value(("stat_flip", s)))
                        for z in range(2):
                            sp.dma_start(f32(q2[4 + z:5 + z, h.slot, s, :].rearrange("o (t q) -> o t q", q=P)),
                                         f32(shiftT[z * RT:(z + 1) * RT, s, :])).then_inc(shift_loaded[s], 16)
                    elif op == "o_first" and h.kind == FOX:
                        b = st[1]
                        s, J, _ = block_of(FOX, block_last(FOX, b))
                        sp.wait_ge(o_free, h.block + b + 3)
                        sp.dma_start(mixT[bass.ds(h.i, 1), s * 64:(s + 1) * 64, J * 512:(J + 1) * 512]
                                     .rearrange("o p n -> (o p) n"), o_sb[0:64, b % 2, :])\
                          .then_inc(o_stored[b % 2], 16)
                    elif op == "o_norm":
                        b = st[1]
                        sp.wait_ge(x_free, h.x_value(("o_bcast", b)))
                        sp.dma_start(mixT[bass.ds(h.i + 4, 1), :, b * 512:(b + 1) * 512]
                                     .rearrange("o p n -> (o p) n"), o_sb[:, b % 2, :])\
                          .then_inc(o_stored[b % 2], 16)
            halves(sp, emit)
            for s in range(2):
                sp.wait_ge(o_stored[s], 16 * (1 + sum(BLOCKS) * DIFF_HEADS // 2))

        @block.gpsimd
        def _(pool):
            pool.sem_inc(p_lo_pool, 4)
            pool.sem_inc(o_pow, 1)
            pool.memset(f32(q2[0:64, FOX, :, :]), 0.0).then_inc(const_pool, 1)
            pool.wait_ge(const_pool, 1)
            pool.memset(made[:, :, :], 0.0).then_inc(const_pool, 1)
            pool.memset(nmax[:, :, :, :, :], -MASKED).then_inc(const_pool, 1)
            pool.memset(rsum[:, :, :, :, :], 0.0).then_inc(const_pool, 1)
            pool.memset(mean[:, :], 1.0 / P).then_inc(const_pool, 1)
            pool.memset(power[:, :], -0.5).then_inc(const_pool, 1)
            pool.wait_ge(const_pool, 6)
            for n, (compare, fill, step, mult) in enumerate(((ALU.not_equal, 1.0, -1, 1),
                                                             (ALU.is_ge, MASKED, -1, 1),
                                                             (ALU.is_ge, MASKED, 1, -1))):
                pool.affine_select(out=made[:, n, :], in_=made[:, n, :], compare_op=compare, fill=fill,
                                   base=0, pattern=[[step, P]], channel_multiplier=mult).then_inc(const_pool, 1)
            pool.wait_ge(const_pool, 9)

            def emit(h):
                full, narrow = h.kind is not None, None
                split_last = -1
                for st in h.steps:
                    op = st[0]
                    if op == "prep":
                        _, s, p = st
                        base = 24 * h.n + (12 * s + 3 * p)
                        cols = slice(p * 512, (p + 1) * 512)
                        if full:
                            pool.wait_ge(p_lo_pool, h.lo_value(split_last, True))
                            pool.wait_ge(o_pow, BLOCKS[DIFF] * h.i + 1)
                            full = False
                        pool.wait_ge(hi_ready, base + 2)
                        pool.tensor_tensor(q1[64:P, h.slot, s, cols], stage[64:P, piece_index("q", s, p) % STAGES, :],
                                           f32(q2[64:P, h.slot, s, cols]), ALU.subtract).then_inc(lo_ready, 1)
                        pool.wait_ge(hi_ready, base + 3)
                        pool.tensor_tensor(k2[64:P, h.slot, s, cols], stage[64:P, piece_index("k", s, p) % STAGES, :],
                                           f32(k1[64:P, h.slot, s, cols]), ALU.subtract).then_inc(lo_ready, 1)
                        narrow = 16 * h.n + (8 * s + 2 * p + 2)
                        if h.kind is None and (s, p) == (0, 3):
                            for t in (q2, k2):
                                pool.memset(f32(t[0:64, DIFF, :, :]), 0.0).then_inc(const_pool, 1)
                    elif (op == "split" and on_pool(h.kind, st[1])) or op == "o_pow":
                        if narrow is not None:
                            pool.wait_ge(lo_ready, narrow)
                            narrow = None
                        full = True
                        if op == "o_pow":
                            pool.wait_ge(x_free, h.x_value(("o_var", st[1])))
                            pool.tensor_tensor(rstd[:, :], var[:, :], power[:, :], ALU.pow).then_inc(o_pow, 1)
                            if h.steps is not last_plan:
                                pool.wait_ge(o_pow, BLOCKS[DIFF] * h.i + (st[1] + 2))
                            continue
                        m = split_last = st[1]
                        _, J, j = block_of(h.kind, m)
                        off = width(J, j)
                        c = m if h.kind == FOX else 2 * m
                        pool.wait_ge(p_hi_ready, h.combo + m + 1)
                        pool.tensor_tensor(p_lo[:, m % SRING, off:512], probs[:, c % PRING, off:512],
                                           f32(p_hi[:, m % SRING, off:512]), ALU.subtract).then_inc(p_lo_pool, 1)
            halves(pool, emit)

        @block.scalar
        def _(act):
            act.sem_inc(exped, 2)
            for n, v in enumerate(lams):
                act.dma_start(lam_in[:, n, :], v[0:1, :].to_broadcast([P, HD])).then_inc(const_loaded, 16)
            act.dma_start(gsub[:, :], g_subln.rearrange("o d -> d o")).then_inc(const_loaded, 16)
            act.preload_act_table_set("natural_log_exp_and_others")
            act.wait_ge(const_dve, 6)
            act.activation(lam_s[:, 2:4], lam_s[:, 0:2], ACT.Exp).then_inc(const_act, 1)

            def emit(h):
                for st in h.steps:
                    op = st[0]
                    if op == "stat_exp":
                        g = st[1]
                        s, qt, ch = stats[g]
                        n = stat_width(qt, ch)
                        act.wait_ge(stat_maxed, STAT * h.n + g + 1)
                        scores = bank(h, "stat_scores", g)[:, 0:n]
                        act.activation(scores, scores, ACT.Exp,
                                       bias=nmax[:, h.slot, s, ch, qt:qt + 1],
                                       accum_out=rsum[:, h.slot, s, ch, qt:qt + 1]).then_inc(stat_exped, 1)
                    elif op == "stat_corr":
                        act.wait_ge(stat_dve, 7 * (2 * h.n + st[1]) + 2)
                        act.activation(corr[:, :, :], corr[:, :, :], ACT.Exp).then_inc(stat_act, 1)
                    elif op == "stat_ln":
                        act.wait_ge(stat_dve, 7 * (2 * h.n + st[1]) + 4)
                        act.activation(logsum[:, :], total[:, :], ACT.Ln).then_inc(stat_act, 1)
                    elif op == "v_split":
                        g = st[1]
                        act.wait_ge(x_ready, h.x_value(("v_flip", g)))
                        src = bank(h, "v_flip", g).rearrange("p (t v) -> p t v", v=P)
                        if h.prep_kind == FOX:
                            for s in range(2):
                                last = act.activation(vals[:, h.slot, 4 * g:4 * g + 4, s * P:s * P + 64],
                                                      src[:, :, s * 64:(s + 1) * 64], ACT.Copy)
                            last.then_inc(v_hi_ready, 1)
                        else:
                            act.activation(vals[:, h.slot, 4 * g:4 * g + 4, 0:P], src, ACT.Copy)\
                               .then_inc(v_hi_ready, 1)
                    elif op == "exp":
                        c = st[1]
                        _, J, j = raws[h.kind][c]
                        off = width(J, j)
                        act.wait_ge(scored, h.raw + c + 2)
                        if c >= PRING:
                            m = c - PRING if h.kind == FOX else (c - PRING) // 2
                            pool = on_pool(h.kind, m)
                        else:
                            m = -((PRING - c + 1) // 2) if h.kind == FOX else c - PRING
                            pool = on_pool(1 - h.kind, m + COMBOS[1 - h.kind])
                        act.wait_ge(p_lo_pool if pool else p_lo_dve, h.lo_value(m, pool))
                        act.activation(probs[:, c % PRING, off:512], ps_sc[:, c % 2, off:512], ACT.Exp)\
                           .then_inc(exped, 1)
                    elif op == "o_first" and h.kind == FOX:
                        b = st[1]
                        act.wait_ge(p_used, h.combo + block_last(FOX, b) + 1 + SRING)
                        act.wait_ge(o_free, h.block + b + 2)
                        if b == 0:
                            act.wait_ge(x_ready, h.x)
                        act.activation(o_half[0:64, :], ps_o[64:P, b % 2, :], ACT.Copy).then_inc(o_half_ready, 1)
                    elif op == "o_first":
                        b = st[1]
                        act.wait_ge(o_free, h.block + b + 3)
                        if b:
                            act.wait_ge(x_ready, h.x_value(("o_var", b - 1)))
                        act.activation(o_half[:, :], o_sb[:, b % 2, :], ACT.Square).then_inc(o_squared, 1)
            halves(act, emit)

        @block.vector
        def _(dve):
            dve.sem_inc(p_lo_dve, 4)
            dve.sem_inc(o_free, 2)
            for s in range(2):
                dve.sem_inc(o_stored[s], 16)
            dve.memset(f32(k2[0:64, FOX, :, :]), 0.0).then_inc(const_dve, 1)
            dve.wait_ge(const_pool, 9)
            for n, t in enumerate((ident_r, mask_q, mask_k)):
                dve.tensor_copy(t[:, :], made[:, n, :]).then_inc(const_dve, 1)
            dve.wait_ge(const_loaded, 80)
            lam_v = lam_in[:, :, :].rearrange("p (a b) d -> p a b d", b=2)
            dve.tensor_tensor(lam_v[:, :, 0, :], lam_v[:, :, 0, :], lam_v[:, :, 1, :], ALU.mult)\
               .then_inc(const_dve, 1)
            dve.wait_ge(const_dve, 5)
            dve.tensor_reduce(lam_s[:, 0:2], lam_v[:, :, 0, :], AX.X, ALU.add).then_inc(const_dve, 1)
            dve.wait_ge(const_act, 1)
            dve.tensor_tensor(nlam[:, :], lam_s[:, 3:4], lam_s[:, 2:3], ALU.subtract).then_inc(const_dve, 1)
            dve.wait_ge(const_dve, 7)
            dve.tensor_scalar(nlam[:, :], nlam[:, :], LAM_INIT, None, ALU.subtract).then_inc(const_dve, 1)
            dve.tensor_scalar(gsub[:, :], gsub[:, :], 1.0 - LAM_INIT, None, ALU.mult).then_inc(const_dve, 1)
            dve.wait_ge(const_dve, 9)

            def emit(h):
                for st in h.steps:
                    op = st[0]
                    if op == "prep":
                        _, s, p = st
                        base = 24 * h.n + (12 * s + 3 * p)
                        cols = slice(p * 512, (p + 1) * 512)
                        q_at, k_at = piece_index("q", s, p), piece_index("k", s, p)
                        if h.kind is not None and (s, p) == (0, 0):
                            dve.wait_ge(scored, h.raw + 1)
                        dve.wait_ge(staged[q_at % STAGES], staged_value(h.n, q_at))
                        dve.tensor_copy(q1[:, h.slot, s, cols], stage[:, q_at % STAGES, :]).then_inc(hi_ready, 1)
                        dve.wait_ge(hi_ready, base + 1)
                        dve.tensor_copy(q2[64:P, h.slot, s, cols], f32(q1[64:P, h.slot, s, cols]))\
                           .then_inc(hi_ready, 1)
                        dve.wait_ge(staged[k_at % STAGES], staged_value(h.n, k_at))
                        dve.tensor_copy(k1[:, h.slot, s, cols], stage[:, k_at % STAGES, :]).then_inc(hi_ready, 1)
                    elif op == "stat_max":
                        g = st[1]
                        s, qt, ch = stats[g]
                        dve.wait_ge(stat_scored, STAT * h.n + g + 1)
                        dve.tensor_reduce(nmax[:, h.slot, s, ch, qt:qt + 1],
                                          bank(h, "stat_scores", g)[:, 0:stat_width(qt, ch)], AX.X,
                                          ALU.max, negate=True).then_inc(stat_maxed, 1)
                    elif op in STAT_STEPS:
                        s = st[1]
                        base = 7 * (2 * h.n + s)
                        act_base = 2 * (2 * h.n + s)
                        nm, rs = nmax[:, h.slot, s], rsum[:, h.slot, s]
                        if op == "stat_top":
                            dve.wait_ge(stat_exped, STAT * h.n + STAT // 2 * (s + 1))
                            dve.tensor_reduce(top[:, :], nm.rearrange("p c t -> p t c"), AX.X, ALU.min)\
                               .then_inc(stat_dve, 1)
                            dve.wait_ge(stat_dve, base + 1)
                            dve.tensor_tensor(corr[:, :, :], top[:, :].unsqueeze(1).to_broadcast([P, 4, RT]), nm,
                                              ALU.subtract).then_inc(stat_dve, 1)
                        elif op == "stat_sum":
                            dve.wait_ge(stat_act, act_base + 1)
                            dve.tensor_tensor(corr[:, :, :], corr[:, :, :], rs, ALU.mult).then_inc(stat_dve, 1)
                            dve.wait_ge(stat_dve, base + 3)
                            dve.tensor_reduce(total[:, :], corr[:, :, :].rearrange("p c t -> p t c"), AX.X, ALU.add)\
                               .then_inc(stat_dve, 1)
                        elif op == "stat_shift":
                            dve.wait_ge(stat_act, act_base + 2)
                            dve.tensor_tensor(total[:, :], top[:, :], logsum[:, :], ALU.subtract)\
                               .then_inc(stat_dve, 1)
                            dve.wait_ge(stat_dve, base + 5)
                            dve.tensor_copy(shift[:, 0:RT], total[:, :]).then_inc(stat_dve, 1)
                            dve.wait_ge(stat_dve, base + 6)
                            dve.tensor_tensor(shift[:, RT:2 * RT], total[:, :], f32(shift[:, 0:RT]),
                                              ALU.subtract).then_inc(stat_dve, 1)
                        elif op == "stat_flip":
                            dve.wait_ge(x_ready, h.x_value(st))
                            if h.kind is not None:
                                dve.wait_ge(shift_loaded[s], 32 * h.n)
                            dve.tensor_copy(shiftT[:, s, :], bank(h, "stat_flip", s)[0:2 * RT, 0:P])\
                               .then_inc(x_free, 1)
                    elif op == "v_split":
                        g = st[1]
                        dve.wait_ge(v_hi_ready, 4 * h.n + g + 1)
                        src = bank(h, "v_flip", g).rearrange("p (t v) -> p t v", v=P)
                        t4 = slice(4 * g, 4 * g + 4)
                        if h.prep_kind == FOX:
                            for s in range(2):
                                last = dve.tensor_tensor(vals[:, h.slot, t4, s * P + 64:(s + 1) * P],
                                                         src[:, :, s * 64:(s + 1) * 64],
                                                         f32(vals[:, h.slot, t4, s * P:s * P + 64]), ALU.subtract)
                        else:
                            last = dve.tensor_tensor(vals[:, h.slot, t4, P:2 * P], src,
                                                     f32(vals[:, h.slot, t4, 0:P]), ALU.subtract)
                        last.then_inc(x_free, 1)
                    elif op == "split":
                        m = st[1]
                        _, J, j = block_of(h.kind, m)
                        off = width(J, j)
                        c = m if h.kind == FOX else 2 * m
                        if h.kind == FOX:
                            dve.wait_ge(exped, h.raw + c + 3)
                        else:
                            dve.wait_ge(exped, h.raw + c + 4)
                            dve.scalar_tensor_tensor(out=probs[:, c % PRING, off:512],
                                                     in0=probs[:, (c + 1) % PRING, off:512], scalar=nlam[:, :],
                                                     in1=probs[:, c % PRING, off:512],
                                                     op0=ALU.mult, op1=ALU.add).then_inc(combined, 1)
                            dve.wait_ge(combined, COMBOS[DIFF] * h.i + m + 1)
                        dve.wait_ge(p_used, h.combo + m + 1)
                        dve.tensor_copy(p_hi[:, m % SRING, off:512], probs[:, c % PRING, off:512])\
                           .then_inc(p_hi_ready, 1)
                        if not on_pool(h.kind, m):
                            dve.wait_ge(p_hi_ready, h.combo + m + 1)
                            dve.tensor_tensor(p_lo[:, m % SRING, off:512], probs[:, c % PRING, off:512],
                                              f32(p_hi[:, m % SRING, off:512]), ALU.subtract).then_inc(p_lo_dve, 1)
                    elif op == "o_first":
                        b = st[1]
                        dve.wait_ge(o_stored[b % 2], 8 * sum(BLOCKS) * h.i
                                    + (16 * (b // 2 + 1) + 8 * BLOCKS[FOX] * h.kind))
                        if h.kind == FOX:
                            dve.wait_ge(o_half_ready, BLOCKS[FOX] * h.i + b + 1)
                            dve.tensor_tensor(o_sb[0:64, b % 2, :], ps_o[0:64, b % 2, :], o_half[0:64, :], ALU.add)\
                               .then_inc(o_free, 1)
                        else:
                            dve.wait_ge(p_used, h.combo + block_last(DIFF, b) + 1 + SRING)
                            dve.tensor_copy(o_sb[:, b % 2, :], ps_o[:, b % 2, :]).then_inc(o_free, 1)
                    elif op == "o_var":
                        dve.wait_ge(x_ready, h.x_value(st))
                        dve.tensor_scalar(var[:, :], bank(h, "o_var", st[1])[:, 0:4], EPS, None, ALU.add)\
                           .then_inc(x_free, 1)
                    elif op == "o_norm":
                        b = st[1]
                        dve.wait_ge(x_ready, h.x_value(("o_bcast", b)))
                        dve.scalar_tensor_tensor(out=o_sb[:, b % 2, :], in0=o_sb[:, b % 2, :], scalar=gsub[:, :],
                                                 in1=bank(h, "o_bcast", b), op0=ALU.mult, op1=ALU.mult)\
                           .then_inc(x_free, 1)
            halves(dve, emit)

        @block.tensor
        def _(pe):
            pe.sem_inc(scored, 1)
            pe.sem_inc(p_used, SRING)
            pe.wait_ge(const_dve, 4)

            def claim(h, st):
                n = h.users.index(st)
                if n < RING:
                    if h.kind is not None:
                        pe.wait_ge(stat_exped, STAT * h.n)
                        pe.wait_ge(x_free, h.x)
                else:
                    before = h.users[n - RING]
                    if before[0] == "stat_scores":
                        pe.wait_ge(stat_exped, STAT * h.n + (before[1] + 1))
                    else:
                        pe.wait_ge(x_free, h.x_value(before))
                return bank(h, *st)

            def emit(h):
                for st in h.steps:
                    op = st[0]
                    if op == "stat_scores":
                        g = st[1]
                        s, qt, ch = stats[g]
                        if qt % 4 == 0 and ch == 0:
                            pe.wait_ge(lo_ready, 16 * h.n + (8 * s + 2 * (qt // 4) + 2))
                        if g == 0:
                            pe.wait_ge(rows_loaded, 64 * (h.n + 1))
                        scores = claim(h, st)
                        n = stat_width(qt, ch)
                        q = slice(qt * P, (qt + 1) * P)
                        keys = slice(512 * ch, 512 * ch + n)
                        out = scores[:, 0:n]
                        pe.matmul(out, q2[:, h.slot, s, q], k2[:, h.slot, s, keys], start=True, stop=False)
                        if ch == qt // 4:
                            pe.matmul(scores[:, n - P:n], ident_r[:, :], mask_q[:, :],
                                      start=False, stop=False)
                        pe.matmul(out, q1[:, h.slot, s, q], k1[:, h.slot, s, keys], start=False, stop=True)\
                          .then_inc(stat_scored, 1)
                    elif op == "stat_flip":
                        s = st[1]
                        pe.wait_ge(stat_dve, 7 * (2 * h.n + s) + 7)
                        x = claim(h, st)
                        pe.transpose(x[0:2 * RT, 0:P], f32(shift[:, :]), ident).then_inc(x_ready, 1)
                    elif op == "v_flip":
                        g = st[1]
                        idx = piece_index("v", 0, g)
                        pe.wait_ge(staged[idx % STAGES], staged_value(h.n, idx))
                        x = claim(h, st)
                        for t in range(4):
                            last = pe.transpose(x[:, t * P:(t + 1) * P],
                                                stage[:, idx % STAGES, t * P:(t + 1) * P], ident)
                        last.then_inc(x_ready, 1)
                    elif op == "scores":
                        c = st[1]
                        s, J, j = raws[h.kind][c]
                        slot = h.kind
                        off = width(J, j)
                        if c == 0 or (c == 1 and h.kind == DIFF) or (h.kind == FOX and c == RAW // 2):
                            pe.wait_ge(shift_loaded[s], h.shift_value)
                        pe.wait_ge(exped, h.raw + c + 1)
                        out = ps_sc[:, c % 2, off:512]
                        keys = slice(j * P, (j + 1) * P)
                        qs = slice(J * 512 + off, (J + 1) * 512)
                        pe.matmul(out, k2[:, slot, s, keys], q2[:, slot, s, qs], start=True, stop=False)
                        if j >= 4 * J:
                            pe.matmul(ps_sc[:, c % 2, off:off + P], ident_r[:, :], mask_k[:, :],
                                      start=False, stop=False)
                        pe.matmul(out, k1[:, slot, s, keys], q1[:, slot, s, qs], start=False, stop=True)\
                          .then_inc(scored, 1)
                    elif op == "pv":
                        m = st[1]
                        s, J, j = block_of(h.kind, m)
                        off = width(J, j)
                        slot, ring = h.kind, m % SRING
                        pool = on_pool(h.kind, m)
                        b = block_number(h.kind, m)
                        pe.wait_ge(p_lo_pool if pool else p_lo_dve, h.lo_value(m, pool))
                        if j == 0:
                            pe.wait_ge(o_free, h.block + b + 1)
                        out = ps_o[:, b % 2, off:512]
                        end = j == 4 * J + 3
                        if h.kind == FOX:
                            v = vals[:, slot, j, s * P:(s + 1) * P]
                            pe.matmul(out, v, p_hi[:, ring, off:512], start=(j == 0), stop=False)
                            pe.matmul(out, v, p_lo[:, ring, off:512], start=False, stop=end).then_inc(p_used, 1)
                        else:
                            v_hi, v_lo = vals[:, slot, j, 0:P], vals[:, slot, j, P:2 * P]
                            pe.matmul(out, v_hi, p_hi[:, ring, off:512], start=(j == 0), stop=False)
                            pe.matmul(out, v_lo, p_hi[:, ring, off:512], start=False, stop=False)
                            pe.matmul(out, v_hi, p_lo[:, ring, off:512], start=False, stop=end)\
                              .then_inc(p_used, 1)
                    elif op == "o_var":
                        b = st[1]
                        pe.wait_ge(o_squared, BLOCKS[DIFF] * h.i + b + 1)
                        x = claim(h, st)
                        for t in range(4):
                            last = pe.matmul(x[:, t:t + 1], o_half[:, t * P:(t + 1) * P], mean[:, :],
                                             start=True, stop=True)
                        last.then_inc(x_ready, 1)
                    elif op == "o_bcast":
                        b = st[1]
                        pe.wait_ge(o_pow, BLOCKS[DIFF] * h.i + b + 2)
                        x = claim(h, st)
                        for t in range(4):
                            last = pe.matmul(x[:, t * P:(t + 1) * P], rstd[:, t:t + 1].to_broadcast([P, P]), ident,
                                             start=True, stop=True)
                        last.then_inc(x_ready, 1)
            halves(pe, emit)


def mix_out(nc, mixT, w_out, x, g_post_mix, g_pre_mlp, x2, h2T, rows_hi, rows_lo):
    with ExitStack() as ctx:
        r = Room(nc, ctx, "mo")
        w_hi = r.sb("w_hi", [P, KT, D], F32R)
        w_lo = r.sb("w_lo", [P, KT, D], F32R)
        m_raw = r.sb("m_raw", [P, 2, KT, P])
        m_hi = r.sb("m_hi", [P, 2, KT, P], F32R)
        m_lo = r.sb("m_lo", [P, 2, KT, P], F32R)
        xin = r.sb("xin", [P, 2, D])
        y = r.sb("y", [P, 2, D])
        xn = r.sb("xn", [P, 2, D])
        h_hi = r.sb("h_hi", [P, 2, KT, P], F32R)
        h_lo = r.sb("h_lo", [P, 2, KT, P], F32R)
        g_post = r.sb("g_post", [P, D])
        g_pre = r.sb("g_pre", [P, D])
        ident = r.sb("ident", [P, P])
        power = r.sb("power", [P, 1])
        eps = r.sb("eps", [P, 1])
        ss = r.sb("ss", [P, 2, RT])
        rstd = r.sb("rstd", [P, 2, RT])
        acc = r.ps("acc", [P, 2, D])
        flip = r.ps("flip", [P, 2, D])
        const_ready = r.sem("const_ready")
        gains_loaded = r.sem("gains_loaded")
        w_loaded = [r.sem(f"w_loaded{k}") for k in range(KT)]
        w_hi_ready = r.sem("w_hi_ready")
        w_ready = r.sem("w_ready")
        m_loaded = [r.sem(f"m_loaded{s}") for s in range(2)]
        x_loaded = [r.sem(f"x_loaded{s}") for s in range(2)]
        m_hi_ready = r.sem("m_hi_ready")
        m_ready = r.sem("m_ready")
        multiplied = r.sem("multiplied")
        ss_ready = r.sem("ss_ready")
        rstd_step = r.sem("rstd_step")
        y_step = r.sem("y_step")
        xn_ready = r.sem("xn_ready")
        flipped = r.sem("flipped")
        h_hi_ready = r.sem("h_hi_ready")
        h_ready = r.sem("h_ready")
        x2_stored = [r.sem(f"x2_stored{s}") for s in range(2)]
        h_stored = [r.sem(f"h_stored{s}") for s in range(2)]
        block = ctx.enter_context(nc.Block())
        LAST = RT // 2
        w_raw = [y[:, 0, :], y[:, 1, :], xn[:, 0, :], xn[:, 1, :]] + \
                [f32(h[:, s].rearrange("p k r -> p (k r)")) for h in (h_hi, h_lo) for s in range(2)]

        def kept(t, s, slots, rows, resident):
            return rows[:, :, bass.ts(t - LAST, P)] if resident else slots[:, s]

        @block.sync
        def _(sp):
            sp.dma_start(m_raw[:, 0], mixT[:, :, 0:P].rearrange("k p n -> p k n")).then_inc(m_loaded[0], 16)
            for k in range(KT):
                sp.dma_start(w_raw[k], w_out[0, k * P:(k + 1) * P, :]).then_inc(w_loaded[k], 16)
            sp.dma_start(g_post[:, :], g_post_mix[0:1, :].to_broadcast([P, D])).then_inc(gains_loaded, 16)
            sp.dma_start(g_pre[:, :], g_pre_mlp[0:1, :].to_broadcast([P, D])).then_inc(gains_loaded, 16)
            sp.dma_start(xin[:, 0, :], x[0, 0:P, :]).then_inc(x_loaded[0], 16)
            sp.dma_start(m_raw[:, 1], mixT[:, :, P:2 * P].rearrange("k p n -> p k n")).then_inc(m_loaded[1], 16)
            sp.dma_start(xin[:, 1, :], x[0, P:2 * P, :]).then_inc(x_loaded[1], 16)
            with sp.Fori(0, LAST - 1) as i:
                for s in range(2):
                    t = 2 * i + s + 2
                    sp.wait_ge(m_ready, t + 1)
                    sp.dma_start(m_raw[:, s], mixT[:, :, bass.ts(t, P)].rearrange("k p n -> p k n"))\
                      .then_inc(m_loaded[s], 16)
                    sp.wait_ge(y_step, 2 * (t - 1))
                    sp.dma_start(xin[:, s, :], x[0, bass.ts(t, P), :]).then_inc(x_loaded[s], 16)

        @block.gpsimd
        def _(pool):
            pool.memset(ident[:, :], 0.0).then_inc(const_ready, 1)
            pool.memset(power[:, :], -0.5).then_inc(const_ready, 1)
            pool.memset(eps[:, :], EPS).then_inc(const_ready, 1)
            pool.wait_ge(const_ready, 1)
            pool.affine_select(out=ident[:, :], in_=ident[:, :], compare_op=ALU.not_equal, fill=1.0,
                               base=0, pattern=[[-1, P]], channel_multiplier=1).then_inc(const_ready, 1)
            pool.wait_ge(const_ready, 4)
            with pool.Fori(0, RT) as t:
                for n in range(2):
                    pool.wait_ge(ss_ready, 2 * t + n + 1)
                    pool.tensor_tensor(ss[:, n, bass.ds(t, 1)], ss[:, n, bass.ds(t, 1)], eps[:, :], ALU.add)\
                        .then_inc(rstd_step, 1)
                    pool.wait_ge(rstd_step, 4 * t + 2 * n + 1)
                    pool.tensor_tensor(rstd[:, n, bass.ds(t, 1)], ss[:, n, bass.ds(t, 1)], power[:, :],
                                       ALU.pow).then_inc(rstd_step, 1)

        @block.scalar
        def _(act):
            for s in range(2):
                act.sem_inc(x2_stored[s], 16)
                act.sem_inc(h_stored[s], 32)

            def tile(i, s, t):
                act.wait_ge(multiplied, t + 3)
                act.wait_ge(xn_ready, t + 1)
                act.wait_ge(flipped, t + 1)
                act.activation(xn[:, s, :], acc[:, s, :], ACT.Square, scale=ROOT, accum_out=ss[:, 0, bass.ds(t, 1)])\
                   .then_inc(ss_ready, 1)
                act.wait_ge(y_step, 2 * t + 2)
                act.activation(xn[:, s, :], y[:, s, :], ACT.Square, scale=ROOT, accum_out=ss[:, 1, bass.ds(t, 1)])\
                   .then_inc(ss_ready, 1)
                act.dma_start(x2[bass.ts(t, P), :], y[:, s, :]).then_inc(x2_stored[s], 16)

            def keep(i, s, t, resident):
                act.wait_ge(flipped, t + 3)
                if not resident:
                    act.wait_ge(h_stored[s], 32 * (i + 1))
                act.activation(kept(t, s, h_hi, rows_hi, resident),
                               flip[:, s, :].rearrange("p (k r) -> p k r", r=P), ACT.Copy).then_inc(h_hi_ready, 1)
                if not resident:
                    act.wait_ge(h_ready, t + 3)
                    for n, src in enumerate((h_hi, h_lo)):
                        act.dma_start(h2T[n, :, :, bass.ts(t, P)].rearrange("k p n -> p k n"), f32(src[:, s]))\
                           .then_inc(h_stored[s], 16)
            act.sem_inc(flipped, 2)
            for k in range(KT):
                act.wait_ge(w_loaded[k], 16)
                act.activation(w_hi[:, k, :], w_raw[k], ACT.Copy).then_inc(w_hi_ready, 1)
            tile(0, 0, 0)
            for lo, hi, resident in ((0, LAST // 2, False), (LAST // 2, LAST - 1, True)):
                with act.Fori(lo, hi) as i:
                    tile(i, 1, 2 * i + 1)
                    keep(i, 0, 2 * i, resident)
                    tile(i + 1, 0, 2 * i + 2)
                    keep(i, 1, 2 * i + 1, resident)
            tile(LAST - 1, 1, RT - 1)
            keep(LAST - 1, 0, RT - 2, True)
            keep(LAST - 1, 1, RT - 1, True)
            for s in range(2):
                act.wait_ge(x2_stored[s], 16 * (LAST + 1))
                act.wait_ge(h_stored[s], 32 * (LAST // 2 + 1))

        @block.vector
        def _(dve):
            dve.sem_inc(m_ready, 2)
            dve.sem_inc(xn_ready, 2)
            dve.sem_inc(h_ready, 2)

            def split_mix(i, s, t):
                dve.wait_ge(m_loaded[s], 16 * (i + 1))
                dve.wait_ge(multiplied, t + 1)
                dve.tensor_copy(m_hi[:, s], m_raw[:, s]).then_inc(m_hi_ready, 1)
                dve.wait_ge(m_hi_ready, t + 1)
                dve.tensor_tensor(m_lo[:, s], m_raw[:, s], f32(m_hi[:, s]), ALU.subtract).then_inc(m_ready, 1)

            def norms(i, s, t):
                dve.wait_ge(rstd_step, 4 * t + 2)
                dve.wait_ge(x2_stored[s], 16 * (i + 1))
                dve.scalar_tensor_tensor(out=y[:, s, :], in0=acc[:, s, :], scalar=rstd[:, 0, bass.ds(t, 1)],
                                         in1=g_post[:, :], op0=ALU.mult, op1=ALU.mult).then_inc(y_step, 1)
                dve.wait_ge(x_loaded[s], 16 * (i + 1))
                dve.wait_ge(y_step, 2 * t + 1)
                dve.tensor_tensor(y[:, s, :], y[:, s, :], xin[:, s, :], ALU.add).then_inc(y_step, 1)

            def pre_norm(i, s, t):
                dve.wait_ge(rstd_step, 4 * t + 4)
                dve.scalar_tensor_tensor(out=xn[:, s, :], in0=y[:, s, :], scalar=rstd[:, 1, bass.ds(t, 1)],
                                         in1=g_pre[:, :], op0=ALU.mult, op1=ALU.mult).then_inc(xn_ready, 1)

            def keep_lo(s, t, resident):
                dve.wait_ge(h_hi_ready, t + 1)
                dve.tensor_tensor(kept(t, s, h_lo, rows_lo, resident),
                                  flip[:, s, :].rearrange("p (k r) -> p k r", r=P),
                                  f32(kept(t, s, h_hi, rows_hi, resident)), ALU.subtract).then_inc(h_ready, 1)

            split_mix(0, 0, 0)
            for k in range(KT):
                dve.wait_ge(w_hi_ready, k + 1)
                dve.tensor_tensor(w_lo[:, k, :], w_raw[k], f32(w_hi[:, k, :]), ALU.subtract)\
                   .then_inc(w_ready, 1)
            dve.wait_ge(gains_loaded, 32)
            split_mix(0, 1, 1)
            norms(0, 0, 0)
            pre_norm(0, 0, 0)
            for lo, hi, resident in ((0, LAST // 2, False), (LAST // 2, LAST - 1, True)):
                with dve.Fori(lo, hi) as i:
                    split_mix(i + 1, 0, 2 * i + 2)
                    norms(i, 1, 2 * i + 1)
                    keep_lo(0, 2 * i, resident)
                    pre_norm(i, 1, 2 * i + 1)
                    split_mix(i + 1, 1, 2 * i + 3)
                    norms(i + 1, 0, 2 * i + 2)
                    keep_lo(1, 2 * i + 1, resident)
                    pre_norm(i + 1, 0, 2 * i + 2)
            norms(LAST - 1, 1, RT - 1)
            keep_lo(0, RT - 2, True)
            pre_norm(LAST - 1, 1, RT - 1)
            keep_lo(1, RT - 1, True)

        @block.tensor
        def _(pe):
            pe.sem_inc(multiplied, 2)

            def multiply_first():
                pe.wait_ge(m_ready, 3)
                for k in range(KT):
                    pe.wait_ge(w_ready, k + 1)
                    for lhs, rhs in ((m_hi, w_hi), (m_hi, w_lo), (m_lo, w_hi)):
                        for b in range(D // 512):
                            cols = slice(b * 512, (b + 1) * 512)
                            last = pe.matmul(acc[:, 0, cols], lhs[:, 0, k], rhs[:, k, cols],
                                             start=(k == 0 and rhs is w_hi and lhs is m_hi),
                                             stop=(k == KT - 1 and lhs is m_lo))
                last.then_inc(multiplied, 1)

            def multiply(i, s, t):
                pe.wait_ge(m_ready, t + 3)
                if not isinstance(t, int) or t > 1:
                    pe.wait_ge(y_step, 2 * t - 3)
                for b in range(D // 512):
                    cols = slice(b * 512, (b + 1) * 512)
                    for k in range(KT):
                        pe.matmul(acc[:, s, cols], m_hi[:, s, k], w_hi[:, k, cols], start=(k == 0), stop=False)
                        pe.matmul(acc[:, s, cols], m_hi[:, s, k], w_lo[:, k, cols], start=False, stop=False)
                        last = pe.matmul(acc[:, s, cols], m_lo[:, s, k], w_hi[:, k, cols],
                                         start=False, stop=(k == KT - 1))
                last.then_inc(multiplied, 1)

            def transpose(s, t):
                pe.wait_ge(xn_ready, t + 3)
                pe.wait_ge(h_ready, t + 1)
                for k in range(KT):
                    last = pe.transpose(flip[:, s, k * P:(k + 1) * P], xn[:, s, k * P:(k + 1) * P], ident[:, :])
                last.then_inc(flipped, 1)
            pe.wait_ge(const_ready, 4)
            multiply_first()
            multiply(0, 1, 1)
            transpose(0, 0)
            with pe.Fori(0, LAST - 1) as i:
                multiply(i, 0, 2 * i + 2)
                transpose(1, 2 * i + 1)
                multiply(i, 1, 2 * i + 3)
                transpose(0, 2 * i + 2)
            transpose(1, RT - 1)


def mlp(nc, h_hi, h_lo, h2T, w_up, w_down, x2, g_post_mlp, out):
    SW = S // 2
    ST = SW // P
    FC = 256
    FT = FC // P
    NC = DFF // FC
    RB = SW // 512
    UB = FT * RB
    YB = ST * D // 512
    XS = 4
    with ExitStack() as ctx:
        r = Room(nc, ctx, "ml")
        y = r.sb("y", [P, ST, D])
        u_hi = r.sb("u_hi", [P, 2, FT, SW], F32R)
        u_lo = r.sb("u_lo", [P, 2, FT, SW], F32R)
        up_raw = r.sb("up_raw", [P, KT, FC])
        up_hi = r.sb("up_hi", [P, KT, FC], F32R)
        up_lo = r.sb("up_lo", [P, KT, FC], F32R)
        dn_raw = r.sb("dn_raw", [P, FT, D])
        dn_hi = r.sb("dn_hi", [P, FT, D], F32R)
        dn_lo = r.sb("dn_lo", [P, FT, D], F32R)
        relu = r.sb("relu", [P, 2, 512])
        gain = r.sb("gain", [P, D])
        xres = r.sb("xres", [P, XS, D])
        junk = r.sb("junk", [P, D])
        power = r.sb("power", [P, 1])
        ss = r.sb("ss", [P, 2 * ST])
        rstd = r.sb("rstd", [P, 2 * ST])
        ps_u = r.ps("ps_u", [P, 4, 512])
        ps_y = r.ps("ps_y", [P, 4, 512])
        const_ready = r.sem("const_ready")
        gain_loaded = r.sem("gain_loaded")
        h_loaded = [r.sem(f"h_loaded{rb}") for rb in range(RB)]
        up_loaded = r.sem("up_loaded")
        dn_loaded = r.sem("dn_loaded")
        up_hi_ready = r.sem("up_hi_ready")
        up_lo_ready = r.sem("up_lo_ready")
        dn_hi_ready = r.sem("dn_hi_ready")
        dn_lo_ready = r.sem("dn_lo_ready")
        up_done = r.sem("up_done")
        dn_done = r.sem("dn_done")
        relued = r.sem("relued")
        u_step = r.sem("u_step")
        y_added = r.sem("y_added")
        y_cleared = r.sem("y_cleared")
        ss_ready = r.sem("ss_ready")
        rstd_step = r.sem("rstd_step")
        x_loaded = [r.sem(f"x_loaded{s}") for s in range(XS)]
        y_normed = r.sem("y_normed")
        out_ready = r.sem("out_ready")
        last_ready = r.sem("last_ready")
        stored = [r.sem(f"stored{s}") for s in range(XS)]
        block = ctx.enter_context(nc.Block())
        up_v = w_up.rearrange("o (k p) f -> p (o k) f", p=P)
        dn_v = w_down.rearrange("o (k p) d -> p (o k) d", p=P)
        by_half = [(t, half) for half in range(2) for t in range(ST)]
        by_tile = [(t, half) for half in range(2) for t in range(ST // 2)] + \
                  [(t, half) for t in range(ST // 2, ST) for half in range(2)]

        def sweeps(eng, up, down):
            up(0, 0, 0)
            for w in range(2):
                with eng.Fori(0, NC // 2 - 1) as i:
                    up(w, 2 * i + 1, 1)
                    down(w, 2 * i, 0)
                    up(w, 2 * i + 2, 0)
                    down(w, 2 * i + 1, 1)
                up(w, NC - 1, 1)
                down(w, NC - 2, 0)
                down(w, NC - 1, 1)
                if w == 0:
                    up(1, 0, 0)

        def row(n):
            return ((1 - n // ST) * ST + n % ST) * P

        def first(c):
            return isinstance(c, int) and c == 0

        def final(c):
            return isinstance(c, int) and c == NC - 1

        def finished(t):
            return max(by_tile.index((t, half)) for half in range(2)) + 1

        @block.sync
        def _(sp):
            def load_up(n, c):
                sp.wait_ge(up_lo_ready, FT * (n + 1))
                sp.dma_start(up_raw[:, :, :], up_v[:, :, bass.ds(c * FC, FC)]).then_inc(up_loaded, 16)

            def load_h():
                for rb in range(RB):
                    rows = slice(rb * 512, (rb + 1) * 512)
                    for z, dst in enumerate((h_hi, h_lo)):
                        for k in range(0, KT, 2):
                            sp.dma_start(f32(dst[:, k:k + 2, rows]),
                                         h2T[z, k:k + 2, :, rows].rearrange("k p n -> p k n"))\
                              .then_inc(h_loaded[rb], 16)

            def load_x(n):
                if n >= XS:
                    sp.wait_ge(stored[n % XS], 16 * (n // XS))
                sp.dma_start(xres[:, n % XS, :], x2[row(n):row(n) + P, :]).then_inc(x_loaded[n % XS], 16)

            def store(n):
                if n % ST == ST - 1:
                    sp.wait_ge(last_ready, n // ST + 1)
                else:
                    sp.wait_ge(out_ready, n - n // ST + 1)
                sp.dma_start(out[0, row(n):row(n) + P, :], xres[:, n % XS, :]).then_inc(stored[n % XS], 16)

            def up(w, c, s):
                n = w * NC + c
                if not final(c) and not (first(c) and w):
                    load_up(n + 1, c + 1)

            def down(w, c, s):
                n = w * NC + c
                sp.wait_ge(dn_lo_ready, 2 * n + 2)
                sp.dma_start(dn_raw[:, :, :], dn_v[:, bass.ds(c * FT, FT), :]).then_inc(dn_loaded, 16)
                if final(c):
                    for t in range(XS - 1):
                        load_x(w * ST + t)
                    if w == 0:
                        load_up(NC, 0)
                        sp.wait_ge(up_done, UB + UB * NC)
                        load_h()
                        load_up(NC + 1, 1)
                    for t in range(ST):
                        if t + XS - 1 < ST:
                            load_x(w * ST + t + XS - 1)
                        store(w * ST + t)
            load_up(0, 0)
            sp.dma_start(gain[:, :], g_post_mlp[0:1, :].to_broadcast([P, D])).then_inc(gain_loaded, 16)
            sweeps(sp, up, down)
            for s in range(XS):
                sp.wait_ge(stored[s], 16 * (2 * ST // XS))

        @block.gpsimd
        def _(pool):
            pool.sem_inc(up_lo_ready, FT)
            pool.sem_inc(dn_lo_ready, 2)
            pool.memset(power[:, :], -0.5).then_inc(const_ready, 1)

            def lo_up(n):
                for f in range(FT):
                    cols = slice(f * P, (f + 1) * P)
                    pool.wait_ge(up_hi_ready, FT * n + f + 1)
                    pool.tensor_tensor(up_lo[:, :, cols], up_raw[:, :, cols], f32(up_hi[:, :, cols]),
                                       ALU.subtract).then_inc(up_lo_ready, 1)

            def lo_down(n):
                for half in range(2):
                    cols = slice(half * 512, (half + 1) * 512)
                    pool.wait_ge(dn_hi_ready, 2 * n + half + 1)
                    pool.tensor_tensor(dn_lo[:, :, cols], dn_raw[:, :, cols], f32(dn_hi[:, :, cols]),
                                       ALU.subtract).then_inc(dn_lo_ready, 1)

            def up(w, c, s):
                n = w * NC + c
                if first(c):
                    lo_up(n + 1)
                else:
                    lo_down(n - 1)

            def add_residual(n):
                t = n % ST
                if t < ST - 1:
                    pool.wait_ge(x_loaded[n % XS], 16 * (n // XS + 1))
                    pool.wait_ge(y_normed, n + 1)
                    pool.tensor_tensor(xres[:, n % XS, :], xres[:, n % XS, :], y[:, t, :], ALU.add)\
                        .then_inc(out_ready, 1)
                if n < ST:
                    if t < ST - 1:
                        pool.wait_ge(out_ready, n + 1)
                    else:
                        pool.wait_ge(last_ready, 1)
                    pool.memset(y[:, t, :], 0.0).then_inc(y_cleared, 1)

            def down(w, c, s):
                n = w * NC + c
                if not final(c):
                    if not isinstance(c, int) or w == 0:
                        lo_up(n + 2)
                    return
                lo_down(n)
                for t in range(ST):
                    m = w * ST + t
                    pool.wait_ge(ss_ready, m + 1)
                    pool.tensor_scalar(ss[:, m:m + 1], ss[:, m:m + 1], EPS, None, ALU.add).then_inc(rstd_step, 1)
                    pool.wait_ge(rstd_step, 2 * m + 1)
                    pool.tensor_tensor(rstd[:, m:m + 1], ss[:, m:m + 1], power[:, :], ALU.pow)\
                        .then_inc(rstd_step, 1)
                    if t:
                        add_residual(m - 1)
                add_residual(w * ST + ST - 1)
            pool.wait_ge(const_ready, 1)
            lo_up(0)
            for t in range(ST):
                pool.memset(y[:, t, :], 0.0).then_inc(y_cleared, 1)
            sweeps(pool, up, down)

        @block.scalar
        def _(act):
            act.sem_inc(relued, 4)

            def hi_up(n, f, early=False):
                cols = slice(f * P, (f + 1) * P)
                act.wait_ge(up_loaded, 16 * (n + 1))
                if early:
                    act.wait_ge(up_done, UB * n + RB * (f + 1))
                else:
                    act.wait_ge(up_done, UB * (n + 1))
                act.activation(up_hi[:, :, cols], up_raw[:, :, cols], ACT.Copy).then_inc(up_hi_ready, 1)

            def hi_down(n, early):
                act.wait_ge(dn_loaded, 16 * (n + 1))
                for half in range(2):
                    cols = slice(half * 512, (half + 1) * 512)
                    if early and half == 0:
                        act.wait_ge(dn_done, YB * (n + 1) + ST)
                    elif early or half == 0:
                        act.wait_ge(dn_done, YB * (n + 2))
                    act.activation(dn_hi[:, :, cols], dn_raw[:, :, cols], ACT.Copy).then_inc(dn_hi_ready, 1)

            def up(w, c, s):
                n = w * NC + c
                if not first(c):
                    hi_down(n - 1, False)
                for b in range(UB):
                    g = n * UB + b
                    act.wait_ge(up_done, g + 1 + UB)
                    act.wait_ge(u_step, 3 * g + 3)
                    act.activation(relu[:, b % 2, :], ps_u[:, b % 4, :], ACT.Relu).then_inc(relued, 1)
                    if first(c) and b % RB == RB - 1:
                        hi_up(n + 1, b // RB, early=True)

            def down(w, c, s):
                n = w * NC + c
                if not final(c):
                    if not isinstance(c, int) or w == 0:
                        for f in range(FT):
                            hi_up(n + 2, f)
                    return
                hi_down(n, True)
                for t in range(ST):
                    m = w * ST + t
                    act.wait_ge(y_added, 4 + YB * n + finished(t))
                    if m:
                        act.wait_ge(ss_ready, m)
                    act.activation(junk[:, :], y[:, t, :], ACT.Square, scale=ROOT, accum_out=ss[:, m:m + 1])\
                       .then_inc(ss_ready, 1)
            for f in range(FT):
                hi_up(0, f)
            sweeps(act, up, down)

        @block.vector
        def _(dve):
            dve.sem_inc(u_step, 6)
            dve.sem_inc(y_added, 4)

            def up(w, c, s):
                n = w * NC + c
                for b in range(UB):
                    g = n * UB + b
                    f, rb = b // RB, b % RB
                    rows = slice(rb * 512, (rb + 1) * 512)
                    dve.wait_ge(relued, g + 5)
                    if b == 0:
                        dve.wait_ge(dn_done, YB * (n + 1))
                    dve.tensor_tensor(relu[:, b % 2, :], relu[:, b % 2, :], relu[:, b % 2, :], ALU.mult)\
                       .then_inc(u_step, 1)
                    dve.wait_ge(u_step, 3 * g + 7)
                    dve.tensor_copy(u_hi[:, s, f, rows], relu[:, b % 2, :]).then_inc(u_step, 1)
                    dve.wait_ge(u_step, 3 * g + 8)
                    dve.tensor_tensor(u_lo[:, s, f, rows], relu[:, b % 2, :], f32(u_hi[:, s, f, rows]),
                                      ALU.subtract).then_inc(u_step, 1)

            def normalise(w, t):
                n = w * ST + t
                dve.wait_ge(rstd_step, 2 * n + 2)
                dve.scalar_tensor_tensor(out=y[:, t, :], in0=y[:, t, :], scalar=rstd[:, n:n + 1],
                                         in1=gain[:, :], op0=ALU.mult, op1=ALU.mult).then_inc(y_normed, 1)

            def down(w, c, s):
                n = w * NC + c
                if not isinstance(c, int):
                    dve.wait_ge(y_cleared, ST * (w + 1))
                normed = 0
                for b, (t, half) in enumerate(by_tile if final(c) else by_half):
                    g = n * YB + b
                    cols = slice(half * 512, (half + 1) * 512)
                    dve.wait_ge(dn_done, g + 1 + 2 * YB)
                    dve.wait_ge(y_added, g + 4)
                    dve.tensor_tensor(y[:, t, cols], y[:, t, cols], ps_y[:, b % 4, :], ALU.add)\
                       .then_inc(y_added, 1)
                    if final(c) and finished(normed) + 3 <= b:
                        normalise(w, normed)
                        normed += 1
                if final(c):
                    for t in range(normed, ST):
                        normalise(w, t)
                    m = w * ST + ST - 1
                    dve.wait_ge(x_loaded[m % XS], 16 * (m // XS + 1))
                    dve.wait_ge(y_normed, m + 1)
                    dve.tensor_tensor(xres[:, m % XS, :], xres[:, m % XS, :], y[:, ST - 1, :], ALU.add)\
                       .then_inc(last_ready, 1)
            dve.wait_ge(gain_loaded, 16)
            sweeps(dve, up, down)

        @block.tensor
        def _(pe):
            pe.sem_inc(up_done, UB)
            pe.sem_inc(dn_done, 2 * YB)

            def up(w, c, s):
                n = w * NC + c
                for b in range(UB):
                    g = n * UB + b
                    f, rb = b // RB, b % RB
                    rows = slice(rb * 512, (rb + 1) * 512)
                    cols = slice(f * P, (f + 1) * P)
                    if rb == 0:
                        pe.wait_ge(up_hi_ready, FT * n + f + 1)
                        pe.wait_ge(up_lo_ready, FT * (n + 1) + f + 1)
                    if first(c) and w and f == 0:
                        pe.wait_ge(h_loaded[rb], 16 * KT)
                    pe.wait_ge(relued, g + 1)
                    for k in range(KT):
                        pe.matmul(ps_u[:, b % 4, :], up_hi[:, k, cols], h_hi[:, k, rows],
                                  start=(k == 0), stop=False)
                        pe.matmul(ps_u[:, b % 4, :], up_hi[:, k, cols], h_lo[:, k, rows], start=False, stop=False)
                        last = pe.matmul(ps_u[:, b % 4, :], up_lo[:, k, cols], h_hi[:, k, rows],
                                         start=False, stop=(k == KT - 1))
                    last.then_inc(up_done, 1)

            def down(w, c, s):
                n = w * NC + c
                pe.wait_ge(u_step, 6 + 3 * UB * (n + 1))
                arrived = 0
                for b, (t, half) in enumerate(by_tile if final(c) else by_half):
                    g = n * YB + b
                    cols = slice(half * 512, (half + 1) * 512)
                    rows = slice(t * P, (t + 1) * P)
                    if half == arrived:
                        pe.wait_ge(dn_hi_ready, 2 * n + half + 1)
                        pe.wait_ge(dn_lo_ready, 2 * n + half + 3)
                        arrived += 1
                    pe.wait_ge(y_added, g + 1)
                    for f in range(FT):
                        pe.matmul(ps_y[:, b % 4, :], u_hi[:, s, f, rows], dn_hi[:, f, cols],
                                  start=(f == 0), stop=False)
                        pe.matmul(ps_y[:, b % 4, :], u_hi[:, s, f, rows], dn_lo[:, f, cols],
                                  start=False, stop=False)
                        last = pe.matmul(ps_y[:, b % 4, :], u_lo[:, s, f, rows], dn_hi[:, f, cols],
                                         start=False, stop=(f == FT - 1))
                    last.then_inc(dn_done, 1)
            sweeps(pe, up, down)


def hybrid_block(nc, x, g_pre_mix, w_in, b_forget, lambda_q1, lambda_k1, lambda_q2, lambda_k2,
                 g_subln, w_out, g_post_mix, g_pre_mlp, w_up, w_down, g_post_mlp, out):
    qkvT = nc.dram_tensor("qkvT", [QKV_TILES + 1, P, S], F32).ap()
    q_rows = nc.dram_tensor("q_rows", [6, FOX_HEADS + DIFF_HEADS, S], F32).ap()
    k_rows = nc.dram_tensor("k_rows", [6, FOX_HEADS + DIFF_HEADS, S], F32).ap()
    mixT = nc.dram_tensor("mixT", [KT, P, S], F32).ap()
    x2 = nc.dram_tensor("x2", [S, D], F32).ap()
    h2T = nc.dram_tensor("h2T", [2, KT, P, S // 2], F32).ap()
    project(nc, x, g_pre_mix, w_in, b_forget, qkvT, q_rows, k_rows)
    attend(nc, qkvT, q_rows, k_rows, (lambda_q1, lambda_k1, lambda_q2, lambda_k2), g_subln, mixT)
    with ExitStack() as ctx:
        r = Room(nc, ctx, "h2")
        rows_hi = r.sb("rows_hi", [P, KT, S // 2], F32R)
        rows_lo = r.sb("rows_lo", [P, KT, S // 2], F32R)
        mix_out(nc, mixT, w_out, x, g_post_mix, g_pre_mlp, x2, h2T, rows_hi, rows_lo)
        mlp(nc, rows_hi, rows_lo, h2T, w_up, w_down, x2, g_post_mlp, out)


_INS = ["x", "g_pre_mix", "w_in", "b_forget", "lambda_q1", "lambda_k1", "lambda_q2", "lambda_k2",
        "g_subln", "w_out", "g_post_mix", "g_pre_mlp", "w_up", "w_down", "g_post_mlp"]


def kernel(**inputs):
    import numpy as _np
    import concourse.bacc as _bacc
    from concourse import mybir as _mybir
    from concourse.bass_utils import run_bass_kernel_spmd as _run

    nc = _bacc.Bacc("TRN2", target_bir_lowering=False, num_devices=1)
    arrays, args = {}, []
    for name in _INS:
        a = _np.ascontiguousarray(inputs[name])
        arrays[f"in_{name}_dram"] = a
        args.append(nc.dram_tensor(f"in_{name}_dram", a.shape, _mybir.dt.from_np(a.dtype), kind="ExternalInput").ap())
    args.append(nc.dram_tensor("out_0_dram", (1, S, D), _mybir.dt.float32, kind="ExternalOutput").ap())
    hybrid_block(nc, *args)
    r = _run(nc, [arrays], core_ids=[0])
    return r.results[0]["out_0_dram"]
```
